# Optimizing a Trainium2 kernel written in Bass

```python
import math
import jax, jax.numpy as jnp
from jax import lax
import numpy as np

D_MODEL = 1024
BATCH = 1
SEQ = 2048
DEPTH = 1
DEC_BATCH = 8
DEC_SEQ = 8
PAST_LEN = 16384
PAGE_SIZE = 128

D_MIX = D_MODEL
D_SSM = D_MIX // 2
D_RWKV = D_MIX - D_SSM
SSM_GROUP = 16
N_SSM_GROUPS = D_SSM // SSM_GROUP
SSM_STATE = 64
RWKV_HEAD = 64
N_RWKV_HEADS = D_RWKV // RWKV_HEAD
DECAY_LORA = 64
AAA_LORA = 64
GATE_LORA = 128
N_SHIFT = 3 * D_RWKV + DECAY_LORA + AAA_LORA + GATE_LORA
N_IN = D_SSM + N_SHIFT
D_FF = 2816
CONV_W = 3
D_PLE = 256
RMS_EPS = 1e-6
GN_EPS = 64e-5
L2_EPS = 1e-12

kernel_name = 's5_rwkv7_hybrid_decode_step'

def _rmsnorm(x, g):
    xf = x.astype(jnp.float32)
    y = xf * lax.rsqrt(jnp.mean(xf * xf, axis=-1, keepdims=True) + RMS_EPS)
    return y * g.astype(jnp.float32)

def _s5(u, h0_re, h0_im, lam_re, lam_im, log_dt, b_re, b_im, c_re, c_im, d_skip, w_glu, b_glu):
    bsz, seq_len, _ = u.shape
    ug = u.reshape(bsz, seq_len, N_SSM_GROUPS, SSM_GROUP)
    dt = jnp.exp(log_dt)[:, None]
    mag = jnp.exp(lam_re * dt)
    ab_re = mag * jnp.cos(lam_im * dt)
    ab_im = mag * jnp.sin(lam_im * dt)
    den = lam_re * lam_re + lam_im * lam_im
    nr = ab_re - 1.0
    f_re = (nr * lam_re + ab_im * lam_im) / den
    f_im = (ab_im * lam_re - nr * lam_im) / den
    bb_re = f_re[..., None] * b_re - f_im[..., None] * b_im
    bb_im = f_re[..., None] * b_im + f_im[..., None] * b_re
    bu_re = jnp.einsum('blgc,gpc->blgp', ug, bb_re)
    bu_im = jnp.einsum('blgc,gpc->blgp', ug, bb_im)
    bu_re = bu_re.at[:, 0].add(ab_re * h0_re - ab_im * h0_im)
    bu_im = bu_im.at[:, 0].add(ab_re * h0_im + ab_im * h0_re)
    a_re = jnp.broadcast_to(ab_re, bu_re.shape)
    a_im = jnp.broadcast_to(ab_im, bu_im.shape)

    def combine(e1, e2):
        a1r, a1i, b1r, b1i = e1
        a2r, a2i, b2r, b2i = e2
        return (a1r * a2r - a1i * a2i, a1r * a2i + a1i * a2r,
                a2r * b1r - a2i * b1i + b2r, a2r * b1i + a2i * b1r + b2i)

    _, _, h_re, h_im = lax.associative_scan(combine, (a_re, a_im, bu_re, bu_im), axis=1)
    y = jnp.einsum('blgp,gcp->blgc', h_re, c_re) - jnp.einsum('blgp,gcp->blgc', h_im, c_im)
    y = y.reshape(bsz, seq_len, D_SSM) + d_skip * u
    y = jax.nn.gelu(y)
    y = y * jax.nn.sigmoid(y @ w_glu + b_glu)
    return y, h_re[:, -1], h_im[:, -1]

def _rwkv7(z, s0, w0, w2, a0, a2, g2, k_k, k_a, r_k, lnx_g, lnx_b):
    bsz, seq_len, _ = z.shape
    c1, c2, c3 = D_RWKV, 2 * D_RWKV, 3 * D_RWKV
    c4, c5 = c3 + DECAY_LORA, c3 + DECAY_LORA + AAA_LORA
    r, k, v = z[..., :c1], z[..., c1:c2], z[..., c2:c3]
    xw, xa, xg = z[..., c3:c4], z[..., c4:c5], z[..., c5:]
    w = -jax.nn.softplus(-(w0 + jnp.tanh(xw) @ w2)) - 0.5
    decay = jnp.exp(-jnp.exp(w))
    a = jax.nn.sigmoid(a0 + xa @ a2)
    g = jax.nn.sigmoid(xg) @ g2
    hs = (bsz, seq_len, N_RWKV_HEADS, RWKV_HEAD)
    kk = (k * k_k).reshape(hs)
    kk = kk / jnp.maximum(jnp.sqrt(jnp.sum(kk * kk, axis=-1, keepdims=True)), L2_EPS)
    k = k * (1.0 + (a - 1.0) * k_a)
    r4, k4, v4 = r.reshape(hs), k.reshape(hs), v.reshape(hs)
    w4, a4 = decay.reshape(hs), a.reshape(hs)

    def step(S, inp):
        r_t, w_t, k_t, v_t, kk_t, a_t = inp
        sa = jnp.einsum('bhvk,bhk->bhv', S, -kk_t)
        S = (S * w_t[:, :, None, :] + sa[..., None] * (kk_t * a_t)[:, :, None, :]
             + v_t[..., None] * k_t[:, :, None, :])
        return S, jnp.einsum('bhvk,bhk->bhv', S, r_t)

    tm = lambda t: jnp.moveaxis(t, 1, 0)
    s_last, y = lax.scan(step, s0, (tm(r4), tm(w4), tm(k4), tm(v4), tm(kk), tm(a4)))
    y = jnp.moveaxis(y, 0, 1)
    mu = jnp.mean(y, axis=-1, keepdims=True)
    var = jnp.mean(jnp.square(y - mu), axis=-1, keepdims=True)
    y = ((y - mu) * lax.rsqrt(var + GN_EPS)).reshape(bsz, seq_len, D_RWKV) * lnx_g + lnx_b
    bonus = jnp.sum(r4 * k4 * r_k, axis=-1, keepdims=True) * v4
    y = (y + bonus.reshape(bsz, seq_len, D_RWKV)) * g
    return y, s_last

def _layer(h, pe, st, w):
    ssm_re0, ssm_im0, rwkv0, shift0, conv0 = st
    (norm1_g, w_in, shift_mu, lam_re, lam_im, log_dt, b_re, b_im, c_re, c_im, d_skip,
     w_glu, b_glu, w0, w2, a0, a2, g2, k_k, k_a, r_k, lnx_g, lnx_b, w_out,
     norm2_g, w_up, conv_w, conv_b, w_down, w_ple, w_pg) = w
    f32 = jnp.float32
    seq_len = h.shape[1]
    x = _rmsnorm(h, norm1_g)
    proj = x @ w_in.astype(f32)
    u = proj[..., :D_SSM]
    zr = proj[..., D_SSM:]
    prev = jnp.concatenate([shift0.astype(f32)[:, None], zr[:, :-1]], axis=1)
    z = zr + (prev - zr) * shift_mu
    y_a, hre, him = _s5(u, ssm_re0.astype(f32), ssm_im0.astype(f32), lam_re, lam_im, log_dt,
                        b_re, b_im, c_re, c_im, d_skip, w_glu, b_glu)
    y_b, s_last = _rwkv7(z, rwkv0.astype(f32), w0, w2, a0, a2, g2, k_k, k_a, r_k, lnx_g, lnx_b)
    h = h + jnp.concatenate([y_a, y_b], axis=-1) @ w_out
    x2 = _rmsnorm(h, norm2_g)
    up = x2 @ w_up
    val, gate = up[..., :D_FF], up[..., D_FF:]
    gate_full = jnp.concatenate([conv0.astype(f32), gate], axis=1)
    conv = conv_b + sum(gate_full[:, j:j + seq_len] * conv_w[j] for j in range(CONV_W))
    h = h + (jax.nn.silu(conv) * val) @ w_down
    h = h + (pe.astype(f32) @ w_ple) * jax.nn.sigmoid(h @ w_pg)
    new_st = (hre, him, s_last, zr[:, -1], gate_full[:, -(CONV_W - 1):])
    return h, new_st

def setup_inputs(seed: int = 0) -> dict:
    key = jax.random.key(seed)
    ks = iter(jax.random.split(key, 64))
    f32 = jnp.float32
    nrm = lambda shape, s: jax.random.normal(next(ks), shape, f32) * s
    uni = lambda shape, lo, hi: jax.random.uniform(next(ks), shape, f32, lo, hi)
    G, P, H, N = N_SSM_GROUPS, SSM_STATE, N_RWKV_HEADS, RWKV_HEAD
    lam_im_init = jnp.broadcast_to(math.pi * jnp.arange(P, dtype=f32), (DEPTH, G, P))
    return {
        'x_prompt': nrm((BATCH, SEQ, D_MODEL), 1.0),
        'x_sample': nrm((DEC_BATCH, DEC_SEQ, D_MODEL), 1.0),
        'p_prompt': nrm((DEPTH, BATCH, SEQ, D_PLE), 1.0),
        'p_sample': nrm((DEPTH, DEC_BATCH, DEC_SEQ, D_PLE), 1.0),
        'state_ssm_re': nrm((DEPTH, DEC_BATCH, G, P), 0.1),
        'state_ssm_im': nrm((DEPTH, DEC_BATCH, G, P), 0.1),
        'state_rwkv': nrm((DEPTH, DEC_BATCH, H, N, N), 0.1),
        'state_shift': nrm((DEPTH, DEC_BATCH, N_SHIFT), 1.0),
        'state_conv': nrm((DEPTH, DEC_BATCH, CONV_W - 1, D_FF), 1.0),
        'norm1_g': 1.0 + nrm((DEPTH, D_MODEL), 0.02),
        'w_in': nrm((DEPTH, D_MODEL, N_IN), D_MODEL ** -0.5),
        'shift_mu': uni((DEPTH, N_SHIFT), 0.0, 1.0),
        'ssm_lam_re': -0.5 + nrm((DEPTH, G, P), 1e-3),
        'ssm_lam_im': lam_im_init + nrm((DEPTH, G, P), 1e-3),
        'ssm_log_dt': uni((DEPTH, G), math.log(1e-3), math.log(1e-1)),
        'ssm_b_re': nrm((DEPTH, G, P, SSM_GROUP), (2 * SSM_GROUP) ** -0.5),
        'ssm_b_im': nrm((DEPTH, G, P, SSM_GROUP), (2 * SSM_GROUP) ** -0.5),
        'ssm_c_re': nrm((DEPTH, G, SSM_GROUP, P), P ** -0.5),
        'ssm_c_im': nrm((DEPTH, G, SSM_GROUP, P), P ** -0.5),
        'ssm_d': nrm((DEPTH, D_SSM), 1.0),
        'ssm_w_glu': nrm((DEPTH, D_SSM, D_SSM), D_SSM ** -0.5),
        'ssm_b_glu': nrm((DEPTH, D_SSM), 0.01),
        'rwkv_w0': uni((DEPTH, D_RWKV), -6.0, -1.0),
        'rwkv_w2': nrm((DEPTH, DECAY_LORA, D_RWKV), 0.1 * DECAY_LORA ** -0.5),
        'rwkv_a0': nrm((DEPTH, D_RWKV), 0.1),
        'rwkv_a2': nrm((DEPTH, AAA_LORA, D_RWKV), 0.1 * AAA_LORA ** -0.5),
        'rwkv_g2': nrm((DEPTH, GATE_LORA, D_RWKV), GATE_LORA ** -0.5),
        'rwkv_k_k': 0.85 + nrm((DEPTH, D_RWKV), 0.02),
        'rwkv_k_a': 1.0 + nrm((DEPTH, D_RWKV), 0.02),
        'rwkv_r_k': nrm((DEPTH, H, N), 0.1),
        'rwkv_lnx_g': 1.0 + nrm((DEPTH, D_RWKV), 0.02),
        'rwkv_lnx_b': nrm((DEPTH, D_RWKV), 0.01),
        'w_out': nrm((DEPTH, D_MIX, D_MODEL), D_MIX ** -0.5),
        'norm2_g': 1.0 + nrm((DEPTH, D_MODEL), 0.02),
        'w_up': nrm((DEPTH, D_MODEL, 2 * D_FF), D_MODEL ** -0.5),
        'conv_w': nrm((DEPTH, CONV_W, D_FF), CONV_W ** -0.5),
        'conv_b': nrm((DEPTH, D_FF), 0.01),
        'w_down': nrm((DEPTH, D_FF, D_MODEL), D_FF ** -0.5),
        'w_ple': nrm((DEPTH, D_PLE, D_MODEL), D_PLE ** -0.5),
        'w_pg': nrm((DEPTH, D_MODEL, D_MODEL), D_MODEL ** -0.5),
        'final_g': 1.0 + nrm((D_MODEL,), 0.02),
    }

def reference(x_prompt, x_sample, p_prompt, p_sample, state_ssm_re, state_ssm_im, state_rwkv,
              state_shift, state_conv, norm1_g, w_in, shift_mu, ssm_lam_re, ssm_lam_im,
              ssm_log_dt, ssm_b_re, ssm_b_im, ssm_c_re, ssm_c_im, ssm_d, ssm_w_glu, ssm_b_glu,
              rwkv_w0, rwkv_w2, rwkv_a0, rwkv_a2, rwkv_g2, rwkv_k_k, rwkv_k_a, rwkv_r_k,
              rwkv_lnx_g, rwkv_lnx_b, w_out, norm2_g, w_up, conv_w, conv_b, w_down, w_ple,
              w_pg, final_g):
    f32 = jnp.float32
    weights = (norm1_g, w_in, shift_mu, ssm_lam_re, ssm_lam_im, ssm_log_dt, ssm_b_re, ssm_b_im,
               ssm_c_re, ssm_c_im, ssm_d, ssm_w_glu, ssm_b_glu, rwkv_w0, rwkv_w2, rwkv_a0,
               rwkv_a2, rwkv_g2, rwkv_k_k, rwkv_k_a, rwkv_r_k, rwkv_lnx_g, rwkv_lnx_b, w_out,
               norm2_g, w_up, conv_w, conv_b, w_down, w_ple, w_pg)
    bp = x_prompt.shape[0]
    zero_st = (jnp.zeros((bp, N_SSM_GROUPS, SSM_STATE), f32),
               jnp.zeros((bp, N_SSM_GROUPS, SSM_STATE), f32),
               jnp.zeros((bp, N_RWKV_HEADS, RWKV_HEAD, RWKV_HEAD), f32),
               jnp.zeros((bp, N_SHIFT), f32),
               jnp.zeros((bp, CONV_W - 1, D_FF), f32))
    hp = x_prompt.astype(f32)
    hs = x_sample.astype(f32)
    new_p = [[] for _ in range(5)]
    new_s = [[] for _ in range(5)]
    for i in range(DEPTH):
        w_i = tuple(t[i].astype(f32) for t in weights)
        hp, stp = _layer(hp, p_prompt[i], zero_st, w_i)
        st_in = (state_ssm_re[i], state_ssm_im[i], state_rwkv[i], state_shift[i], state_conv[i])
        hs, sts = _layer(hs, p_sample[i], st_in, w_i)
        for j in range(5):
            new_p[j].append(stp[j])
            new_s[j].append(sts[j])
    y_prompt = _rmsnorm(hp, final_g).astype(x_prompt.dtype)
    y_sample = _rmsnorm(hs, final_g).astype(x_sample.dtype)
    ssm_re_p = jnp.stack(new_p[0]).astype(state_ssm_re.dtype)
    ssm_im_p = jnp.stack(new_p[1]).astype(state_ssm_im.dtype)
    rwkv_p = jnp.stack(new_p[2]).astype(state_rwkv.dtype)
    shift_p = jnp.stack(new_p[3]).astype(state_shift.dtype)
    conv_p = jnp.stack(new_p[4]).astype(state_conv.dtype)
    ssm_re_s = jnp.stack(new_s[0]).astype(state_ssm_re.dtype)
    ssm_im_s = jnp.stack(new_s[1]).astype(state_ssm_im.dtype)
    rwkv_s = jnp.stack(new_s[2]).astype(state_rwkv.dtype)
    shift_s = jnp.stack(new_s[3]).astype(state_shift.dtype)
    conv_s = jnp.stack(new_s[4]).astype(state_conv.dtype)
    return (y_prompt, y_sample, ssm_re_p, ssm_im_p, rwkv_p, shift_p, conv_p,
            ssm_re_s, ssm_im_s, rwkv_s, shift_s, conv_s)


_drawn_inputs = setup_inputs


def setup_inputs(seed=0):
    import zlib

    import numpy as np

    out = dict(_drawn_inputs(seed))
    spreads = {}
    factors = {'ssm_lam_re': 64.0,
     'ssm_b_glu': 64.0,
     'rwkv_w2': 8.0,
     'rwkv_k_k': 2.733,
     'rwkv_lnx_g': 6.879,
     'rwkv_lnx_b': 28.665,
     'norm2_g': 2.732,
     'conv_b': 8.0,
     'ssm_c_re': 6.229,
     'ssm_c_im': 6.198}
    for name, (base, spread) in spreads.items():
        noise = np.random.default_rng([zlib.crc32(name.encode()), seed]).standard_normal(out[name].shape)
        drawn = base * np.exp(spread * noise) if base else spread * noise
        out[name] = __import__('jax').numpy.asarray(drawn.astype(out[name].dtype))
    for name, factor in factors.items():
        out[name] = (out[name] * factor).astype(out[name].dtype)
    return out
```

```python
import math
from contextlib import ExitStack

import concourse.bass as bass
from concourse import mybir

P = 128
F32 = mybir.dt.float32
I32 = mybir.dt.int32
ALU = mybir.AluOpType
ACT = mybir.ActivationFunctionType
AX = mybir.AxisListType

D = 1024
KD = D // P
SEQ, DB, DS = 2048, 8, 8
T = SEQ + DB * DS
TW = 352
NT = T // TW
DSSM, DRW = 512, 512
KU, KR = DSSM // P, DRW // P
ZT = 14
KIN = KU + ZT
FF = 2816
KF = FF // P
PLE = 256
KP = PLE // P
CONV = 3
RMS_EPS, GN_EPS, L2_EPS = 1e-6, 64e-5, 1e-12
LASTP = SEQ - (NT - 1) * TW


class Env:

    def __init__(self, nc, ctx, tag):
        self.nc, self.ctx, self.tag = nc, ctx, tag

    def sb(self, name, shape, dt=F32):
        return self.ctx.enter_context(self.nc.sbuf_tensor(f"{self.tag}_{name}", shape, dt))

    def ps(self, name, shape):
        return self.ctx.enter_context(self.nc.psum_tensor(f"{self.tag}_{name}", shape, F32))

    def sem(self, name):
        return self.ctx.enter_context(self.nc.semaphore(f"{self.tag}_{name}"))


def bcast(ap, n):
    p, a = ap.shape
    return ap.unsqueeze(2).to_broadcast([p, a, n])


def tok(n):
    return slice(n * TW, (n + 1) * TW)


def project_in(nc, ins, scratch, u):
    with ExitStack() as ctx:
        e = Env(nc, ctx, "in")
        w = e.sb("w", [P, KD, KIN * P])
        xn = e.sb("xn", [P, KD, T])
        sq = e.sb("sq", [P, KD, TW])
        ssum = e.sb("ssum", [P, TW])
        rms = e.sb("rms", [P, TW])
        zout = e.sb("zout", [P, ZT, TW])
        g = e.sb("g", [P, KD])
        eps = e.sb("eps", [P, 1])
        ones = e.sb("ones", [P, P])
        pn = [e.ps(f"pn{i}", [P, 512]) for i in range(2)]
        pp = [e.ps(f"pp{i}", [P, 512]) for i in range(6)]
        x_in = [e.sem(f"x_in{n}") for n in range(NT)]
        w_in = [e.sem(f"w_in{k}") for k in range(KD)]
        g_in = e.sem("g_in")
        const_ready = e.sem("const_ready")
        sq_ready, ssum_ready, ms_ready = e.sem("sq_ready"), e.sem("ssum_ready"), e.sem("ms_ready")
        rms_ready, inv_ready, xn_ready = e.sem("rms_ready"), e.sem("inv_ready"), e.sem("xn_ready")
        proj_ready = e.sem("proj_ready")
        act_out, dve_out = e.sem("act_out"), e.sem("dve_out")
        z_stored = [e.sem(f"z_stored{h}") for h in range(2)]
        HZ = ZT // 2
        DVE_M = [m for m in range(KIN) if m % 2]
        ACT_M = [m for m in range(KIN) if m % 2 == 0]

        with nc.Block() as block:
            @block.sync
            def _(sp):
                for n in range(NT):
                    sp.dma_start(xn[:, :, tok(n)], ins["xT"][:, :, tok(n)]).then_inc(x_in[n], 16)
                    if n == 0:
                        sp.dma_start(g[:], ins["norm1_g"]).then_inc(g_in, 16)
                        for k in range(KD):
                            sp.dma_start(w[:, k, :], ins["w_in"][k]).then_inc(w_in[k], 16)
                dst = scratch["zr"].rearrange("z p t -> p z t")
                for n in range(NT):
                    for h in range(2):
                        last = KU + (h + 1) * HZ
                        sp.wait_ge(act_out, n * len(ACT_M) + sum(m < last for m in ACT_M))
                        sp.wait_ge(dve_out, n * len(DVE_M) + sum(m < last for m in DVE_M))
                        sp.dma_start(dst[:, h * HZ:(h + 1) * HZ, tok(n)],
                                     zout[:, h * HZ:(h + 1) * HZ, :]).then_inc(z_stored[h], 16)
                for h in range(2):
                    sp.wait_ge(z_stored[h], 16 * (NT + 1))

            @block.gpsimd
            def _(pool):
                pool.memset(ones[:], 1.0 / D).then_inc(const_ready, 1)
                pool.memset(eps[:], RMS_EPS).then_inc(const_ready, 1)
                for h in range(2):
                    pool.sem_inc(z_stored[h], 16)

            def copy_out(eng, n, m, out_sem):
                eng.wait_ge(proj_ready, n * KIN + m + 1)
                if m < KU:
                    dst = u[:, m, bass.ds(n * TW, TW)]
                else:
                    if (m - KU) % HZ < 2:
                        eng.wait_ge(z_stored[(m - KU) // HZ], 16 * (n + 1))
                    dst = zout[:, m - KU, :]
                src = pp[m % 6][:, 0:TW]
                if eng is nc.scalar or eng.engine == nc.scalar.engine:
                    eng.copy(dst, src).then_inc(out_sem, 1)
                else:
                    eng.tensor_copy(dst, src).then_inc(out_sem, 1)

            @block.scalar
            def _(act):
                act.wait_ge(const_ready, 2)
                for n in range(NT):
                    act.wait_ge(x_in[n], 16)
                    if n:
                        act.wait_ge(ssum_ready, n)
                    act.square(sq[:], xn[:, :, tok(n)]).then_inc(sq_ready, 1)
                    act.wait_ge(ms_ready, n + 1)
                    if n:
                        act.wait_ge(inv_ready, n)
                    act.activation(rms[:], pn[n % 2][:, 0:TW], ACT.Sqrt, bias=eps[:, 0:1]).then_inc(rms_ready, 1)
                with act.Fori(0, NT) as n:
                    for m in ACT_M:
                        copy_out(act, n, m, act_out)

            @block.vector
            def _(dve):
                dve.wait_ge(g_in, 16)
                for n in range(NT):
                    dve.wait_ge(sq_ready, n + 1)
                    if n:
                        dve.wait_ge(ms_ready, n)
                    dve.tensor_reduce(ssum[:], sq[:].rearrange("p k t -> p t k"), AX.X, ALU.add).then_inc(ssum_ready, 1)
                    dve.wait_ge(rms_ready, n + 1)
                    dve.reciprocal(rms[:], rms[:]).then_inc(inv_ready, 1)
                    dve.wait_ge(inv_ready, n + 1)
                    for k in range(KD):
                        xk = xn[:, k, tok(n)]
                        dve.scalar_tensor_tensor(xk, xk, g[:, k:k + 1], rms[:], ALU.mult, ALU.mult).then_inc(xn_ready, 1)
                with dve.Fori(0, NT) as n:
                    for m in DVE_M:
                        copy_out(dve, n, m, dve_out)

            @block.tensor
            def _(pe):
                pe.wait_ge(const_ready, 2)
                for n in range(NT):
                    pe.wait_ge(ssum_ready, n + 1)
                    if n >= 2:
                        pe.wait_ge(rms_ready, n - 1)
                    pe.matmul(pn[n % 2][:, 0:TW], ones[:], ssum[:], start=True, stop=True).then_inc(ms_ready, 1)
                for k in range(KD):
                    pe.wait_ge(w_in[k], 16)
                pe.wait_ge(xn_ready, KD * NT)
                def project(n, first):
                    for m in range(KIN):
                        back = 6
                        if not first or m >= back:
                            q, r = (n, m - back) if m >= back else (n - 1, m - back + KIN)
                            sem, lot = (act_out, ACT_M) if r in ACT_M else (dve_out, DVE_M)
                            pe.wait_ge(sem, q * len(lot) + lot.index(r) + 1)
                        for k in range(KD):
                            mm = pe.matmul(pp[m % 6][:, 0:TW], w[:, k, m * P:(m + 1) * P], xn[:, k, bass.ds(n * TW, TW)] if not first else xn[:, k, tok(0)],
                                           start=(k == 0), stop=(k == KD - 1))
                        mm.then_inc(proj_ready, 1)
                project(0, True)
                with pe.Fori(1, NT) as n:
                    project(n, False)


def mix_out(nc, ins, y, hT, xn):
    with ExitStack() as ctx:
        e = Env(nc, ctx, "mo")
        w = e.sb("w", [P, KD, D])
        sq = e.sb("sq", [P, KD, TW])
        ssum = e.sb("ssum", [P, TW])
        rms = e.sb("rms", [P, TW])
        g = e.sb("g", [P, KD])
        eps = e.sb("eps", [P, 1])
        ones = e.sb("ones", [P, P])
        pn = [e.ps(f"pn{i}", [P, 512]) for i in range(2)]
        pp = [e.ps(f"pp{i}", [P, 512]) for i in range(6)]
        x_in = [e.sem(f"x_in{n}") for n in range(NT)]
        w_in = [e.sem(f"w_in{k}") for k in range(KD)]
        g_in, const_ready = e.sem("g_in"), e.sem("const_ready")
        out_ready, h_ready = e.sem("out_ready"), e.sem("h_ready")
        sq_ready, ssum_ready, ms_ready = e.sem("sq_ready"), e.sem("ssum_ready"), e.sem("ms_ready")
        rms_ready, inv_ready, xn_ready = e.sem("rms_ready"), e.sem("inv_ready"), e.sem("xn_ready")

        with nc.Block() as block:
            @block.sync
            def _(sp):
                for k in range(KD):
                    sp.dma_start(w[:, k, :], ins["w_out"][k]).then_inc(w_in[k], 16)
                    if k < NT:
                        sp.dma_start(hT[:, :, tok(k)], ins["xT"][:, :, tok(k)]).then_inc(x_in[k], 16)
                sp.dma_start(g[:], ins["norm2_g"]).then_inc(g_in, 16)

            @block.gpsimd
            def _(pool):
                pool.memset(ones[:], 1.0 / D).then_inc(const_ready, 1)
                pool.memset(eps[:], RMS_EPS).then_inc(const_ready, 1)

            @block.scalar
            def _(act):
                act.wait_ge(const_ready, 2)
                for n in range(NT):
                    act.wait_ge(h_ready, KD * (n + 1))
                    if n:
                        act.wait_ge(ssum_ready, n)
                    act.square(sq[:], hT[:, :, tok(n)]).then_inc(sq_ready, 1)
                    act.wait_ge(ms_ready, n + 1)
                    if n:
                        act.wait_ge(xn_ready, KD * n)
                    act.activation(rms[:], pn[n % 2][:, 0:TW], ACT.Sqrt, bias=eps[:, 0:1]).then_inc(rms_ready, 1)

            @block.vector
            def _(dve):
                def residual(n):
                    dve.wait_ge(x_in[n], 16)
                    for m in range(KD):
                        i = n * KD + m
                        dve.wait_ge(out_ready, i + 1)
                        hm = hT[:, m, tok(n)]
                        dve.tensor_tensor(hm, pp[i % 6][:, 0:TW], hm, ALU.add).then_inc(h_ready, 1)

                def norm_sum(n):
                    dve.wait_ge(sq_ready, n + 1)
                    if n:
                        dve.wait_ge(ms_ready, n)
                    dve.tensor_reduce(ssum[:], sq[:].rearrange("p k t -> p t k"), AX.X, ALU.add).then_inc(ssum_ready, 1)

                def norm_apply(n):
                    dve.wait_ge(rms_ready, n + 1)
                    dve.reciprocal(rms[:], rms[:]).then_inc(inv_ready, 1)
                    dve.wait_ge(inv_ready, n + 1)
                    for k in range(KD):
                        dve.scalar_tensor_tensor(xn[:, k, tok(n)], hT[:, k, tok(n)], g[:, k:k + 1], rms[:],
                                                 ALU.mult, ALU.mult).then_inc(xn_ready, 1)

                dve.wait_ge(g_in, 16)
                for n in range(NT):
                    residual(n)
                    norm_sum(n)
                    norm_apply(n)

            @block.tensor
            def _(pe):
                pe.wait_ge(const_ready, 2)

                def mean_square(n):
                    pe.wait_ge(ssum_ready, n + 1)
                    if n >= 2:
                        pe.wait_ge(rms_ready, n - 1)
                    pe.matmul(pn[n % 2][:, 0:TW], ones[:], ssum[:], start=True, stop=True).then_inc(ms_ready, 1)

                for n in range(NT):
                    for m in range(KD):
                        i = n * KD + m
                        if i >= 6:
                            pe.wait_ge(h_ready, i - 5)
                        for k in range(KD):
                            if i == 0:
                                pe.wait_ge(w_in[k], 16)
                            mm = pe.matmul(pp[i % 6][:, 0:TW], w[:, k, m * P:(m + 1) * P], y[k // KU][:, k % KU, tok(n)],
                                           start=(k == 0), stop=(k == KD - 1))
                        mm.then_inc(out_ready, 1)
                        if m == 4 and n:
                            mean_square(n - 1)
                mean_square(NT - 1)


def wait_count(eng, sem, turn, per, c):
    if isinstance(turn, int):
        if turn * per + c > 0:
            eng.wait_ge(sem, turn * per + c)
    else:
        eng.wait_ge(sem, turn * per + c)


def conv_ffn(nc, ins, outs, hT, xn):
    G = 2
    NG = KF // G
    GB = DS + 2
    with ExitStack() as ctx:
        e = Env(nc, ctx, "ff")
        wg = [e.sb(f"wg{q}", [P, KD, P]) for q in range(G)]
        wv = [e.sb(f"wv{q}", [P, KD, P]) for q in range(G)]
        wd = [e.sb(f"wd{q}", [P, D]) for q in range(G)]
        f = e.sb("f", [P, G, T])
        gp = e.sb("gp", [P, 2 + SEQ])
        gs = e.sb("gs", [P, DB, GB])
        cv = e.sb("cv", [P, 2, TW])
        sg = e.sb("sg", [P, 2, TW])
        cw = e.sb("cw", [P, KF, 4])
        taps = e.sb("taps", [P, G, 4])
        st = e.sb("st", [P, KF, DB, 2])
        keep_p = e.sb("keep_p", [P, KF, 2])
        keep_s = e.sb("keep_s", [P, KF, DB, 2])
        pg = [e.ps(f"pg{i}", [P, 512]) for i in range(2)]
        pv = [e.ps(f"pv{i}", [P, 512]) for i in range(2)]
        pd = [e.ps(f"pd{i}", [P, 512]) for i in range(4)]
        up_in = [e.sem(f"up_in{q}") for q in range(G)]
        down_in = e.sem("down_in")
        par_in = e.sem("par_in")
        zero_ready = e.sem("zero_ready")
        gate_mm, val_mm, down_mm = e.sem("gate_mm"), e.sem("val_mm"), e.sem("down_mm")
        gate_out = e.sem("gate_out")
        taps_ready = e.sem("taps_ready")
        tap0, tap1, conv_ready = e.sem("tap0"), e.sem("tap1"), e.sem("conv_ready")
        silu_ready, f_ready = e.sem("silu_ready"), e.sem("f_ready")
        h_ready = e.sem("h_ready")
        kept, stored = e.sem("kept"), e.sem("stored")
        NF = G * NT
        ND = NT * KD

        def turns(eng, body):
            body(0)
            with eng.Fori(1, NG) as g:
                body(g)

        with nc.Block() as block:
            @block.sync
            def _(sp):
                sp.dma_start(cw[:], ins["conv_wb"]).then_inc(par_in, 16)
                sp.dma_start(st[:], ins["state_conv"]).then_inc(par_in, 16)
                for g in range(NG):
                    for q in range(G):
                        if g:
                            sp.wait_ge(val_mm, NT * (G * (g - 1) + q + 1))
                        sp.dma_start(wg[q][:], ins["w_gate"][:, :, (G * g + q) * P:(G * g + q + 1) * P]).then_inc(up_in[q], 16)
                        sp.dma_start(wv[q][:], ins["w_val"][:, :, (G * g + q) * P:(G * g + q + 1) * P]).then_inc(up_in[q], 16)
                    if g:
                        sp.wait_ge(down_mm, ND * g)
                    for q in range(G):
                        sp.dma_start(wd[q][:], ins["w_down"][G * g + q]).then_inc(down_in, 16)
                sp.wait_ge(kept, KF)
                sp.dma_start(outs["conv_p"], keep_p[:]).then_inc(stored, 16)
                sp.dma_start(outs["conv_s"], keep_s[:]).then_inc(stored, 16)
                sp.wait_ge(stored, 32)

            @block.gpsimd
            def _(pool):
                pool.memset(gp[:, 0:2], 0.0).then_inc(zero_ready, 1)

            @block.scalar
            def _(act):
                act.wait_ge(zero_ready, 1)

                def turn(g):
                    for i in range(NF):
                        n, b = i % NT, i % 2
                        wait_count(act, gate_mm, g, NF, i + 1)
                        wait_count(act, conv_ready, g, NF, (i // NT - 1) * NT + min(n + 2, NT))
                        if n < NT - 1:
                            act.copy(gp[:, 2 + n * TW:2 + (n + 1) * TW], pg[b][:, 0:TW]).then_inc(gate_out, 1)
                        else:
                            act.copy(gp[:, 2 + n * TW:2 + SEQ], pg[b][:, 0:LASTP])
                            act.copy(gs[:, :, 2:GB], pg[b][:, LASTP:TW].rearrange("p (b s) -> p b s", b=DB)).then_inc(gate_out, 1)
                        wait_count(act, conv_ready, g, NF, i + 1)
                        wait_count(act, f_ready, g, NF, i - 1)
                        act.activation(sg[:, b, :], cv[:, b, :], ACT.Silu).then_inc(silu_ready, 1)
                turns(act, turn)

            @block.vector
            def _(dve):
                dve.wait_ge(par_in, 32)

                def turn(g):
                    for q in range(G):
                        dve.tensor_copy(taps[:, q, :], cw[:, bass.ds(g * G + q, 1), :].rearrange("p a c -> p (a c)")).then_inc(taps_ready, 1)
                    wait_count(dve, taps_ready, g, 2 * G, G)
                    for i in range(NF):
                        q, n, b = i // NT, i % NT, i % 2
                        tap = [taps[:, q, j:j + 1] for j in range(4)]
                        wait_count(dve, gate_out, g, NF, i + 1)
                        wait_count(dve, silu_ready, g, NF, i - 1)
                        c = cv[:, b, :]
                        if n < NT - 1:
                            rows = [(c, lambda j: gp[:, n * TW + j:n * TW + j + TW])]
                        else:
                            ff = bass.ds(g * G + q, 1)
                            dve.tensor_copy(keep_p[:, ff, :].rearrange("p a s -> p (a s)"), gp[:, SEQ:SEQ + 2])
                            dve.tensor_copy(keep_s[:, ff, :, :].rearrange("p a b s -> p (a b) s"), gs[:, :, DS:GB]).then_inc(kept, 1)
                            dve.tensor_copy(gs[:, :, 0:2], st[:, ff, :, :].rearrange("p a b s -> p (a b) s")).then_inc(taps_ready, 1)
                            wait_count(dve, taps_ready, g, 2 * G, G + q + 1)
                            rows = [(c[:, 0:LASTP], lambda j: gp[:, n * TW + j:n * TW + j + LASTP]),
                                    (c[:, LASTP:TW].rearrange("p (b s) -> p b s", b=DB), lambda j: gs[:, :, j:j + DS])]
                        for out, row in rows:
                            last = dve.tensor_scalar(out, row(2), tap[2], tap[3], ALU.mult, ALU.add)
                        last.then_inc(tap0, 1)
                        wait_count(dve, tap0, g, NF, i + 1)
                        for out, row in rows:
                            last = dve.scalar_tensor_tensor(out, row(1), tap[1], out, ALU.mult, ALU.add)
                        last.then_inc(tap1, 1)
                        wait_count(dve, tap1, g, NF, i + 1)
                        for out, row in rows:
                            last = dve.scalar_tensor_tensor(out, row(0), tap[0], out, ALU.mult, ALU.add)
                        last.then_inc(conv_ready, 1)
                        wait_count(dve, silu_ready, g, NF, i + 1)
                        wait_count(dve, val_mm, g, NF, i + 1)
                        dve.tensor_tensor(f[:, q, tok(n)], pv[b][:, 0:TW], sg[:, b, :], ALU.mult).then_inc(f_ready, 1)
                    for i in range(ND):
                        n, m = i // KD, i % KD
                        wait_count(dve, down_mm, g, ND, i + 1)
                        hm = hT[:, m, tok(n)]
                        dve.tensor_tensor(hm, pd[i % 4][:, 0:TW], hm, ALU.add).then_inc(h_ready, 1)
                turns(dve, turn)

            @block.tensor
            def _(pe):
                def turn(g):
                    for i in range(NF):
                        q, n, b = i // NT, i % NT, i % 2
                        if n == 0:
                            wait_count(pe, up_in[q], g, 32, 32)
                        wait_count(pe, gate_out, g, NF, i - 1)
                        for k in range(KD):
                            mm = pe.matmul(pg[b][:, 0:TW], wg[q][:, k, :], xn[:, k, tok(n)], start=(k == 0), stop=(k == KD - 1))
                        mm.then_inc(gate_mm, 1)
                        wait_count(pe, f_ready, g, NF, i - 1)
                        for k in range(KD):
                            mm = pe.matmul(pv[b][:, 0:TW], wv[q][:, k, :], xn[:, k, tok(n)], start=(k == 0), stop=(k == KD - 1))
                        mm.then_inc(val_mm, 1)
                    wait_count(pe, down_in, g, 16 * G, 16 * G)
                    for i in range(ND):
                        n, m = i // KD, i % KD
                        if m == 0:
                            wait_count(pe, f_ready, g, NF, NT + n + 1)
                        wait_count(pe, h_ready, g, ND, i - 3)
                        for q in range(G):
                            mm = pe.matmul(pd[i % 4][:, 0:TW], wd[q][:, m * P:(m + 1) * P], f[:, q, tok(n)], start=(q == 0), stop=(q == G - 1))
                        mm.then_inc(down_mm, 1)
                turns(pe, turn)


def gated_embedding(nc, ins, outs, hT, mix):
    with ExitStack() as ctx:
        e = Env(nc, ctx, "pe")
        wpg = e.sb("wpg", [P, KD, D])
        wple = e.sb("wple", [P, KP, D])
        flat = [x[:].rearrange("p k t -> p (k t)") for x in mix]
        n3 = 2 * KD * TW
        h3 = flat[0][:, 0:n3].rearrange("p (b k t) -> p b k t", b=2, k=KD)
        sq = flat[0][:, n3:n3 + KD * TW].rearrange("p (k t) -> p k t", k=KD)
        pt = flat[1][:, 0:KP * T].rearrange("p (k t) -> p k t", k=KP)
        sig = e.sb("sig", [P, 2, TW])
        ssum = e.sb("ssum", [P, TW])
        rms = e.sb("rms", [P, TW])
        g = e.sb("g", [P, KD])
        eps = e.sb("eps", [P, 1])
        ones = e.sb("ones", [P, P])
        pn = [e.ps(f"pn{i}", [P, 512]) for i in range(2)]
        pg = [e.ps(f"pg{i}", [P, 512]) for i in range(3)]
        pl = [e.ps(f"pl{i}", [P, 512]) for i in range(3)]
        w_in = [e.sem(f"w_in{k}") for k in range(KD)]
        ple_in, p_in, g_in, const_ready = e.sem("ple_in"), e.sem("p_in"), e.sem("g_in"), e.sem("const_ready")
        gate_mm, ple_mm = e.sem("gate_mm"), e.sem("ple_mm")
        sig_ready, prod_ready, h_ready = e.sem("sig_ready"), e.sem("prod_ready"), e.sem("h_ready")
        sq_ready, ssum_ready, ms_ready = e.sem("sq_ready"), e.sem("ssum_ready"), e.sem("ms_ready")
        rms_ready, inv_ready, y_ready = e.sem("rms_ready"), e.sem("inv_ready"), e.sem("y_ready")
        y_stored = [e.sem(f"y_stored{b}") for b in range(2)]

        with nc.Block() as block:
            @block.sync
            def _(sp):
                for k in range(KD):
                    sp.dma_start(wpg[:, k, :], ins["w_pg"][k]).then_inc(w_in[k], 16)
                for k in range(KP):
                    sp.dma_start(wple[:, k, :], ins["w_ple"][k]).then_inc(ple_in, 16)
                sp.dma_start(pt, ins["pT"]).then_inc(p_in, 16)
                sp.dma_start(g[:], ins["final_g"]).then_inc(g_in, 16)
                for n in range(NT):
                    sp.wait_ge(y_ready, KD * (n + 1))
                    sp.dma_start(outs["yT"][:, :, tok(n)], h3[:, n % 2]).then_inc(y_stored[n % 2], 16)
                for b in range(2):
                    sp.wait_ge(y_stored[b], 16 * (NT // 2))

            @block.gpsimd
            def _(pool):
                pool.memset(ones[:], 1.0 / D).then_inc(const_ready, 1)
                pool.memset(eps[:], RMS_EPS).then_inc(const_ready, 1)

            @block.scalar
            def _(act):
                act.wait_ge(const_ready, 2)
                for n in range(NT):
                    for m in range(KD):
                        i = n * KD + m
                        act.wait_ge(gate_mm, i + 1)
                        if i >= 2:
                            act.wait_ge(prod_ready, i - 1)
                        act.activation(sig[:, i % 2, :], pg[i % 3][:, 0:TW], ACT.Sigmoid).then_inc(sig_ready, 1)
                    act.wait_ge(h_ready, KD * (n + 1))
                    if n:
                        act.wait_ge(ssum_ready, n)
                    act.square(sq, h3[:, n % 2]).then_inc(sq_ready, 1)
                    act.wait_ge(ms_ready, n + 1)
                    if n:
                        act.wait_ge(y_ready, KD * n)
                    act.activation(rms[:], pn[n % 2][:, 0:TW], ACT.Sqrt, bias=eps[:, 0:1]).then_inc(rms_ready, 1)

            @block.vector
            def _(dve):
                dve.wait_ge(g_in, 16)
                for n in range(NT):
                    b = n % 2
                    if n >= 2:
                        dve.wait_ge(y_stored[b], 16 * (n // 2))
                    for m in range(KD):
                        i = n * KD + m
                        dve.wait_ge(sig_ready, i + 1)
                        dve.wait_ge(ple_mm, i + 1)
                        s = sig[:, i % 2, :]
                        dve.tensor_tensor(h3[:, b, m, :], pl[i % 3][:, 0:TW], s, ALU.mult).then_inc(prod_ready, 1)
                        dve.wait_ge(prod_ready, i + 1)
                        dve.tensor_tensor(h3[:, b, m, :], h3[:, b, m, :], hT[:, m, tok(n)], ALU.add).then_inc(h_ready, 1)
                    dve.wait_ge(sq_ready, n + 1)
                    if n:
                        dve.wait_ge(ms_ready, n)
                    dve.tensor_reduce(ssum[:], sq.rearrange("p k t -> p t k"), AX.X, ALU.add).then_inc(ssum_ready, 1)
                    dve.wait_ge(rms_ready, n + 1)
                    dve.reciprocal(rms[:], rms[:]).then_inc(inv_ready, 1)
                    dve.wait_ge(inv_ready, n + 1)
                    for k in range(KD):
                        y = h3[:, b, k, :]
                        dve.scalar_tensor_tensor(y, y, g[:, k:k + 1], rms[:], ALU.mult, ALU.mult).then_inc(y_ready, 1)

            @block.tensor
            def _(pe):
                pe.wait_ge(const_ready, 2)
                pe.wait_ge(ple_in, 16 * KP)
                pe.wait_ge(p_in, 16)

                def mean_square(n):
                    pe.wait_ge(ssum_ready, n + 1)
                    if n >= 2:
                        pe.wait_ge(rms_ready, n - 1)
                    pe.matmul(pn[n % 2][:, 0:TW], ones[:], ssum[:], start=True, stop=True).then_inc(ms_ready, 1)

                for n in range(NT):
                    for m in range(KD):
                        i = n * KD + m
                        if i >= 3:
                            pe.wait_ge(prod_ready, i - 2)
                        for k in range(KD):
                            if i == 0:
                                pe.wait_ge(w_in[k], 16)
                            mm = pe.matmul(pg[i % 3][:, 0:TW], wpg[:, k, m * P:(m + 1) * P], hT[:, k, tok(n)], start=(k == 0), stop=(k == KD - 1))
                        mm.then_inc(gate_mm, 1)
                        for k in range(KP):
                            mm = pe.matmul(pl[i % 3][:, 0:TW], wple[:, k, m * P:(m + 1) * P], pt[:, k, tok(n)], start=(k == 0), stop=(k == KP - 1))
                        mm.then_inc(ple_mm, 1)
                        if m == 2 and n:
                            mean_square(n - 1)
                mean_square(NT - 1)


C = 64
Q = 2
TB = C * Q
NB = SEQ // TB
TS = DB * DS
HP = 4
HD = 64
LOGW = math.exp(-0.5)
HALF = [slice(0, HD), slice(HD, P)]

PREP_DVE = ["dz", "zmu", "z", "sg", "kk", "w", "a", "ld", "L", "Lp", "t0", "t1", "kp", "aa", "rk0", "rk",
            "nmax", "ninv", "kkn", "b", "bonus"]
PREP_ACT = ["th", "sx", "kk2", "wt", "at", "g", "e1", "e2", "e3", "nrm"]
PREP_PE = ["w", "a", "g", "ss", "bonus"]
STAGES = ["AabT", "Aab", "AqbT", "D2", "Dt2", "AakT", "D4", "Dt4", "X2", "AqkT", "D8", "X3", "Bt", "X4", "Kt", "X", "Vt",
          "Z32", "X32t", "X32", "Z64", "X64t", "RH", "U", "S", "Y"]
INTRA = STAGES[:22]
DVE_OUT = ["Dt", "Xt", "D", "O32", "O64", "AqbT", "AakT", "X2", "AqkT", "X3", "X4", "X32t", "X32", "X64t", "Sadd", "S"]
ACT_OUT = ["D2", "Dt2", "D4", "Dt4", "D8", "Bt", "Kt", "X", "Vt", "Z32", "Z64", "RH", "U", "Ylo", "Y"]
COPIED = {"AabT": "Dt", "Aab": "O64", "S": "Sadd"}
HAT_DVE = ["b", "a", "k"]
POST_DVE = ["d", "inv", "dn", "dg", "db", "dbonus", "y"]
NBANK = 3


def at(turn, order, name):
    return turn * len(order) + order.index(name) + 1


def delta_rule(nc, ins, outs, scratch, yb):
    with ExitStack() as ctx:
        e = Env(nc, ctx, "rw")
        w2 = e.sb("w2", [P, DRW])
        g2 = e.sb("g2", [P, DRW])
        mu = e.sb("mu", [P, ZT])
        col = {n: e.sb(n, [P, HP]) for n in ("w0", "a0", "k_k", "k_a", "r_k", "lnx_g", "lnx_b")}
        kah, ka1 = e.sb("kah", [P, HP]), e.sb("ka1", [P, HP])
        masks = e.sb("masks", [P, 13, P])
        bd64 = e.sb("bd64", [P, P])
        rows8 = e.sb("rows8", [P, DB])
        seg = e.sb("seg", [P, 2, HP * TB])
        geps = e.sb("geps", [P, 1])
        Z = e.sb("Z", [P, ZT * (TB + 1)])
        z = e.sb("z", [P, ZT * TB])
        names = ("kk", "kk2", "w", "a", "L", "Lp", "E2", "E3", "t", "kp", "kkn", "b", "bonus", "g")
        B = {n: e.sb("p_" + n, [P, HP * TB]) for n in names}
        B |= {n: e.sb("p_" + n, [P, TB]) for n in ("th", "sx")}
        B |= {"nrm": B["kk2"], "ld": B["w"], "E1": B["Lp"], "rk": B["t"], "aa": B["a"]}
        bonus_h, g_h = e.sb("bonus_h", [P, HP * TB]), e.sb("g_h", [P, HP * TB])
        pc = e.sb("pc", [P, HP, DB])
        yt, ysq = e.sb("yt", [P, HP * TB]), e.sb("ysq", [P, HP * TB])
        yd, ysd = yt, ysq
        before_smp = e.sb("before_smp", [P, ZT, DB])
        keep = e.sb("keep", [P, ZT, 1 + DB])
        cn = ("aT", "bT", "kT", "rT", "vT", "Dt", "D", "O32", "O64", "AqbT", "AakT", "AqkT", "D2", "Dt2", "D4", "Dt4", "Xt")
        M = [{n: e.sb(f"{n}{q}", [P, HP, P]) for n in cn} for q in range(Q)]
        for m in M:
            m.update(D8=m["Dt"], Z=m["D"], Kt=m["D2"], Bt=m["Dt2"], X=m["D4"], Vt=m["Dt4"], RH=m["O32"], U=m["O64"])
        S = [e.sb(f"S{q}", [P, HP, P]) for q in range(Q)]
        Sb = [M[1][n] for n in ("aT", "bT", "kT", "rT", "vT", "AqbT", "AakT", "AqkT")]
        bank = [[e.ps(f"bank{q}{i}", [P, HP, P]) for i in range(NBANK)] for q in range(Q)]
        side = [e.ps(f"side{i}", [P, HP * P]) for i in range(2)]

        par_in, z_in = e.sem("par_in"), e.sem("z_in")
        setup, zero = e.sem("setup"), e.sem("zero")
        prep_dve, prep_act, prep_pe = e.sem("prep_dve"), e.sem("prep_act"), e.sem("prep_pe")
        hats_dve = e.sem("hats_dve")
        hats_pool = [e.sem(f"hats_pool{q}") for q in range(Q)]
        mm = [e.sem(f"mm{q}") for q in range(Q)]
        dve_out = [e.sem(f"dve_out{q}") for q in range(Q)]
        act_out = [e.sem(f"act_out{q}") for q in range(Q)]
        post_pe, post_act, post_dve = e.sem("post_pe"), e.sem("post_act"), e.sem("post_dve")
        keep_ready, stored = e.sem("keep_ready"), e.sem("stored")
        smp_in, smp_pe, smp_dve, smp_act = e.sem("smp_in"), e.sem("smp_pe"), e.sem("smp_dve"), e.sem("smp_act")
        hats_a, hats_b = e.sem("hats_a"), e.sem("hats_b")
        hats_act = [e.sem(f"hats_act{q}") for q in range(Q)]
        BD, MD, MO32, MO64, MDT, MSU, MU, ID, SD, SDT, SSU, SU, NONE = range(13)
        FIRST, SAMPLES = 0, NB

        def is_first(t):
            return isinstance(t, int) and t == FIRST

        def is_samples(t):
            return isinstance(t, int) and t == SAMPLES

        STATE_AT = {"RH": 1, "U": 4, "S": 6, "Y": 8}
        HATS_AT = 13

        def schedule(eng, half):
            half(FIRST, 0)
            half(FIRST, 1)
            half(1, 0)
            with eng.Fori(1, NB - 2) as t:
                half(t, 1)
                half(t + 1, 0)
            for t in (NB - 2, NB - 1):
                half(t, 1)
                half(t + 1, 0)

        def width(t):
            return TS if is_samples(t) else TB

        def chunks(t):
            return 1 if is_samples(t) else Q

        def v3(buf, W, w=None):
            return buf[:, 0:HP * W].rearrange("p (j t) -> p j t", t=W)

        def zv(i, n, W):
            return z[:, i * W:(i + n) * W].rearrange("p (j t) -> p j t", t=W)

        def mask(m):
            return masks[:, m:m + 1, :].to_broadcast([P, HP, P])

        def copied(stage):
            return COPIED.get(stage, stage)

        def wait_copied(eng, q, t, name):
            name = copied(name)
            if name in DVE_OUT:
                eng.wait_ge(dve_out[q], at(t, DVE_OUT, name))
            else:
                eng.wait_ge(act_out[q], at(t, ACT_OUT, name))

        with nc.Block() as block:
            @block.sync
            def _(sp):
                for dst, name in ((w2, "w2a2"), (g2, "g2"), (mu, "mu"), (masks, "masks"), (rows8, "rows8"), (seg, "seg")):
                    sp.dma_start(dst[:], ins[name]).then_inc(par_in, 16)
                for n, dst in col.items():
                    sp.dma_start(dst[:], ins[n]).then_inc(par_in, 16)
                sp.dma_start(before_smp[:], ins["state_shift"]).then_inc(par_in, 16)
                src = scratch["zr"].rearrange("z p t -> p z t")
                Zp = Z[:].rearrange("p (z t) -> p z t", t=TB + 1)
                sp.dma_start(Zp[:, :, 1:], src[:, :, 0:TB]).then_inc(z_in, 16)
                for t in range(1, NB):
                    sp.wait_ge(prep_dve, at(t - 1, PREP_DVE, "z"))
                    sp.dma_start(Zp[:], src[:, :, t * TB - 1:(t + 1) * TB]).then_inc(z_in, 16)
                Zs = Z[:, 0:ZT * DB * (DS + 1)].rearrange("p (z b s) -> p z b s", b=DB, s=DS + 1)
                sp.wait_ge(prep_dve, at(NB - 1, PREP_DVE, "z"))
                sp.wait_ge(keep_ready, 1)
                for zt in range(ZT):
                    sp.dma_start(Zs[:, zt, :, 1:], src[:, zt, SEQ:T].rearrange("p (b s) -> p b s", b=DB)).then_inc(z_in, 16)
                sp.wait_ge(mm[1], at(NB - 1, STAGES, "Y"))
                for b in range(DB):
                    for h in HALF:
                        sp.dma_start(Sb[b][h, :, h], ins["state_rwkv"][h, b]).then_inc(smp_in, 16)
                sp.wait_ge(keep_ready, 2)
                sp.dma_start(outs["shift"], keep[:]).then_inc(stored, 16)
                sp.wait_ge(dve_out[1], at(NB - 1, DVE_OUT, "S"))
                for h in range(2):
                    sp.dma_start(outs["rwkv_p"][HALF[h]], S[0][HALF[h], :, HALF[h]]).then_inc(stored, 16)
                sp.wait_ge(smp_dve, 4 * DB)
                for b in range(DB):
                    for h in range(2):
                        sp.dma_start(outs["rwkv_s"][HALF[h], b], Sb[b][HALF[h], :, HALF[h]]).then_inc(stored, 16)
                sp.wait_ge(stored, 16 * (3 + 2 * DB))

            @block.gpsimd
            def _(pool):
                pool.memset(S[0][:], 0.0).then_inc(zero, 1)
                pool.memset(Z[:].rearrange("p (z t) -> p z t", t=TB + 1)[:, :, 0:1], 0.0).then_inc(zero, 1)
                for q in range(Q):
                    for n in ("aT", "bT", "kT", "rT", "vT"):
                        pool.memset(M[q][n][:], 0.0).then_inc(zero, 1)
                pool.memset(geps[:], GN_EPS).then_inc(zero, 1)
                pool.wait_ge(zero, 13)

                def hats(t, q):
                    W = width(t)
                    pool.wait_ge(prep_act, at(t, PREP_ACT, "e3"))
                    if not is_first(t):
                        pool.wait_ge(mm[q], at(t - 1, STAGES, "Y"))
                    cq = slice(q * C, (q + 1) * C)
                    for n, h in enumerate(HALF):
                        pool.tensor_tensor(M[q]["rT"][h, :, h], zv(0, 4, W)[h, :, cq], v3(B["E3"], W)[h, :, cq], ALU.mult).then_inc(hats_pool[q], 1)
                        pool.wait_ge(hats_pool[q], 2 * t + n + 1)

                hats(FIRST, 0)
                hats(FIRST, 1)
                with pool.Fori(1, NB - 1) as t:
                    for q in range(Q):
                        hats(t, q)
                hats(NB - 1, 0)
                pool.tensor_copy(keep[:, :, 0:1], Z[:].rearrange("p (z t) -> p z t", t=TB + 1)[:, :, TB:TB + 1]).then_inc(keep_ready, 1)
                pool.wait_ge(keep_ready, 1)
                hats(NB - 1, 1)
                hats(SAMPLES, 0)
                pool.wait_ge(prep_dve, at(SAMPLES, PREP_DVE, "z"))
                Zs = Z[:, 0:ZT * DB * (DS + 1)].rearrange("p (z b s) -> p z b s", b=DB, s=DS + 1)
                pool.tensor_copy(keep[:, :, 1:], Zs[:, :, :, DS]).then_inc(keep_ready, 1)

            @block.vector
            def _(dve):
                dve.wait_ge(par_in, 16 * 14)
                dve.tensor_scalar(kah[:], col["k_a"][:], 0.5, None, ALU.mult).then_inc(setup, 1)
                dve.tensor_scalar(ka1[:], col["k_a"][:], -0.5, 1.0, ALU.mult, ALU.add).then_inc(setup, 1)
                dve.tensor_scalar(bd64[:], masks[:, BD, :], 1.0 / HD, None, ALU.mult).then_inc(setup, 1)
                dve.wait_ge(setup, 3)
                dve.wait_ge(zero, 13)

                def prepare(s, part):
                    W = width(s)
                    b = {n: v3(x, W) for n, x in B.items() if n not in ("th", "sx")}
                    r, k, v = zv(0, 4, W), zv(4, 4, W), zv(8, 4, W)

                    def mine(name):
                        dve.wait_ge(prep_dve, at(s, PREP_DVE, name))

                    def act_did(name):
                        dve.wait_ge(prep_act, at(s, PREP_ACT, name))

                    def pe_did(name):
                        dve.wait_ge(prep_pe, at(s, PREP_PE, name))

                    if part == 0:
                        if is_samples(s):
                            dve.wait_ge(z_in, 16 * (NB + ZT))
                            Zs = Z[:, 0:ZT * DB * (DS + 1)].rearrange("p (z b s) -> p z b s", b=DB, s=DS + 1)
                            dve.tensor_copy(Zs[:, :, :, 0], before_smp[:]).then_inc(setup, 1)
                            dve.wait_ge(setup, 4)
                            before, row = Zs[:, :, :, 0:DS], Zs[:, :, :, 1:]
                            zz = z[:, 0:ZT * W].rearrange("p (z b s) -> p z b s", b=DB, s=DS)
                        else:
                            dve.wait_ge(z_in, 16 * (s + 1))
                            Zp = Z[:].rearrange("p (z t) -> p z t", t=TB + 1)
                            before, row = Zp[:, :, 0:TB], Zp[:, :, 1:]
                            zz = zv(0, ZT, W)
                        if not is_first(s):
                            for q in range(Q):
                                dve.wait_ge(hats_pool[q], s * 2)
                                dve.wait_ge(hats_act[q], s * (2 - q) - (1 - q))
                        dve.tensor_tensor(zz, before, row, ALU.subtract).then_inc(prep_dve, 1)
                        mine("dz")
                        dve.tensor_tensor(zv(0, ZT, W), zv(0, ZT, W), bcast(mu[:], W), ALU.mult).then_inc(prep_dve, 1)
                        mine("zmu")
                        dve.tensor_tensor(zz, zz, row, ALU.add).then_inc(prep_dve, 1)
                    if part == 1:
                        act_did("sx")
                        dve.tensor_scalar(B["sx"][:, 0:W], B["sx"][:, 0:W], 0.5, 0.5, ALU.mult, ALU.add).then_inc(prep_dve, 1)
                        mine("z")
                        dve.tensor_tensor(b["kk"], k, bcast(col["k_k"][:], W), ALU.mult).then_inc(prep_dve, 1)
                    if part == 2:
                        pe_did("w")
                        dve.tensor_tensor(b["w"], v3(side[0], W), bcast(col["w0"][:], W), ALU.add).then_inc(prep_dve, 1)
                        pe_did("a")
                        dve.tensor_tensor(b["a"], v3(side[1], W), bcast(col["a0"][:], W), ALU.add).then_inc(prep_dve, 1)
                    if part == 3:
                        act_did("wt")
                        dve.tensor_scalar(b["ld"], b["w"], -LOGW / 2, -LOGW / 2, ALU.mult, ALU.add).then_inc(prep_dve, 1)
                        mine("ld")
                        dve.tensor_tensor_scan(B["L"][:, 0:HP * W], seg[:, 1 if is_samples(s) else 0, 0:HP * W], B["ld"][:, 0:HP * W], 0.0,
                                               ALU.mult, ALU.add).then_inc(prep_dve, 1)
                        mine("L")
                        dve.tensor_tensor(b["Lp"], b["L"], b["ld"], ALU.subtract).then_inc(prep_dve, 1)
                        act_did("at")
                        dve.tensor_tensor(b["t"], b["a"], bcast(kah[:], W), ALU.mult).then_inc(prep_dve, 1)
                        mine("t0")
                        dve.tensor_tensor(b["t"], b["t"], bcast(ka1[:], W), ALU.add).then_inc(prep_dve, 1)
                        mine("t1")
                        dve.tensor_tensor(b["kp"], k, b["t"], ALU.mult).then_inc(prep_dve, 1)
                        dve.tensor_scalar(b["aa"], b["a"], 0.5, 0.5, ALU.mult, ALU.add).then_inc(prep_dve, 1)
                        mine("kp")
                        dve.tensor_tensor(b["rk"], r, b["kp"], ALU.mult).then_inc(prep_dve, 1)
                        mine("rk0")
                        dve.tensor_tensor(b["rk"], b["rk"], bcast(col["r_k"][:], W), ALU.mult).then_inc(prep_dve, 1)
                    if part == 4:
                        act_did("nrm")
                        dve.tensor_scalar(b["nrm"], b["nrm"], L2_EPS, None, ALU.max).then_inc(prep_dve, 1)
                        mine("nmax")
                        dve.reciprocal(b["nrm"], b["nrm"]).then_inc(prep_dve, 1)
                        mine("ninv")
                        dve.tensor_tensor(b["kkn"], b["kk"], b["nrm"], ALU.mult).then_inc(prep_dve, 1)
                        mine("kkn")
                        dve.tensor_tensor(b["b"], b["kkn"], b["aa"], ALU.mult).then_inc(prep_dve, 1)
                        pe_did("bonus")
                        if not is_first(s):
                            dve.wait_ge(hats_act[0], 2 * s)
                        dve.tensor_tensor(b["bonus"], v3(side[0], W), v, ALU.mult).then_inc(prep_dve, 1)

                def hats(t, q):
                    W = width(t)
                    b = {n: v3(x, W) for n, x in B.items() if n not in ("th", "sx")}
                    dve.wait_ge(prep_act, at(t, PREP_ACT, "e3"))
                    dve.wait_ge(prep_dve, at(t, PREP_DVE, "b"))
                    if not is_first(t):
                        dve.wait_ge(mm[q], at(t - 1, STAGES, "Y"))
                    cq = slice(q * C, (q + 1) * C)
                    m = M[q]
                    for h in HALF:
                        last = dve.tensor_tensor(m["bT"][h, :, h], b["b"][h, :, cq], b["E2"][h, :, cq], ALU.mult)
                    last.then_inc(hats_dve, 1)
                    for h in HALF:
                        last = dve.scalar_tensor_tensor(m["aT"][h, :, h], b["kkn"][h, :, cq], -1.0, b["E1"][h, :, cq], ALU.mult, ALU.mult)
                    last.then_inc(hats_dve, 1)
                    for h in HALF:
                        last = dve.tensor_tensor(m["kT"][h, :, h], b["kp"][h, :, cq], b["E2"][h, :, cq], ALU.mult)
                    last.then_inc(hats_dve, 1)

                def copy_out(q, t, stage):
                    m, smp = M[q], is_samples(t)
                    src = bank[q][STAGES.index(stage) % NBANK][:]
                    dve.wait_ge(mm[q], at(t, STAGES, stage))

                    def masked(name, which):
                        dve.tensor_tensor(m[name][:], src, mask(which), ALU.mult).then_inc(dve_out[q], 1)

                    if stage == "AabT":
                        masked("Dt", SDT if smp else MDT)
                        dve.wait_ge(dve_out[q], at(t, DVE_OUT, "Dt"))
                        dve.tensor_tensor(m["Xt"][:], m["Dt"][:], mask(ID), ALU.add).then_inc(dve_out[q], 1)
                    elif stage == "Aab":
                        masked("D", SD if smp else MD)
                        masked("O32", NONE if smp else MO32)
                        masked("O64", NONE if smp else MO64)
                    elif stage in ("AqbT", "AqkT"):
                        masked(stage, SU if smp else MU)
                    elif stage == "AakT":
                        masked(stage, SSU if smp else MSU)
                    elif stage in ("X2", "X3", "X4", "X32t", "X64t"):
                        dve.tensor_tensor(m["Xt"][:], src, m["Xt"][:], ALU.add).then_inc(dve_out[q], 1)
                    elif stage == "X32":
                        dve.wait_ge(act_out[q], at(t, ACT_OUT, "X"))
                        dve.tensor_tensor(m["X"][:], src, m["X"][:], ALU.add).then_inc(dve_out[q], 1)
                    elif stage == "S":
                        old, new = S[q], S[1 - q]
                        dve.tensor_tensor(new[:], src, old[:], ALU.add).then_inc(dve_out[q], 1)
                        dve.wait_ge(dve_out[q], at(t, DVE_OUT, "Sadd"))
                        dve.wait_ge(hats_act[0], (t + 1) * 2)
                        dve.tensor_tensor(new[:], new[:], pc[:, :, q:q + 1].to_broadcast([P, HP, P]), ALU.mult).then_inc(dve_out[q], 1)

                def finish(t, part):
                    W = width(t)
                    y, d, sd = v3(yt, W), v3(yd, W), v3(ysd, W)

                    def mine(name):
                        dve.wait_ge(post_dve, at(t, POST_DVE, name))

                    if part == 0:
                        dve.wait_ge(post_pe, 2 * t + 1)
                        dve.tensor_tensor(d, y, v3(side[1], W), ALU.subtract).then_inc(post_dve, 1)
                        return
                    dve.wait_ge(post_act, 2 * t + 2)
                    dve.reciprocal(sd, sd).then_inc(post_dve, 1)
                    mine("inv")
                    dve.tensor_tensor(d, d, sd, ALU.mult).then_inc(post_dve, 1)
                    mine("dn")
                    dve.tensor_tensor(d, d, bcast(col["lnx_g"][:], W), ALU.mult).then_inc(post_dve, 1)
                    mine("dg")
                    dve.tensor_tensor(d, d, bcast(col["lnx_b"][:], W), ALU.add).then_inc(post_dve, 1)
                    mine("db")
                    dve.wait_ge(hats_act[0], (t + 1) * 2)
                    dve.tensor_tensor(d, d, v3(bonus_h, W), ALU.add).then_inc(post_dve, 1)
                    mine("dbonus")
                    dve.tensor_tensor(yb[:, :, bass.ds(t * TB, W)], d, v3(g_h, W), ALU.mult).then_inc(post_dve, 1)

                ADD = {"AabT", "Aab", "AqbT", "AakT", "X2", "AqkT", "X3", "X4", "X32t", "X32", "X64t"}
                PREP_AT = {1: 1, 4: 2, 6: 3, 10: 4}

                def half(t, q):
                    before = (t, 0) if q else (t - 1, 1)
                    for i, stage in enumerate(INTRA):
                        if stage in ADD:
                            copy_out(q, t, stage)
                        if i == STATE_AT["S"] and not (q == 0 and is_first(t)):
                            copy_out(before[1], before[0], "S")
                        if q and i in PREP_AT:
                            prepare(t + 1, PREP_AT[i])
                        if q == 0 and not is_first(t):
                            if i == 11:
                                finish(t - 1, 0)
                            if i == 15:
                                finish(t - 1, 1)
                        if i == HATS_AT:
                            if q:
                                hats(t + 1, 0)
                            elif not is_samples(t):
                                hats(t, 1)
                        if i == HATS_AT + 3 and q == 0 and not is_samples(t):
                            prepare(t + 1, 0)

                for part in range(5):
                    prepare(FIRST, part)
                hats(FIRST, 0)
                schedule(dve, half)
                m = M[0]
                for b in range(DB):
                    if b == 0:
                        dve.wait_ge(smp_act, 3)
                        dve.wait_ge(act_out[0], at(SAMPLES, ACT_OUT, "Vt"))
                        dve.wait_ge(smp_pe, 4)
                    dve.tensor_scalar(M[1]["D2"][:], m["U"][:], rows8[:, b:b + 1], None, ALU.mult).then_inc(smp_dve, 1)
                    dve.tensor_scalar(M[1]["Dt2"][:], m["Vt"][:], rows8[:, b:b + 1], None, ALU.mult).then_inc(smp_dve, 1)
                    if b == 0:
                        dve.wait_ge(smp_in, 16 * 2 * DB)
                    dve.wait_ge(smp_pe, 5 + b)
                    dve.tensor_tensor(Sb[b][:], bank[0][b % NBANK][:], Sb[b][:], ALU.add).then_inc(smp_dve, 1)
                    dve.wait_ge(smp_dve, 4 * b + 3)
                    dve.wait_ge(hats_act[0], (SAMPLES + 1) * 2)
                    dve.tensor_tensor(Sb[b][:], Sb[b][:], pc[:, :, b:b + 1].to_broadcast([P, HP, P]), ALU.mult).then_inc(smp_dve, 1)
                finish(SAMPLES, 0)
                finish(SAMPLES, 1)

            @block.scalar
            def _(act):
                act.wait_ge(zero, 13)

                def prepare(s, part):
                    W = width(s)
                    b = {n: v3(x, W) for n, x in B.items() if n not in ("th", "sx")}

                    def dve_did(name):
                        act.wait_ge(prep_dve, at(s, PREP_DVE, name))

                    def pe_did(name):
                        act.wait_ge(prep_pe, at(s, PREP_PE, name))

                    if part == 0:
                        dve_did("z")
                        act.activation(B["th"][0:HD, 0:W], zv(12, 1, W)[0:HD, 0, :], ACT.Tanh).then_inc(prep_act, 1)
                        act.activation(B["sx"][:, 0:W], zv(13, 1, W)[:, 0, :], ACT.Tanh, scale=0.5).then_inc(prep_act, 1)
                    if part == 1:
                        dve_did("kk")
                        act.square(b["kk2"], b["kk"]).then_inc(prep_act, 1)
                    if part == 2:
                        dve_did("w")
                        act.activation(b["w"], b["w"], ACT.Tanh, scale=0.5).then_inc(prep_act, 1)
                        dve_did("a")
                        act.activation(b["a"], b["a"], ACT.Tanh, scale=0.5).then_inc(prep_act, 1)
                    if part == 3:
                        if not is_first(s):
                            act.wait_ge(hats_pool[0], s * 2)
                            act.wait_ge(hats_pool[1], s * 2)
                            act.wait_ge(hats_dve, s * 6)
                        pe_did("g")
                        act.copy(b["g"], v3(side[0], W)).then_inc(prep_act, 1)
                        dve_did("Lp")
                        act.activation(b["E1"], b["Lp"], ACT.Exp).then_inc(prep_act, 1)
                        act.activation(b["E2"], b["L"], ACT.Exp, scale=-1.0).then_inc(prep_act, 1)
                        act.activation(b["E3"], b["L"], ACT.Exp).then_inc(prep_act, 1)
                    if part == 4:
                        pe_did("ss")
                        act.activation(b["nrm"], v3(side[1], W), ACT.Sqrt).then_inc(prep_act, 1)

                def hats(t, q):
                    W = width(t)
                    if not is_first(t):
                        act.wait_ge(mm[q], at(t - 1, STAGES, "Y"))
                    for h in HALF:
                        last = act.copy(M[q]["vT"][h, :, h], zv(8, 4, W)[h, :, q * C:(q + 1) * C])
                    last.then_inc(hats_act[q], 1)

                def keep_back(t):
                    W = width(t)
                    act.wait_ge(prep_dve, at(t, PREP_DVE, "bonus"))
                    if not is_first(t):
                        act.wait_ge(post_dve, at(t - 1, POST_DVE, "y"))
                        act.wait_ge(dve_out[1], at(t - 1, DVE_OUT, "S"))
                    act.copy(bonus_h[:, 0:HP * W], B["bonus"][:, 0:HP * W])
                    act.copy(g_h[:, 0:HP * W], B["g"][:, 0:HP * W])
                    step = DS if is_samples(t) else C
                    act.copy(pc[:, :, 0:W // step], v3(B["E3"], W)[:, :, step - 1::step]).then_inc(hats_act[0], 1)

                def copy_out(q, t, stage):
                    dst = {"Z32": "Z", "Z64": "Z"}.get(stage, stage)
                    act.wait_ge(mm[q], at(t, STAGES, stage))
                    act.copy(M[q][dst][:], bank[q][STAGES.index(stage) % NBANK][:]).then_inc(act_out[q], 1)

                def rows_out(q, t):
                    if q == 0 and not is_first(t):
                        act.wait_ge(post_dve, at(t - 1, POST_DVE, "y"))
                    act.wait_ge(mm[q], at(t, STAGES, "Y"))
                    src = bank[q][STAGES.index("Y") % NBANK]
                    for h in HALF:
                        act.copy(v3(yt, TB)[h, :, q * C:(q + 1) * C], src[h, :, h]).then_inc(act_out[q], 1)

                def finish(t, part):
                    W = width(t)
                    if part == 0:
                        act.wait_ge(post_dve, at(t, POST_DVE, "d"))
                        act.square(v3(ysq, W), v3(yd, W)).then_inc(post_act, 1)
                        return
                    act.wait_ge(post_pe, 2 * t + 2)
                    act.activation(v3(ysd, W), v3(side[0], W), ACT.Sqrt, bias=geps[:, 0:1]).then_inc(post_act, 1)

                PLAIN = {"D2", "Dt2", "D4", "Dt4", "D8", "Bt", "Kt", "X", "Vt", "Z32", "Z64"}
                PREP_AT = {0: 0, 2: 1, 5: 2, 7: 3, 9: 4}

                def half(t, q):
                    before = (t, 0) if q else (t - 1, 1)
                    for i, stage in enumerate(INTRA):
                        if q and i == 0:
                            keep_back(t)
                        if stage in PLAIN:
                            copy_out(q, t, stage)
                        if not (q == 0 and is_first(t)):
                            if i == STATE_AT["RH"]:
                                copy_out(before[1], before[0], "RH")
                            if i == STATE_AT["U"]:
                                copy_out(before[1], before[0], "U")
                            if i == STATE_AT["Y"]:
                                rows_out(before[1], before[0])
                        if q and i in PREP_AT:
                            prepare(t + 1, PREP_AT[i])
                        if q == 0 and not is_first(t):
                            if i == 12:
                                finish(t - 1, 0)
                            if i == 14:
                                finish(t - 1, 1)
                        if i == HATS_AT:
                            if q:
                                hats(t + 1, 0)
                            elif not is_samples(t):
                                hats(t, 1)

                for part in range(5):
                    prepare(FIRST, part)
                hats(FIRST, 0)
                schedule(act, half)
                keep_back(SAMPLES)
                m = M[0]
                act.wait_ge(smp_pe, 1)
                act.copy(m["RH"][:], bank[1][2][:]).then_inc(smp_act, 1)
                act.wait_ge(smp_pe, 2)
                act.copy(m["Z"][:], bank[1][0][:]).then_inc(smp_act, 1)
                act.wait_ge(smp_pe, 3)
                act.copy(m["U"][:], bank[1][2][:]).then_inc(smp_act, 1)
                act.wait_ge(smp_pe, 4)
                act.wait_ge(post_dve, at(NB - 1, POST_DVE, "y"))
                for h in HALF:
                    last = act.copy(v3(yt, TS)[h], bank[1][1][h, :, h])
                last.then_inc(smp_act, 1)
                finish(SAMPLES, 0)
                finish(SAMPLES, 1)

            @block.tensor
            def _(pe):
                pe.wait_ge(par_in, 16 * 14)
                pe.wait_ge(setup, 3)
                pe.wait_ge(zero, 13)
                ident = masks[:, ID, :]

                def prepare(s, part):
                    W = width(s)

                    def low_rank(bank_, w, x):
                        for j in range(HP):
                            last = pe.matmul(v3(bank_, W)[:, j, :], w[:, j * P:(j + 1) * P], x, start=True, stop=True)
                        last.then_inc(prep_pe, 1)

                    def dve_did(name):
                        pe.wait_ge(prep_dve, at(s, PREP_DVE, name))

                    def act_did(name):
                        pe.wait_ge(prep_act, at(s, PREP_ACT, name))

                    if part == 0:
                        act_did("th")
                        if isinstance(s, int) and s <= 1:
                            if s == 1:
                                pe.wait_ge(prep_dve, at(0, PREP_DVE, "bonus"))
                                pe.wait_ge(prep_act, at(0, PREP_ACT, "nrm"))
                        else:
                            pe.wait_ge(post_act, 2 * (s - 1))
                            pe.wait_ge(post_dve, at(s - 2, POST_DVE, "d"))
                        low_rank(side[0], w2[0:HD, :], B["th"][0:HD, 0:W])
                        low_rank(side[1], w2[HD:P, :], zv(12, 1, W)[HD:P, 0, :])
                    if part == 1:
                        dve_did("w")
                        low_rank(side[0], g2[:], B["sx"][:, 0:W])
                        dve_did("a")
                        act_did("kk2")
                        pe.matmul(side[1][:, 0:HP * W], masks[:, BD, :], B["kk2"][:, 0:HP * W], start=True, stop=True).then_inc(prep_pe, 1)
                    if part == 2:
                        act_did("g")
                        dve_did("rk")
                        pe.matmul(side[0][:, 0:HP * W], masks[:, BD, :], B["rk"][:, 0:HP * W], start=True, stop=True).then_inc(prep_pe, 1)

                LAST_IN_BANK = ["S", "Y", "U"]

                def product(q, t, stage, operands, after=(), transpose=False):
                    i = STAGES.index(stage)
                    names = [copied(n) for n in after] + ([copied(STAGES[i - NBANK])] if i >= NBANK else [])
                    for sem, order in ((dve_out[q], DVE_OUT), (act_out[q], ACT_OUT)):
                        mine = [n for n in names if n in order]
                        if mine:
                            pe.wait_ge(sem, at(t, order, max(mine, key=order.index)))
                    if i < NBANK and not is_first(t):
                        wait_copied(pe, q, t - 1, LAST_IN_BANK[i])
                    out = bank[q][STAGES.index(stage) % NBANK]
                    for j in range(HP):
                        for n, (l, r) in enumerate(operands):
                            if transpose:
                                last = pe.transpose(out[:, j, :], l[:, j, :], ident)
                            else:
                                last = pe.matmul(out[:, j, :], l[:, j, :], r[:, j, :], start=(n == 0), stop=(n == len(operands) - 1))
                    last.then_inc(mm[q], 1)

                def intra(q, t, stage):
                    m = M[q]
                    dve_hats = 6 * t + 3 * q
                    if stage == "AabT":
                        pe.wait_ge(hats_dve, dve_hats + 2)
                        product(q, t, stage, [(m["bT"], m["aT"])])
                    elif stage == "Aab":
                        product(q, t, stage, [(m["aT"], m["bT"])])
                    elif stage == "AqbT":
                        pe.wait_ge(hats_pool[q], 2 * t + 2)
                        product(q, t, stage, [(m["bT"], m["rT"])])
                    elif stage == "D2":
                        product(q, t, stage, [(m["Dt"], m["D"])], after=["Dt", "D"])
                    elif stage == "Dt2":
                        product(q, t, stage, [(m["D"], m["Dt"])])
                    elif stage == "AakT":
                        pe.wait_ge(hats_dve, dve_hats + 3)
                        product(q, t, stage, [(m["kT"], m["aT"])])
                    elif stage == "D4":
                        product(q, t, stage, [(m["Dt2"], m["D2"])], after=["D2", "Dt2"])
                    elif stage == "Dt4":
                        product(q, t, stage, [(m["D2"], m["Dt2"])])
                    elif stage == "X2":
                        product(q, t, stage, [(m["D2"], m["Xt"])], after=["Xt"])
                    elif stage == "AqkT":
                        product(q, t, stage, [(m["kT"], m["rT"])])
                    elif stage == "D8":
                        product(q, t, stage, [(m["Dt4"], m["D4"])], after=["D4", "Dt4"])
                    elif stage == "X3":
                        product(q, t, stage, [(m["D4"], m["Xt"])], after=["X2"])
                    elif stage == "Bt":
                        product(q, t, stage, [(m["bT"], None)], transpose=True)
                    elif stage == "X4":
                        product(q, t, stage, [(m["D8"], m["Xt"])], after=["D8", "X3"])
                    elif stage == "Kt":
                        product(q, t, stage, [(m["kT"], None)], transpose=True)
                    elif stage == "X":
                        product(q, t, stage, [(m["Xt"], None)], after=["X4"], transpose=True)
                    elif stage == "Vt":
                        pe.wait_ge(hats_act[q], (2 - q) * t + 1)
                        product(q, t, stage, [(m["vT"], None)], transpose=True)
                    elif stage == "Z32":
                        product(q, t, stage, [(m["O32"], m["Xt"])], after=["O32"])
                    elif stage == "X32t":
                        product(q, t, stage, [(m["X"], m["Z"])], after=["X", "Z32"])
                    elif stage == "X32":
                        product(q, t, stage, [(m["Z"], m["X"])])
                    elif stage == "Z64":
                        product(q, t, stage, [(m["O64"], m["Xt"])], after=["X32t"])
                    elif stage == "X64t":
                        product(q, t, stage, [(m["X"], m["Z"])], after=["X32", "Z64"])

                def with_state(q, t, stage):
                    m = M[q]
                    if stage == "RH":
                        if q == 1:
                            pe.wait_ge(dve_out[0], at(t, DVE_OUT, "S"))
                        elif not is_first(t):
                            pe.wait_ge(dve_out[1], at(t - 1, DVE_OUT, "S"))
                        product(q, t, stage, [(m["aT"], S[q]), (m["AakT"], m["Vt"])], after=["AakT", "Vt"])
                    elif stage == "U":
                        product(q, t, stage, [(m["Xt"], m["RH"])], after=["X64t", "RH"])
                    elif stage == "S":
                        product(q, t, stage, [(m["Bt"], m["U"]), (m["Kt"], m["Vt"])], after=["Bt", "Kt", "U"])
                    elif stage == "Y":
                        product(q, t, stage, [(S[q], m["rT"]), (m["U"], m["AqbT"]), (m["Vt"], m["AqkT"])], after=["AqbT", "AqkT"])

                def finish(t, part):
                    W = width(t)
                    if part == 1:
                        pe.wait_ge(post_act, 2 * t + 1)
                        pe.matmul(side[0][:, 0:HP * W], bd64[:], ysq[:, 0:HP * W], start=True, stop=True).then_inc(post_pe, 1)
                        return
                    if is_samples(t):
                        pe.wait_ge(smp_act, 4)
                    else:
                        for q in range(Q):
                            pe.wait_ge(act_out[q], at(t, ACT_OUT, "Y"))
                        pe.wait_ge(prep_act, at(t + 1, PREP_ACT, "nrm"))
                        pe.wait_ge(prep_dve, at(t + 1, PREP_DVE, "bonus"))
                    if is_samples(t):
                        pe.wait_ge(post_dve, at(NB - 1, POST_DVE, "d"))
                        pe.wait_ge(post_act, 2 * NB)
                    pe.matmul(side[1][:, 0:HP * W], bd64[:], yt[:, 0:HP * W], start=True, stop=True).then_inc(post_pe, 1)

                PREP_AT = {2: 0, 5: 1, 9: 2}

                def half(t, q):
                    before = (t, 0) if q else (t - 1, 1)
                    for i, stage in enumerate(INTRA):
                        intra(q, t, stage)
                        if not (q == 0 and is_first(t)):
                            for step, after in STATE_AT.items():
                                if i == after:
                                    with_state(before[1], before[0], step)
                        if q and i in PREP_AT:
                            prepare(t + 1, PREP_AT[i])
                        if q == 0 and not is_first(t):
                            if i == 10:
                                finish(t - 1, 0)
                            if i == 13:
                                finish(t - 1, 1)

                for part in range(3):
                    prepare(FIRST, part)
                schedule(pe, half)
                m = M[0]
                tok_of = lambda ap, j, b: ap[:, j, :].rearrange("p (h b s) -> p h b s", h=2, b=DB)[:, :, b, :]
                pe.wait_ge(smp_in, 16 * 2 * DB)
                wait_copied(pe, 1, NB - 1, "S")
                wait_copied(pe, 1, NB - 1, "Y")
                for j in range(HP):
                    for b in range(DB):
                        last = pe.matmul(tok_of(bank[1][2], j, b), Sb[b][:, j, :], tok_of(m["aT"], j, b), start=True, stop=True)
                last.then_inc(smp_pe, 1)
                pe.wait_ge(smp_act, 1)
                wait_copied(pe, 0, SAMPLES, "AakT")
                wait_copied(pe, 0, SAMPLES, "Vt")
                for j in range(HP):
                    pe.matmul(bank[1][0][:, j, :], m["RH"][:, j, :], ident, start=True, stop=False)
                    last = pe.matmul(bank[1][0][:, j, :], m["AakT"][:, j, :], m["Vt"][:, j, :], start=False, stop=True)
                last.then_inc(smp_pe, 1)
                pe.wait_ge(smp_act, 2)
                wait_copied(pe, 0, SAMPLES, "X64t")
                for j in range(HP):
                    last = pe.matmul(bank[1][2][:, j, :], m["Xt"][:, j, :], m["Z"][:, j, :], start=True, stop=True)
                last.then_inc(smp_pe, 1)
                pe.wait_ge(smp_act, 3)
                wait_copied(pe, 0, SAMPLES, "AqkT")
                for j in range(HP):
                    pe.matmul(bank[1][1][:, j, :], m["U"][:, j, :], m["AqbT"][:, j, :], start=True, stop=False)
                    pe.matmul(bank[1][1][:, j, :], m["Vt"][:, j, :], m["AqkT"][:, j, :], start=False, stop=False)
                    for b in range(DB):
                        last = pe.matmul(tok_of(bank[1][1], j, b), Sb[b][:, j, :], tok_of(m["rT"], j, b), start=False, stop=(b == DB - 1))
                last.then_inc(smp_pe, 1)
                wait_copied(pe, 0, SAMPLES, "Kt")
                wait_copied(pe, 0, SAMPLES, "Z64")
                for b in range(DB):
                    pe.wait_ge(smp_dve, 4 * b + 2)
                    for j in range(HP):
                        pe.matmul(bank[0][b % NBANK][:, j, :], m["Bt"][:, j, :], M[1]["D2"][:, j, :], start=True, stop=False)
                        last = pe.matmul(bank[0][b % NBANK][:, j, :], m["Kt"][:, j, :], M[1]["Dt2"][:, j, :], start=False, stop=True)
                    last.then_inc(smp_pe, 1)
                finish(SAMPLES, 0)
                finish(SAMPLES, 1)


def rwkv_masks():
    import numpy as np
    i = np.arange(P)
    h, t = i // HD, i % HD
    head = h[:, None] == h[None, :]
    low, up = t[:, None] > t[None, :], t[:, None] < t[None, :]
    eq = t[:, None] == t[None, :]
    same = lambda n: head & (t[:, None] // n == t[None, :] // n)
    cross = lambda n: same(2 * n) & (t[:, None] // n > t[None, :] // n)
    ms = [head, same(16) & low, cross(16), cross(32), same(16) & up, head & up, head & (up | eq), head & eq,
          same(DS) & low, same(DS) & up, same(DS) & up, same(DS) & (up | eq), np.zeros((P, P), bool)]
    return np.stack(ms, 1).astype(np.float32)


def sample_rows():
    import numpy as np
    return (np.arange(P)[:, None] % HD // DS == np.arange(DB)[None]).astype(np.float32)


def chunk_starts():
    import numpy as np
    a = np.ones((P, 2, HP * TB), np.float32)
    a[:, 0, ::C] = 0
    a[:, 1, ::DS] = 0
    return a


NG_ = 32
GC = 16
NS = 64
L = P // GC
NJ = NG_ // 2
NBL = SEQ // L
NBS = DB
NBT = NBL + NBS
BI = 16
TWO_PI = 2 * math.pi
PI_A = 6.28125
PI_B = TWO_PI - PI_A
ROUND = 1.5 * 2 ** 23
BELOW_PI = 3.1415925


def state_space(nc, ins, outs, u):
    with ExitStack() as ctx:
        e = Env(nc, ctx, "ss")
        lr, li, dt = (e.sb(n, [P, NJ]) for n in ("lr", "li", "dt"))
        Br, Bi, Cr, Ci = (e.sb(n, [P, NJ, GC]) for n in ("Br", "Bi", "Cr", "Ci"))
        d = e.sb("d", [P, NG_])
        ident = e.sb("ident", [P, P])
        h0 = [e.sb(n, [P, NJ, NBS]) for n in ("h0r", "h0i")]
        wglu, bglu = e.sb("wglu", [P, KU, DSSM]), e.sb("bglu", [P, KU])
        small = {n: e.sb(n, [P, NJ]) for n in ("th", "mag", "k", "rs", "rc", "sin", "cos", "den", "nr", "fr", "fi", "x1", "x2")}
        Ap = [e.sb(n, [P, L + 1, NJ]) for n in ("Apr", "Api")]
        Qp = [e.sb(n, [P, BI + 1, NJ]) for n in ("Qpr", "Qpi")]
        Bb = [e.sb(n, [P, NJ, GC]) for n in ("Bbr", "Bbi")]
        CA = [e.sb(n, [P, NJ, L + 1, GC]) for n in ("CAr", "CAn")]
        RT = [e.sb(n, [P, NJ, P]) for n in ("RTr", "RTi")]
        Tm = e.sb("Tm", [P, NG_, P])
        U = e.sb("U", [P, NG_, NBT])
        H = [e.sb(n, [P, NJ, NBL + 1]) for n in ("Hr", "Hi")]
        HS = [e.sb(n, [P, NJ, NBS]) for n in ("HSr", "HSi")]
        rows = e.sb("rows", [P, NG_ * P])
        G = [e.sb(n, [P, NJ, BI]) for n in ("Gr", "Gi")]
        tmp = [e.sb(f"tmp{i}", [P, NJ, BI]) for i in range(4)]
        sg = e.sb("sg", [P, KU, TW])
        endp = [e.sb(n, [P, NJ]) for n in ("endr", "endi")]
        R = [U[:].rearrange("p g n -> p (g n)")[:, i * NJ * P:(i + 1) * NJ * P].rearrange("p (j s c) -> p j s c", s=L, c=GC) for i in range(2)]
        big = [H[i][:].rearrange("p j n -> p (j n)")[:, 0:NJ * (L + 1) * GC].rearrange("p (j t c) -> p j t c", t=L + 1, c=GC) for i in range(2)]
        Ks = rows[0:GC, :].rearrange("p (g x) -> p g x", x=P)
        dtmp = U[:].rearrange("p g n -> p (g n)")[:, 0:NG_ * P].rearrange("p (g x) -> p g x", x=P)
        bk = [e.ps(f"bk{i}", [P, 512]) for i in range(8)]

        par_in, zero, chain = e.sem("par_in"), e.sem("zero"), e.sem("chain")
        dt_ready, mag_ready, sc_ready = e.sem("dt_ready"), e.sem("mag_ready"), e.sem("sc_ready")
        arg_ready, red_ready = e.sem("arg_ready"), e.sem("red_ready")
        k_ready, r_ready = e.sem("k_ready"), e.sem("r_ready")
        k_mm, k_out, t_moved, t_ready = e.sem("k_mm"), e.sem("k_out"), e.sem("t_moved"), e.sem("t_ready")
        r_mm, r_out = e.sem("r_mm"), e.sem("r_out")
        u_mm, u_act, u_dve = e.sem("u_mm"), e.sem("u_act"), e.sem("u_dve")
        b_mm, b_act, b_dve = e.sem("b_mm"), e.sem("b_act"), e.sem("b_dve")
        h_ready, end_ready = e.sem("h_ready"), e.sem("end_ready")
        y_mm, y_out, x_mm, x_out = e.sem("y_mm"), e.sem("y_out"), e.sem("x_mm"), e.sem("x_out")
        g_mm, g_sig, g_out = e.sem("g_mm"), e.sem("g_sig"), e.sem("g_out")
        stored = e.sem("stored")
        NPAR = 16

        LOTS = [(0, P, 0), (P, P, P * L), (NBL, NBS, SEQ)]
        NK = NG_ // 4
        NR = 2 * NJ // 4
        UF, UG = KU * 2, NG_ // 4
        UL = UF + UG

        def groups(i):
            first = 8 * (i // 2) + i % 2
            return slice(first, first + 7, 2)

        with nc.Block() as block:
            @block.sync
            def _(sp):
                for dst, n in ((lr, "lam_re"), (li, "lam_im"), (dt, "log_dt"), (Br, "b_re"), (Bi, "b_im"), (Cr, "c_re"), (Ci, "c_im"),
                               (d, "ssm_d"), (ident, "ident"), (h0[0], "h0_re"), (h0[1], "h0_im"), (bglu, "b_glu")):
                    sp.dma_start(dst[:], ins[n]).then_inc(par_in, 16)
                for k in range(KU):
                    sp.dma_start(wglu[:, k, :], ins["w_glu"][k]).then_inc(par_in, 16)
                sp.wait_ge(k_out, NK)
                sp.wait_ge(zero, 3)
                for s in range(L):
                    sp.dma_start(Tm[s * GC:(s + 1) * GC, :, s * GC:P], Ks[:, :, 0:P - s * GC]).then_inc(t_moved, 16)
                sp.wait_ge(end_ready, 2)
                for i, n in enumerate(("re", "im")):
                    sp.dma_start(outs[f"ssm_{n}_p"], endp[i][:]).then_inc(stored, 16)
                    sp.dma_start(outs[f"ssm_{n}_s"], HS[i][:]).then_inc(stored, 16)
                sp.wait_ge(stored, 64)

            @block.gpsimd
            def _(pool):
                pool.memset(Tm[:], 0.0).then_inc(zero, 1)
                pool.memset(Ap[0][:, 0, :], 1.0).then_inc(zero, 1)
                pool.memset(Ap[1][:, 0, :], 0.0).then_inc(zero, 1)

            def u_copy(eng, lot, f, n, b0):
                i = lot * UL + f
                eng.wait_ge(u_mm, i + 1)
                src = bk[i % 8]
                if f < UF:
                    ct, half = f // 2, f % 2
                    dst = rows[0:n, :].rearrange("p (g s c) -> p g s c", s=L, c=GC)[:, 8 * ct:8 * ct + 8, 4 * half:4 * half + 4, :]
                    src = src[0:n, :].rearrange("p (s g c) -> p g s c", s=4, c=GC)
                else:
                    g = 4 * (f - UF)
                    dst = U[:, g:g + 4, b0:b0 + n]
                    src = src[:, 0:4 * n].rearrange("p (g n) -> p g n", g=4)
                if f % 2:
                    eng.tensor_copy(dst, src).then_inc(u_dve, 1)
                else:
                    eng.copy(dst, src).then_inc(u_act, 1)

            @block.scalar
            def _(act):
                act.wait_ge(par_in, 16 * NPAR)
                act.activation(dt[:], dt[:], ACT.Exp).then_inc(dt_ready, 1)
                act.wait_ge(mag_ready, 1)
                act.activation(small["mag"][:], small["mag"][:], ACT.Exp).then_inc(sc_ready, 1)
                act.wait_ge(arg_ready, 1)
                act.activation(small["sin"][:], small["rs"][:], ACT.Sin).then_inc(sc_ready, 1)
                act.activation(small["cos"][:], small["rc"][:], ACT.Sin).then_inc(sc_ready, 1)
                for i in range(NK):
                    act.wait_ge(k_mm, i + 1)
                    act.copy(Ks[:, groups(i), :], bk[i % 4][0:GC, :].rearrange("p (g x) -> p g x", x=P)).then_inc(k_out, 1)
                for i in range(NR):
                    act.wait_ge(r_mm, i + 1)
                    act.copy(RT[i // (NJ // 4)][:, 4 * (i % (NJ // 4)):4 * (i % (NJ // 4)) + 4, :],
                             bk[4 + i % 4][:].rearrange("p (j x) -> p j x", x=P)).then_inc(r_out, 1)
                act.wait_ge(t_moved, 16 * L)
                for lot, (b0, n, _) in enumerate(LOTS):
                    for f in range(0, UL, 2):
                        u_copy(act, lot, f, n, b0)
                for j in range(NJ):
                    act.wait_ge(b_mm, 2 * j + 1)
                    src = bk[(2 * j) % 8]
                    act.copy(H[0][:, j, 1:], src[:, 0:NBL])
                    act.copy(HS[0][:, j, :], src[:, NBL:NBT]).then_inc(b_act, 1)
                for lot, (b0, n, _) in enumerate(LOTS):
                    for q in range(UG):
                        i = lot * UG + q
                        act.wait_ge(y_mm, i + 1)
                        if q == 0 and lot:
                            act.wait_ge(x_mm, UF * lot)
                        out = rows[0:n, :].rearrange("p (t g c) -> p g t c", t=L, c=GC)[:, groups(q)]
                        act.activation(out, bk[i % 4][0:n, :].rearrange("p (g t c) -> p g t c", t=L, c=GC), ACT.Gelu_apprx_tanh).then_inc(y_out, 1)
                for n in range(NT):
                    for m in range(KU):
                        i = n * KU + m
                        act.wait_ge(g_mm, i + 1)
                        if m == 0 and n:
                            act.wait_ge(g_out, n)
                        act.activation(sg[:, m, :], bk[i % 4][:, 0:TW], ACT.Sigmoid, bias=bglu[:, m:m + 1]).then_inc(g_sig, 1)

            @block.vector
            def _(dve):
                count = [0]

                def link(ins):
                    count[0] += 1
                    ins.then_inc(chain, 1)
                    dve.wait_ge(chain, count[0])

                def tt(out, a, b, op):
                    link(dve.tensor_tensor(out, a, b, op))

                def ts(out, a, s1, s2, o1, o2=None):
                    link(dve.tensor_scalar(out, a, s1, s2, o1, *([o2] if o2 else [])))

                def cmul(out, a, b, t):
                    tt(t[0], a[0], b[0], ALU.mult)
                    tt(t[1], a[1], b[1], ALU.mult)
                    tt(t[2], a[0], b[1], ALU.mult)
                    tt(t[3], a[1], b[0], ALU.mult)
                    tt(out[0], t[0], t[1], ALU.subtract)
                    tt(out[1], t[2], t[3], ALU.add)

                s = {n: x[:] for n, x in small.items()}

                def reduced(out, x):
                    ts(s["k"], x, 1 / TWO_PI, ROUND, ALU.mult, ALU.add)
                    ts(s["k"], s["k"], -ROUND, None, ALU.add)
                    link(dve.scalar_tensor_tensor(out, s["k"], -PI_A, x, ALU.mult, ALU.add))
                    link(dve.scalar_tensor_tensor(out, s["k"], -PI_B, out, ALU.mult, ALU.add))
                    ts(out, out, BELOW_PI, -BELOW_PI, ALU.min, ALU.max)

                dve.wait_ge(par_in, 16 * NPAR)
                dve.wait_ge(dt_ready, 1)
                tt(s["th"], li[:], dt[:], ALU.mult)
                dve.tensor_tensor(s["mag"], lr[:], dt[:], ALU.mult).then_inc(mag_ready, 1)
                reduced(s["rs"], s["th"])
                ts(s["x1"], s["rs"], math.pi / 2, None, ALU.add)
                reduced(s["rc"], s["x1"])
                dve.sem_inc(arg_ready, 1)
                dve.wait_ge(sc_ready, 3)
                dve.wait_ge(zero, 3)
                tt(Ap[0][:, 1], s["mag"], s["cos"], ALU.mult)
                tt(Ap[1][:, 1], s["mag"], s["sin"], ALU.mult)
                tt(s["x1"], lr[:], lr[:], ALU.mult)
                tt(s["x2"], li[:], li[:], ALU.mult)
                tt(s["den"], s["x1"], s["x2"], ALU.add)
                link(dve.reciprocal(s["den"], s["den"]))
                ts(s["nr"], Ap[0][:, 1], -1.0, None, ALU.add)
                tt(s["x1"], s["nr"], lr[:], ALU.mult)
                tt(s["x2"], Ap[1][:, 1], li[:], ALU.mult)
                tt(s["fr"], s["x1"], s["x2"], ALU.add)
                tt(s["fr"], s["fr"], s["den"], ALU.mult)
                tt(s["x1"], Ap[1][:, 1], lr[:], ALU.mult)
                tt(s["x2"], s["nr"], li[:], ALU.mult)
                tt(s["fi"], s["x1"], s["x2"], ALU.subtract)
                tt(s["fi"], s["fi"], s["den"], ALU.mult)
                t4 = [x[:] for x in tmp]
                cmul([x[:] for x in Bb], [bcast(s["fr"], GC), bcast(s["fi"], GC)], [Br[:], Bi[:]], t4)

                def powers(X, top):
                    n = 1
                    while n < top:
                        w = min(n, top - n)
                        last = [x[:, n:n + 1, :].to_broadcast([P, w, NJ]) for x in X]
                        t = [x[:].rearrange("p j b -> p b j")[:, 0:w, :] for x in tmp]
                        cmul([x[:, n + 1:n + 1 + w, :] for x in X], [x[:, 1:1 + w, :] for x in X], last, t)
                        n += w

                powers(Ap, L)
                at_ = [x[:].rearrange("p t j -> p j t").unsqueeze(3).to_broadcast([P, NJ, L + 1, GC]) for x in Ap]
                c_ = [x[:].unsqueeze(2).to_broadcast([P, NJ, L + 1, GC]) for x in (Cr, Ci)]
                tt(big[0], at_[0], c_[0], ALU.mult)
                tt(big[1], at_[1], c_[1], ALU.mult)
                tt(CA[0][:], big[0], big[1], ALU.subtract)
                tt(big[0], at_[0], c_[1], ALU.mult)
                tt(big[1], at_[1], c_[0], ALU.mult)
                tt(CA[1][:], big[0], big[1], ALU.add)
                dve.tensor_scalar(CA[1][:], CA[1][:], -1.0, None, ALU.mult).then_inc(k_ready, 1)
                for q in range(L):
                    a = [bcast(x[:, L - 1 - q, :], GC) for x in Ap]
                    cmul([R[0][:, :, q, :], R[1][:, :, q, :]], a, [x[:] for x in Bb], t4)
                dve.sem_inc(r_ready, 1)
                for i in range(2):
                    link(dve.tensor_copy(Qp[i][:, 1, :], Ap[i][:, L, :]))
                powers(Qp, BI)
                dve.wait_ge(t_moved, 16 * L)
                dve.wait_ge(r_mm, NR)
                tt(dtmp, ident[:].unsqueeze(1).to_broadcast([P, NG_, P]), bcast(d[:], P), ALU.mult)
                link(dve.tensor_tensor(Tm[:], Tm[:], dtmp, ALU.add))
                dve.sem_inc(t_ready, 1)
                for lot, (b0, n, _) in enumerate(LOTS):
                    for f in range(1, UL, 2):
                        u_copy(dve, lot, f, n, b0)
                for i in range(2):
                    link(dve.memset(H[i][:, :, 0:1], 0.0))
                for j in range(NJ):
                    dve.wait_ge(b_mm, 2 * j + 2)
                    src = bk[(2 * j + 1) % 8]
                    dve.tensor_copy(H[1][:, j, 1:], src[:, 0:NBL])
                    dve.tensor_copy(HS[1][:, j, :], src[:, NBL:NBT]).then_inc(b_dve, 1)
                dve.wait_ge(b_act, NJ)
                dve.wait_ge(b_dve, NJ)

                def add_product(x, a, b, t):
                    tt(t[0], a[0], b[0], ALU.mult)
                    tt(t[1], a[1], b[1], ALU.mult)
                    tt(t[2], a[0], b[1], ALU.mult)
                    tt(t[3], a[1], b[0], ALU.mult)
                    tt(x[0], x[0], t[0], ALU.add)
                    tt(x[1], x[1], t[2], ALU.add)
                    tt(x[0], x[0], t[1], ALU.subtract)
                    tt(x[1], x[1], t[3], ALU.add)

                def run(i):
                    return [x[:, :, 1 + i:1 + i + BI * (BI - 1) + 1:BI] for x in H]

                a8 = [bcast(x[:, 1, :], BI) for x in Qp]
                for i in range(1, BI):
                    add_product(run(i), a8, run(i - 1), t4)
                ends = run(BI - 1)
                for i in range(2):
                    link(dve.memset(G[i][:, :, 0:1], 0.0))
                    link(dve.tensor_copy(G[i][:, :, 1:], ends[i][:, :, 0:BI - 1]))
                a128 = [x[:, BI, :] for x in Qp]
                tj = [x[:, :, 0] for x in tmp]
                for b in range(1, BI):
                    add_product([x[:, :, b] for x in G], a128, [x[:, :, b - 1] for x in G], tj)
                for i in range(BI):
                    add_product(run(i), [bcast(x[:, i + 1, :], BI) for x in Qp], [x[:] for x in G], t4)
                dve.sem_inc(h_ready, 1)
                a8s = [bcast(x[:, 1, :], NBS) for x in Qp]
                add_product([x[:] for x in HS], a8s, [x[:] for x in h0], [x[:, :, 0:NBS] for x in tmp])
                for i in range(2):
                    dve.tensor_copy(endp[i][:], H[i][:, :, NBL]).then_inc(end_ready, 1)
                for lot, (b0, n, t0) in enumerate(LOTS):
                    for f in range(UF):
                        i = lot * UF + f
                        ct, half = f // 2, f % 2
                        dve.wait_ge(x_mm, i + 1)
                        dst = u[:, ct, t0:t0 + n * L].rearrange("p (n t) -> p t n", t=L)[:, 4 * half:4 * half + 4, :]
                        dve.tensor_copy(dst, bk[4 + i % 4][:, 0:4 * n].rearrange("p (t n) -> p t n", t=4)).then_inc(x_out, 1)
                for n in range(NT):
                    dve.wait_ge(g_sig, KU * (n + 1))
                    dve.tensor_tensor(u[:, :, tok(n)], u[:, :, tok(n)], sg[:], ALU.mult).then_inc(g_out, 1)

            @block.tensor
            def _(pe):
                pe.wait_ge(par_in, 16 * NPAR)
                pe.wait_ge(k_ready, 1)
                for i in range(NK):
                    if i >= 4:
                        pe.wait_ge(k_out, i - 3)
                    for n4, g in enumerate(range(NG_)[groups(i)]):
                        j, h = g // 2, slice(NS * (g % 2), NS * (g % 2) + NS)
                        out = bk[i % 4][0:GC, n4 * P:(n4 + 1) * P]
                        for n in range(2):
                            last = pe.matmul(out, Bb[n][h, j, :], CA[n][h, j, 0:L, :], start=(n == 0), stop=(n == 1))
                    last.then_inc(k_mm, 1)
                pe.wait_ge(r_ready, 1)
                for i in range(NR):
                    if i >= 4:
                        pe.wait_ge(r_out, i - 3)
                    x, j0 = i // (NJ // 4), 4 * (i % (NJ // 4))
                    for j in range(j0, j0 + 4):
                        last = pe.transpose(bk[4 + i % 4][:, (j - j0) * P:(j - j0 + 1) * P], R[x][:, j].rearrange("p s c -> p (s c)"), ident[:])
                    last.then_inc(r_mm, 1)
                pe.wait_ge(k_out, NK)
                pe.wait_ge(r_out, NR)
                pe.wait_ge(t_ready, 1)
                for lot, (b0, n, t0) in enumerate(LOTS):
                    for f in range(UL):
                        i = lot * UL + f
                        if i >= 8:
                            pe.wait_ge(u_dve if f % 2 else u_act, (i - 8) // 2 + 1)
                        if f < UF:
                            ct, half = f // 2, f % 2
                            for k in range(4):
                                first = t0 + 4 * half + k
                                last = pe.transpose(bk[i % 8][0:n, k * P:(k + 1) * P], u[:, ct, first:first + L * (n - 1) + 1:L], ident[:])
                        else:
                            if f == UF:
                                pe.wait_ge(u_act, (lot * UL + UF) // 2)
                                pe.wait_ge(u_dve, (lot * UL + UF) // 2)
                            for k in range(4):
                                g = 4 * (f - UF) + k
                                last = pe.transpose(bk[i % 8][:, k * n:(k + 1) * n], rows[0:n, g * P:(g + 1) * P], ident[0:n, 0:n])
                        last.then_inc(u_mm, 1)
                pe.wait_ge(u_act, len(LOTS) * UL // 2)
                pe.wait_ge(u_dve, len(LOTS) * UL // 2)
                for i in range(2 * NJ):
                    j, x = i // 2, i % 2
                    if i >= 8:
                        pe.wait_ge((b_act, b_dve)[x], j - 3)
                    for h in range(2):
                        last = pe.matmul(bk[i % 8][NS * h:NS * h + NS, 0:NBT], RT[x][:, j, NS * h:NS * h + NS], U[:, 2 * j + h, :], start=True, stop=True)
                    last.then_inc(b_mm, 1)
                pe.wait_ge(h_ready, 1)
                for lot, (b0, n, t0) in enumerate(LOTS):
                    for q in range(UG):
                        i = lot * UG + q
                        if i >= 4:
                            pe.wait_ge(y_out, i - 3)
                        for n4, g in enumerate(range(NG_)[groups(q)]):
                            j, h = g // 2, slice(NS * (g % 2), NS * (g % 2) + NS)
                            out = bk[i % 4][0:n, n4 * P:(n4 + 1) * P]
                            pe.matmul(out, U[:, g, b0:b0 + n], Tm[:, g, :], start=True, stop=False)
                            for x in range(2):
                                state = h0[x][h, j, :] if b0 == NBL else H[x][h, j, b0:b0 + n]
                                last = pe.matmul(out, state, CA[x][h, j, 1:, :], start=False, stop=(x == 1))
                        last.then_inc(y_mm, 1)
                    pe.wait_ge(y_out, (lot + 1) * UG)
                    for f in range(UF):
                        i = lot * UF + f
                        ct, half = f // 2, f % 2
                        if i >= 4:
                            pe.wait_ge(x_out, i - 3)
                        for k in range(4):
                            c = (4 * half + k) * DSSM + ct * P
                            last = pe.transpose(bk[4 + i % 4][:, k * n:(k + 1) * n], rows[0:n, c:c + P], ident[0:n, 0:n])
                        last.then_inc(x_mm, 1)
                pe.wait_ge(x_out, UF * len(LOTS))
                for n in range(NT):
                    for m in range(KU):
                        i = n * KU + m
                        if i >= 4:
                            pe.wait_ge(g_sig, i - 3)
                        for k in range(KU):
                            last = pe.matmul(bk[i % 4][:, 0:TW], wglu[:, k, m * P:(m + 1) * P], u[:, k, tok(n)], start=(k == 0), stop=(k == KU - 1))
                        last.then_inc(g_mm, 1)


class Tiles:

    def __init__(self, parts):
        self.parts = parts

    def __getitem__(self, at_):
        p, k, t = at_
        return self.parts[k // KU][p, k % KU, t]


def hybrid_layer(nc, ins, outs, scratch):
    with ExitStack() as ctx:
        u = ctx.enter_context(nc.sbuf_tensor("mix_a", [P, KU, T], F32))
        project_in(nc, ins, scratch, u)
        state_space(nc, ins, outs, u)
        yb = ctx.enter_context(nc.sbuf_tensor("mix_b", [P, KR, T], F32))
        delta_rule(nc, ins, outs, scratch, yb)
        hT = ctx.enter_context(nc.sbuf_tensor("h", [P, KD, T], F32))
        mix_out(nc, ins, (u, yb), hT, Tiles((u, yb)))
        conv_ffn(nc, ins, outs, hT, Tiles((u, yb)))
        gated_embedding(nc, ins, outs, hT, (u, yb))


def kernel(**inputs):
    import numpy as np
    import concourse.bacc as _bacc
    from concourse import mybir as _mybir
    from concourse.bass_utils import run_bass_kernel_spmd as _run

    a = {k: np.asarray(v) for k, v in inputs.items()}

    def tiles(rows):
        return rows.T.reshape(-1, P, rows.shape[0]).transpose(1, 0, 2)

    def columns(v):
        return v.reshape(-1, P).T

    def states(v):
        v = v.reshape(NJ, 2, NS, -1).transpose(1, 2, 0, 3).reshape(P, NJ, -1)
        return v[:, :, 0] if v.shape[2] == 1 else v

    def both(prompt, sample):
        return tiles(np.concatenate([prompt.reshape(SEQ, -1), sample.reshape(TS_ALL, -1)], 0))

    TS_ALL = DB * DS
    w_up = a["w_up"][0].reshape(KD, P, 2 * FF).transpose(1, 0, 2)
    arrays = {
        "xT": both(a["x_prompt"], a["x_sample"]),
        "pT": both(a["p_prompt"], a["p_sample"]),
        "norm1_g": columns(a["norm1_g"]), "norm2_g": columns(a["norm2_g"]), "final_g": columns(a["final_g"]),
        "w_in": a["w_in"].reshape(KD, P, -1), "w_out": a["w_out"].reshape(KD, P, D),
        "w_val": w_up[:, :, 0:FF], "w_gate": w_up[:, :, FF:], "w_down": a["w_down"].reshape(KF, P, D),
        "conv_wb": np.concatenate([a["conv_w"][0], a["conv_b"]], 0).reshape(CONV + 1, KF, P).transpose(2, 1, 0),
        "state_conv": a["state_conv"].reshape(DB, 2, KF, P).transpose(3, 2, 0, 1),
        "w_pg": a["w_pg"].reshape(KD, P, D), "w_ple": a["w_ple"].reshape(KP, P, D),
        "w2a2": np.concatenate([a["rwkv_w2"][0], a["rwkv_a2"][0]], 0), "g2": a["rwkv_g2"][0], "mu": columns(a["shift_mu"]),
        "masks": rwkv_masks(), "seg": chunk_starts(), "rows8": sample_rows(),
        "state_rwkv": a["state_rwkv"].reshape(DB, HP, 2, HD, HD).transpose(2, 4, 0, 1, 3).reshape(P, DB, HP, HD),
        "state_shift": a["state_shift"].reshape(DB, ZT, P).transpose(2, 1, 0),
        "lam_re": states(a["ssm_lam_re"]), "lam_im": states(a["ssm_lam_im"]),
        "log_dt": states(np.repeat(a["ssm_log_dt"][0][:, None], NS, 1)),
        "b_re": states(a["ssm_b_re"]), "b_im": states(a["ssm_b_im"]),
        "c_re": states(a["ssm_c_re"][0].transpose(0, 2, 1)), "c_im": states(a["ssm_c_im"][0].transpose(0, 2, 1)),
        "ssm_d": np.tile(a["ssm_d"].reshape(NG_, GC).T, (L, 1)), "ident": np.eye(P, dtype=np.float32),
        "h0_re": states(a["state_ssm_re"][0].transpose(1, 2, 0)), "h0_im": states(a["state_ssm_im"][0].transpose(1, 2, 0)),
        "w_glu": a["ssm_w_glu"].reshape(KU, P, DSSM), "b_glu": columns(a["ssm_b_glu"]),
    }
    for n in ("w0", "a0", "k_k", "k_a", "r_k", "lnx_g", "lnx_b"):
        arrays[n] = columns(a["rwkv_" + n])
    arrays = {k: np.ascontiguousarray(v) for k, v in arrays.items()}
    shapes = {
        "yT": (P, KD, T), "ssm_re_p": (P, NJ), "ssm_im_p": (P, NJ), "ssm_re_s": (P, NJ, DB), "ssm_im_s": (P, NJ, DB),
        "rwkv_p": (P, HP, HD), "rwkv_s": (P, DB, HP, HD), "shift": (P, ZT, 1 + DB), "conv_p": (P, KF, 2), "conv_s": (P, KF, DB, 2),
    }
    nc = _bacc.Bacc("TRN2", target_bir_lowering=False, num_devices=1)
    ins = {k: nc.dram_tensor(f"in_{k}", v.shape, _mybir.dt.from_np(v.dtype), kind="ExternalInput").ap() for k, v in arrays.items()}
    outs = {k: nc.dram_tensor(f"out_{k}", v, F32, kind="ExternalOutput").ap() for k, v in shapes.items()}
    scratch = {"zr": nc.dram_tensor("scratch_zr", (ZT, P, T), F32, kind="Internal").ap()}
    hybrid_layer(nc, ins, outs, scratch)
    r = _run(nc, [{f"in_{k}": v for k, v in arrays.items()}], core_ids=[0]).results[0]
    o = {k: r[f"out_{k}"] for k in shapes}

    def from_states(v):
        return v.reshape(2, NS, NJ, -1).transpose(3, 2, 0, 1).reshape(1, -1, NG_, NS)

    y = o["yT"].transpose(2, 1, 0).reshape(T, D)
    shift = o["shift"].transpose(2, 1, 0).reshape(1 + DB, -1)
    return (
        y[None, 0:SEQ], y[SEQ:].reshape(DB, DS, D),
        from_states(o["ssm_re_p"]), from_states(o["ssm_im_p"]),
        o["rwkv_p"].reshape(2, HD, HP, HD).transpose(2, 0, 3, 1).reshape(1, 1, 2 * HP, HD, HD),
        shift[None, 0:1], o["conv_p"].transpose(2, 1, 0).reshape(1, 1, 2, FF),
        from_states(o["ssm_re_s"]), from_states(o["ssm_im_s"]),
        o["rwkv_s"].reshape(2, HD, DB, HP, HD).transpose(2, 3, 0, 4, 1).reshape(1, DB, 2 * HP, HD, HD),
        shift[None, 1:], o["conv_s"].transpose(2, 3, 1, 0).reshape(1, DB, 2, FF),
    )
```

```python
import math
from contextlib import ExitStack

import concourse.bass as bass
from concourse import mybir

P = 128
F32 = mybir.dt.float32
I32 = mybir.dt.int32
ALU = mybir.AluOpType
ACT = mybir.ActivationFunctionType
AX = mybir.AxisListType

D = 1024
KD = D // P
SEQ, DB, DS = 2048, 8, 8
T = SEQ + DB * DS
TW = 352
NT = T // TW
DSSM, DRW = 512, 512
KU, KR = DSSM // P, DRW // P
ZT = 14
KIN = KU + ZT
FF = 2816
KF = FF // P
PLE = 256
KP = PLE // P
CONV = 3
RMS_EPS, GN_EPS, L2_EPS = 1e-6, 64e-5, 1e-12
LASTP = SEQ - (NT - 1) * TW


class Env:

    def __init__(self, nc, ctx, tag):
        self.nc, self.ctx, self.tag = nc, ctx, tag

    def sb(self, name, shape, dt=F32):
        return self.ctx.enter_context(self.nc.sbuf_tensor(f"{self.tag}_{name}", shape, dt))

    def ps(self, name, shape):
        return self.ctx.enter_context(self.nc.psum_tensor(f"{self.tag}_{name}", shape, F32))

    def sem(self, name):
        return self.ctx.enter_context(self.nc.semaphore(f"{self.tag}_{name}"))


def bcast(ap, n):
    p, a = ap.shape
    return ap.unsqueeze(2).to_broadcast([p, a, n])


def tok(n):
    return slice(n * TW, (n + 1) * TW)


def project_in(nc, ins, scratch, u):
    with ExitStack() as ctx:
        e = Env(nc, ctx, "in")
        w = e.sb("w", [P, KD, KIN * P])
        xn = e.sb("xn", [P, KD, T])
        sq = e.sb("sq", [P, KD, TW])
        ssum = e.sb("ssum", [P, TW])
        rms = e.sb("rms", [P, TW])
        zout = e.sb("zout", [P, ZT, TW])
        g = e.sb("g", [P, KD])
        eps = e.sb("eps", [P, 1])
        ones = e.sb("ones", [P, P])
        pn = [e.ps(f"pn{i}", [P, 512]) for i in range(2)]
        pp = [e.ps(f"pp{i}", [P, 512]) for i in range(6)]
        x_in = [e.sem(f"x_in{n}") for n in range(NT)]
        w_in = [e.sem(f"w_in{k}") for k in range(KD)]
        g_in = e.sem("g_in")
        const_ready = e.sem("const_ready")
        sq_ready, ssum_ready, ms_ready = e.sem("sq_ready"), e.sem("ssum_ready"), e.sem("ms_ready")
        rms_ready, inv_ready, xn_ready = e.sem("rms_ready"), e.sem("inv_ready"), e.sem("xn_ready")
        proj_ready = e.sem("proj_ready")
        act_out, dve_out = e.sem("act_out"), e.sem("dve_out")
        z_stored = [e.sem(f"z_stored{h}") for h in range(2)]
        HZ = ZT // 2
        DVE_M = [m for m in range(KIN) if m % 2]
        ACT_M = [m for m in range(KIN) if m % 2 == 0]

        with nc.Block() as block:
            @block.sync
            def _(sp):
                for n in range(NT):
                    sp.dma_start(xn[:, :, tok(n)], ins["xT"][:, :, tok(n)]).then_inc(x_in[n], 16)
                    if n == 0:
                        sp.dma_start(g[:], ins["norm1_g"]).then_inc(g_in, 16)
                        for k in range(KD):
                            sp.dma_start(w[:, k, :], ins["w_in"][k]).then_inc(w_in[k], 16)
                dst = scratch["zr"].rearrange("z p t -> p z t")
                for n in range(NT):
                    for h in range(2):
                        last = KU + (h + 1) * HZ
                        sp.wait_ge(act_out, n * len(ACT_M) + sum(m < last for m in ACT_M))
                        sp.wait_ge(dve_out, n * len(DVE_M) + sum(m < last for m in DVE_M))
                        sp.dma_start(dst[:, h * HZ:(h + 1) * HZ, tok(n)],
                                     zout[:, h * HZ:(h + 1) * HZ, :]).then_inc(z_stored[h], 16)
                for h in range(2):
                    sp.wait_ge(z_stored[h], 16 * (NT + 1))

            @block.gpsimd
            def _(pool):
                pool.memset(ones[:], 1.0 / D).then_inc(const_ready, 1)
                pool.memset(eps[:], RMS_EPS).then_inc(const_ready, 1)
                for h in range(2):
                    pool.sem_inc(z_stored[h], 16)

            def copy_out(eng, n, m, out_sem):
                eng.wait_ge(proj_ready, n * KIN + m + 1)
                if m < KU:
                    dst = u[:, m, bass.ds(n * TW, TW)]
                else:
                    if (m - KU) % HZ < 2:
                        eng.wait_ge(z_stored[(m - KU) // HZ], 16 * (n + 1))
                    dst = zout[:, m - KU, :]
                src = pp[m % 6][:, 0:TW]
                if eng is nc.scalar or eng.engine == nc.scalar.engine:
                    eng.copy(dst, src).then_inc(out_sem, 1)
                else:
                    eng.tensor_copy(dst, src).then_inc(out_sem, 1)

            @block.scalar
            def _(act):
                act.wait_ge(const_ready, 2)
                for n in range(NT):
                    act.wait_ge(x_in[n], 16)
                    if n:
                        act.wait_ge(ssum_ready, n)
                    act.square(sq[:], xn[:, :, tok(n)]).then_inc(sq_ready, 1)
                    act.wait_ge(ms_ready, n + 1)
                    if n:
                        act.wait_ge(inv_ready, n)
                    act.activation(rms[:], pn[n % 2][:, 0:TW], ACT.Sqrt, bias=eps[:, 0:1]).then_inc(rms_ready, 1)
                with act.Fori(0, NT) as n:
                    for m in ACT_M:
                        copy_out(act, n, m, act_out)

            @block.vector
            def _(dve):
                dve.wait_ge(g_in, 16)
                for n in range(NT):
                    dve.wait_ge(sq_ready, n + 1)
                    if n:
                        dve.wait_ge(ms_ready, n)
                    dve.tensor_reduce(ssum[:], sq[:].rearrange("p k t -> p t k"), AX.X, ALU.add).then_inc(ssum_ready, 1)
                    dve.wait_ge(rms_ready, n + 1)
                    dve.reciprocal(rms[:], rms[:]).then_inc(inv_ready, 1)
                    dve.wait_ge(inv_ready, n + 1)
                    for k in range(KD):
                        xk = xn[:, k, tok(n)]
                        dve.scalar_tensor_tensor(xk, xk, g[:, k:k + 1], rms[:], ALU.mult, ALU.mult).then_inc(xn_ready, 1)
                with dve.Fori(0, NT) as n:
                    for m in DVE_M:
                        copy_out(dve, n, m, dve_out)

            @block.tensor
            def _(pe):
                pe.wait_ge(const_ready, 2)
                for n in range(NT):
                    pe.wait_ge(ssum_ready, n + 1)
                    if n >= 2:
                        pe.wait_ge(rms_ready, n - 1)
                    pe.matmul(pn[n % 2][:, 0:TW], ones[:], ssum[:], start=True, stop=True).then_inc(ms_ready, 1)
                for k in range(KD):
                    pe.wait_ge(w_in[k], 16)
                pe.wait_ge(xn_ready, KD * NT)
                def project(n, first):
                    for m in range(KIN):
                        back = 6
                        if not first or m >= back:
                            q, r = (n, m - back) if m >= back else (n - 1, m - back + KIN)
                            sem, lot = (act_out, ACT_M) if r in ACT_M else (dve_out, DVE_M)
                            pe.wait_ge(sem, q * len(lot) + lot.index(r) + 1)
                        for k in range(KD):
                            mm = pe.matmul(pp[m % 6][:, 0:TW], w[:, k, m * P:(m + 1) * P], xn[:, k, bass.ds(n * TW, TW)] if not first else xn[:, k, tok(0)],
                                           start=(k == 0), stop=(k == KD - 1))
                        mm.then_inc(proj_ready, 1)
                project(0, True)
                with pe.Fori(1, NT) as n:
                    project(n, False)


def mix_out(nc, ins, y, hT, xn):
    with ExitStack() as ctx:
        e = Env(nc, ctx, "mo")
        w = e.sb("w", [P, KD, D])
        sq = e.sb("sq", [P, KD, TW])
        ssum = e.sb("ssum", [P, TW])
        rms = e.sb("rms", [P, TW])
        g = e.sb("g", [P, KD])
        eps = e.sb("eps", [P, 1])
        ones = e.sb("ones", [P, P])
        pn = [e.ps(f"pn{i}", [P, 512]) for i in range(2)]
        pp = [e.ps(f"pp{i}", [P, 512]) for i in range(6)]
        x_in = [e.sem(f"x_in{n}") for n in range(NT)]
        w_in = [e.sem(f"w_in{k}") for k in range(KD)]
        g_in, const_ready = e.sem("g_in"), e.sem("const_ready")
        out_ready, h_ready = e.sem("out_ready"), e.sem("h_ready")
        sq_ready, ssum_ready, ms_ready = e.sem("sq_ready"), e.sem("ssum_ready"), e.sem("ms_ready")
        rms_ready, inv_ready, xn_ready = e.sem("rms_ready"), e.sem("inv_ready"), e.sem("xn_ready")

        with nc.Block() as block:
            @block.sync
            def _(sp):
                for k in range(KD):
                    sp.dma_start(w[:, k, :], ins["w_out"][k]).then_inc(w_in[k], 16)
                    if k < NT:
                        sp.dma_start(hT[:, :, tok(k)], ins["xT"][:, :, tok(k)]).then_inc(x_in[k], 16)
                sp.dma_start(g[:], ins["norm2_g"]).then_inc(g_in, 16)

            @block.gpsimd
            def _(pool):
                pool.memset(ones[:], 1.0 / D).then_inc(const_ready, 1)
                pool.memset(eps[:], RMS_EPS).then_inc(const_ready, 1)

            @block.scalar
            def _(act):
                act.wait_ge(const_ready, 2)
                for n in range(NT):
                    act.wait_ge(h_ready, KD * (n + 1))
                    if n:
                        act.wait_ge(ssum_ready, n)
                    act.square(sq[:], hT[:, :, tok(n)]).then_inc(sq_ready, 1)
                    act.wait_ge(ms_ready, n + 1)
                    if n:
                        act.wait_ge(xn_ready, KD * n)
                    act.activation(rms[:], pn[n % 2][:, 0:TW], ACT.Sqrt, bias=eps[:, 0:1]).then_inc(rms_ready, 1)

            @block.vector
            def _(dve):
                def residual(n):
                    dve.wait_ge(x_in[n], 16)
                    for m in range(KD):
                        i = n * KD + m
                        dve.wait_ge(out_ready, i + 1)
                        hm = hT[:, m, tok(n)]
                        dve.tensor_tensor(hm, pp[i % 6][:, 0:TW], hm, ALU.add).then_inc(h_ready, 1)

                def norm_sum(n):
                    dve.wait_ge(sq_ready, n + 1)
                    if n:
                        dve.wait_ge(ms_ready, n)
                    dve.tensor_reduce(ssum[:], sq[:].rearrange("p k t -> p t k"), AX.X, ALU.add).then_inc(ssum_ready, 1)

                def norm_apply(n):
                    dve.wait_ge(rms_ready, n + 1)
                    dve.reciprocal(rms[:], rms[:]).then_inc(inv_ready, 1)
                    dve.wait_ge(inv_ready, n + 1)
                    for k in range(KD):
                        dve.scalar_tensor_tensor(xn[:, k, tok(n)], hT[:, k, tok(n)], g[:, k:k + 1], rms[:],
                                                 ALU.mult, ALU.mult).then_inc(xn_ready, 1)

                dve.wait_ge(g_in, 16)
                for n in range(NT):
                    residual(n)
                    norm_sum(n)
                    norm_apply(n)

            @block.tensor
            def _(pe):
                pe.wait_ge(const_ready, 2)

                def mean_square(n):
                    pe.wait_ge(ssum_ready, n + 1)
                    if n >= 2:
                        pe.wait_ge(rms_ready, n - 1)
                    pe.matmul(pn[n % 2][:, 0:TW], ones[:], ssum[:], start=True, stop=True).then_inc(ms_ready, 1)

                for n in range(NT):
                    for m in range(KD):
                        i = n * KD + m
                        if i >= 6:
                            pe.wait_ge(h_ready, i - 5)
                        for k in range(KD):
                            if i == 0:
                                pe.wait_ge(w_in[k], 16)
                            mm = pe.matmul(pp[i % 6][:, 0:TW], w[:, k, m * P:(m + 1) * P], y[k // KU][:, k % KU, tok(n)],
                                           start=(k == 0), stop=(k == KD - 1))
                        mm.then_inc(out_ready, 1)
                        if m == 4 and n:
                            mean_square(n - 1)
                mean_square(NT - 1)


def wait_count(eng, sem, turn, per, c):
    if isinstance(turn, int):
        if turn * per + c > 0:
            eng.wait_ge(sem, turn * per + c)
    else:
        eng.wait_ge(sem, turn * per + c)


def conv_ffn(nc, ins, outs, hT, xn):
    G = 2
    NG = KF // G
    GB = DS + 2
    with ExitStack() as ctx:
        e = Env(nc, ctx, "ff")
        wg = [e.sb(f"wg{q}", [P, KD, P]) for q in range(G)]
        wv = [e.sb(f"wv{q}", [P, KD, P]) for q in range(G)]
        wd = [e.sb(f"wd{q}", [P, D]) for q in range(G)]
        f = e.sb("f", [P, G, T])
        gp = e.sb("gp", [P, 2 + SEQ])
        gs = e.sb("gs", [P, DB, GB])
        cv = e.sb("cv", [P, 2, TW])
        sg = e.sb("sg", [P, 2, TW])
        cw = e.sb("cw", [P, KF, 4])
        taps = e.sb("taps", [P, G, 4])
        st = e.sb("st", [P, KF, DB, 2])
        keep_p = e.sb("keep_p", [P, KF, 2])
        keep_s = e.sb("keep_s", [P, KF, DB, 2])
        pg = [e.ps(f"pg{i}", [P, 512]) for i in range(2)]
        pv = [e.ps(f"pv{i}", [P, 512]) for i in range(2)]
        pd = [e.ps(f"pd{i}", [P, 512]) for i in range(4)]
        up_in = [e.sem(f"up_in{q}") for q in range(G)]
        down_in = e.sem("down_in")
        par_in = e.sem("par_in")
        zero_ready = e.sem("zero_ready")
        gate_mm, val_mm, down_mm = e.sem("gate_mm"), e.sem("val_mm"), e.sem("down_mm")
        gate_out = e.sem("gate_out")
        taps_ready = e.sem("taps_ready")
        tap0, tap1, conv_ready = e.sem("tap0"), e.sem("tap1"), e.sem("conv_ready")
        silu_ready, f_ready = e.sem("silu_ready"), e.sem("f_ready")
        h_ready = e.sem("h_ready")
        kept, stored = e.sem("kept"), e.sem("stored")
        NF = G * NT
        ND = NT * KD

        def turns(eng, body):
            body(0)
            with eng.Fori(1, NG) as g:
                body(g)

        with nc.Block() as block:
            @block.sync
            def _(sp):
                sp.dma_start(cw[:], ins["conv_wb"]).then_inc(par_in, 16)
                sp.dma_start(st[:], ins["state_conv"]).then_inc(par_in, 16)
                for g in range(NG):
                    for q in range(G):
                        if g:
                            sp.wait_ge(val_mm, NT * (G * (g - 1) + q + 1))
                        sp.dma_start(wg[q][:], ins["w_gate"][:, :, (G * g + q) * P:(G * g + q + 1) * P]).then_inc(up_in[q], 16)
                        sp.dma_start(wv[q][:], ins["w_val"][:, :, (G * g + q) * P:(G * g + q + 1) * P]).then_inc(up_in[q], 16)
                    if g:
                        sp.wait_ge(down_mm, ND * g)
                    for q in range(G):
                        sp.dma_start(wd[q][:], ins["w_down"][G * g + q]).then_inc(down_in, 16)
                sp.wait_ge(kept, KF)
                sp.dma_start(outs["conv_p"], keep_p[:]).then_inc(stored, 16)
                sp.dma_start(outs["conv_s"], keep_s[:]).then_inc(stored, 16)
                sp.wait_ge(stored, 32)

            @block.gpsimd
            def _(pool):
                pool.memset(gp[:, 0:2], 0.0).then_inc(zero_ready, 1)

            @block.scalar
            def _(act):
                act.wait_ge(zero_ready, 1)

                def turn(g):
                    for i in range(NF):
                        n, b = i % NT, i % 2
                        wait_count(act, gate_mm, g, NF, i + 1)
                        wait_count(act, conv_ready, g, NF, (i // NT - 1) * NT + min(n + 2, NT))
                        if n < NT - 1:
                            act.copy(gp[:, 2 + n * TW:2 + (n + 1) * TW], pg[b][:, 0:TW]).then_inc(gate_out, 1)
                        else:
                            act.copy(gp[:, 2 + n * TW:2 + SEQ], pg[b][:, 0:LASTP])
                            act.copy(gs[:, :, 2:GB], pg[b][:, LASTP:TW].rearrange("p (b s) -> p b s", b=DB)).then_inc(gate_out, 1)
                        wait_count(act, conv_ready, g, NF, i + 1)
                        wait_count(act, f_ready, g, NF, i - 1)
                        act.activation(sg[:, b, :], cv[:, b, :], ACT.Silu).then_inc(silu_ready, 1)
                turns(act, turn)

            @block.vector
            def _(dve):
                dve.wait_ge(par_in, 32)

                def turn(g):
                    for q in range(G):
                        dve.tensor_copy(taps[:, q, :], cw[:, bass.ds(g * G + q, 1), :].rearrange("p a c -> p (a c)")).then_inc(taps_ready, 1)
                    wait_count(dve, taps_ready, g, 2 * G, G)
                    for i in range(NF):
                        q, n, b = i // NT, i % NT, i % 2
                        tap = [taps[:, q, j:j + 1] for j in range(4)]
                        wait_count(dve, gate_out, g, NF, i + 1)
                        wait_count(dve, silu_ready, g, NF, i - 1)
                        c = cv[:, b, :]
                        if n < NT - 1:
                            rows = [(c, lambda j: gp[:, n * TW + j:n * TW + j + TW])]
                        else:
                            ff = bass.ds(g * G + q, 1)
                            dve.tensor_copy(keep_p[:, ff, :].rearrange("p a s -> p (a s)"), gp[:, SEQ:SEQ + 2])
                            dve.tensor_copy(keep_s[:, ff, :, :].rearrange("p a b s -> p (a b) s"), gs[:, :, DS:GB]).then_inc(kept, 1)
                            dve.tensor_copy(gs[:, :, 0:2], st[:, ff, :, :].rearrange("p a b s -> p (a b) s")).then_inc(taps_ready, 1)
                            wait_count(dve, taps_ready, g, 2 * G, G + q + 1)
                            rows = [(c[:, 0:LASTP], lambda j: gp[:, n * TW + j:n * TW + j + LASTP]),
                                    (c[:, LASTP:TW].rearrange("p (b s) -> p b s", b=DB), lambda j: gs[:, :, j:j + DS])]
                        for out, row in rows:
                            last = dve.tensor_scalar(out, row(2), tap[2], tap[3], ALU.mult, ALU.add)
                        last.then_inc(tap0, 1)
                        wait_count(dve, tap0, g, NF, i + 1)
                        for out, row in rows:
                            last = dve.scalar_tensor_tensor(out, row(1), tap[1], out, ALU.mult, ALU.add)
                        last.then_inc(tap1, 1)
                        wait_count(dve, tap1, g, NF, i + 1)
                        for out, row in rows:
                            last = dve.scalar_tensor_tensor(out, row(0), tap[0], out, ALU.mult, ALU.add)
                        last.then_inc(conv_ready, 1)
                        wait_count(dve, silu_ready, g, NF, i + 1)
                        wait_count(dve, val_mm, g, NF, i + 1)
                        dve.tensor_tensor(f[:, q, tok(n)], pv[b][:, 0:TW], sg[:, b, :], ALU.mult).then_inc(f_ready, 1)
                    for i in range(ND):
                        n, m = i // KD, i % KD
                        wait_count(dve, down_mm, g, ND, i + 1)
                        hm = hT[:, m, tok(n)]
                        dve.tensor_tensor(hm, pd[i % 4][:, 0:TW], hm, ALU.add).then_inc(h_ready, 1)
                turns(dve, turn)

            @block.tensor
            def _(pe):
                def turn(g):
                    for i in range(NF):
                        q, n, b = i // NT, i % NT, i % 2
                        if n == 0:
                            wait_count(pe, up_in[q], g, 32, 32)
                        wait_count(pe, gate_out, g, NF, i - 1)
                        for k in range(KD):
                            mm = pe.matmul(pg[b][:, 0:TW], wg[q][:, k, :], xn[:, k, tok(n)], start=(k == 0), stop=(k == KD - 1))
                        mm.then_inc(gate_mm, 1)
                        wait_count(pe, f_ready, g, NF, i - 1)
                        for k in range(KD):
                            mm = pe.matmul(pv[b][:, 0:TW], wv[q][:, k, :], xn[:, k, tok(n)], start=(k == 0), stop=(k == KD - 1))
                        mm.then_inc(val_mm, 1)
                    wait_count(pe, down_in, g, 16 * G, 16 * G)
                    for i in range(ND):
                        n, m = i // KD, i % KD
                        if m == 0:
                            wait_count(pe, f_ready, g, NF, NT + n + 1)
                        wait_count(pe, h_ready, g, ND, i - 3)
                        for q in range(G):
                            mm = pe.matmul(pd[i % 4][:, 0:TW], wd[q][:, m * P:(m + 1) * P], f[:, q, tok(n)], start=(q == 0), stop=(q == G - 1))
                        mm.then_inc(down_mm, 1)
                turns(pe, turn)


def gated_embedding(nc, ins, outs, hT, mix):
    with ExitStack() as ctx:
        e = Env(nc, ctx, "pe")
        wpg = e.sb("wpg", [P, KD, D])
        wple = e.sb("wple", [P, KP, D])
        flat = [x[:].rearrange("p k t -> p (k t)") for x in mix]
        n3 = 2 * KD * TW
        h3 = flat[0][:, 0:n3].rearrange("p (b k t) -> p b k t", b=2, k=KD)
        sq = flat[0][:, n3:n3 + KD * TW].rearrange("p (k t) -> p k t", k=KD)
        pt = flat[1][:, 0:KP * T].rearrange("p (k t) -> p k t", k=KP)
        sig = e.sb("sig", [P, 2, TW])
        ssum = e.sb("ssum", [P, TW])
        rms = e.sb("rms", [P, TW])
        g = e.sb("g", [P, KD])
        eps = e.sb("eps", [P, 1])
        ones = e.sb("ones", [P, P])
        pn = [e.ps(f"pn{i}", [P, 512]) for i in range(2)]
        pg = [e.ps(f"pg{i}", [P, 512]) for i in range(3)]
        pl = [e.ps(f"pl{i}", [P, 512]) for i in range(3)]
        w_in = [e.sem(f"w_in{k}") for k in range(KD)]
        ple_in, p_in, g_in, const_ready = e.sem("ple_in"), e.sem("p_in"), e.sem("g_in"), e.sem("const_ready")
        gate_mm, ple_mm = e.sem("gate_mm"), e.sem("ple_mm")
        sig_ready, prod_ready, h_ready = e.sem("sig_ready"), e.sem("prod_ready"), e.sem("h_ready")
        sq_ready, ssum_ready, ms_ready = e.sem("sq_ready"), e.sem("ssum_ready"), e.sem("ms_ready")
        rms_ready, inv_ready, y_ready = e.sem("rms_ready"), e.sem("inv_ready"), e.sem("y_ready")
        y_stored = [e.sem(f"y_stored{b}") for b in range(2)]

        with nc.Block() as block:
            @block.sync
            def _(sp):
                for k in range(KD):
                    sp.dma_start(wpg[:, k, :], ins["w_pg"][k]).then_inc(w_in[k], 16)
                for k in range(KP):
                    sp.dma_start(wple[:, k, :], ins["w_ple"][k]).then_inc(ple_in, 16)
                sp.dma_start(pt, ins["pT"]).then_inc(p_in, 16)
                sp.dma_start(g[:], ins["final_g"]).then_inc(g_in, 16)
                for n in range(NT):
                    sp.wait_ge(y_ready, KD * (n + 1))
                    sp.dma_start(outs["yT"][:, :, tok(n)], h3[:, n % 2]).then_inc(y_stored[n % 2], 16)
                for b in range(2):
                    sp.wait_ge(y_stored[b], 16 * (NT // 2))

            @block.gpsimd
            def _(pool):
                pool.memset(ones[:], 1.0 / D).then_inc(const_ready, 1)
                pool.memset(eps[:], RMS_EPS).then_inc(const_ready, 1)

            @block.scalar
            def _(act):
                act.wait_ge(const_ready, 2)
                for n in range(NT):
                    for m in range(KD):
                        i = n * KD + m
                        act.wait_ge(gate_mm, i + 1)
                        if i >= 2:
                            act.wait_ge(prod_ready, i - 1)
                        act.activation(sig[:, i % 2, :], pg[i % 3][:, 0:TW], ACT.Sigmoid).then_inc(sig_ready, 1)
                    act.wait_ge(h_ready, KD * (n + 1))
                    if n:
                        act.wait_ge(ssum_ready, n)
                    act.square(sq, h3[:, n % 2]).then_inc(sq_ready, 1)
                    act.wait_ge(ms_ready, n + 1)
                    if n:
                        act.wait_ge(y_ready, KD * n)
                    act.activation(rms[:], pn[n % 2][:, 0:TW], ACT.Sqrt, bias=eps[:, 0:1]).then_inc(rms_ready, 1)

            @block.vector
            def _(dve):
                dve.wait_ge(g_in, 16)
                for n in range(NT):
                    b = n % 2
                    if n >= 2:
                        dve.wait_ge(y_stored[b], 16 * (n // 2))
                    for m in range(KD):
                        i = n * KD + m
                        dve.wait_ge(sig_ready, i + 1)
                        dve.wait_ge(ple_mm, i + 1)
                        s = sig[:, i % 2, :]
                        dve.tensor_tensor(h3[:, b, m, :], pl[i % 3][:, 0:TW], s, ALU.mult).then_inc(prod_ready, 1)
                        dve.wait_ge(prod_ready, i + 1)
                        dve.tensor_tensor(h3[:, b, m, :], h3[:, b, m, :], hT[:, m, tok(n)], ALU.add).then_inc(h_ready, 1)
                    dve.wait_ge(sq_ready, n + 1)
                    if n:
                        dve.wait_ge(ms_ready, n)
                    dve.tensor_reduce(ssum[:], sq.rearrange("p k t -> p t k"), AX.X, ALU.add).then_inc(ssum_ready, 1)
                    dve.wait_ge(rms_ready, n + 1)
                    dve.reciprocal(rms[:], rms[:]).then_inc(inv_ready, 1)
                    dve.wait_ge(inv_ready, n + 1)
                    for k in range(KD):
                        y = h3[:, b, k, :]
                        dve.scalar_tensor_tensor(y, y, g[:, k:k + 1], rms[:], ALU.mult, ALU.mult).then_inc(y_ready, 1)

            @block.tensor
            def _(pe):
                pe.wait_ge(const_ready, 2)
                pe.wait_ge(ple_in, 16 * KP)
                pe.wait_ge(p_in, 16)

                def mean_square(n):
                    pe.wait_ge(ssum_ready, n + 1)
                    if n >= 2:
                        pe.wait_ge(rms_ready, n - 1)
                    pe.matmul(pn[n % 2][:, 0:TW], ones[:], ssum[:], start=True, stop=True).then_inc(ms_ready, 1)

                for n in range(NT):
                    for m in range(KD):
                        i = n * KD + m
                        if i >= 3:
                            pe.wait_ge(prod_ready, i - 2)
                        for k in range(KD):
                            if i == 0:
                                pe.wait_ge(w_in[k], 16)
                            mm = pe.matmul(pg[i % 3][:, 0:TW], wpg[:, k, m * P:(m + 1) * P], hT[:, k, tok(n)], start=(k == 0), stop=(k == KD - 1))
                        mm.then_inc(gate_mm, 1)
                        for k in range(KP):
                            mm = pe.matmul(pl[i % 3][:, 0:TW], wple[:, k, m * P:(m + 1) * P], pt[:, k, tok(n)], start=(k == 0), stop=(k == KP - 1))
                        mm.then_inc(ple_mm, 1)
                        if m == 2 and n:
                            mean_square(n - 1)
                mean_square(NT - 1)


C = 64
Q = 2
TB = C * Q
NB = SEQ // TB
TS = DB * DS
HP = 4
HD = 64
LOGW = math.exp(-0.5)
HALF = [slice(0, HD), slice(HD, P)]

PREP_POOL = [step + part for part in ("low", "k", "r", "v") for step in ("d_", "m_", "z_")] + ["rk0", "rk"]
PREP_DVE = ["kk", "ld", "L", "t0", "t1", "nmax", "inv0", "inv1", "aa", "sg", "inv2", "inv3", "kkn", "Lp", "b", "kp", "bonus"]
PREP_ACT = ["th", "sx", "kk2", "wt", "at", "nrm", "e1", "e2", "e3", "g"]
PREP_PE = ["w", "a", "ss", "g", "bonus"]
SHIFT = {"low": slice(12, 14), "k": slice(4, 8), "r": slice(0, 4), "v": slice(8, 12)}
STAGES = ["AabT", "Aab", "AqbT", "D2", "Dt2", "AakT", "D4", "Dt4", "X2", "D8", "X3", "Bt", "X4", "Kt", "X", "Z32", "Vt",
          "X32t", "X32", "Z64", "AqkT", "X64t", "RH", "U", "S", "Y"]
INTRA = STAGES[:22]
DVE_OUT = ["Dt", "Xt", "D", "O32", "O64", "AqbT", "AakT", "X2", "X3", "X4", "X32t", "X32", "AqkT", "X64t", "Sadd", "S"]
ACT_OUT = ["D2", "Dt2", "D4", "Dt4", "D8", "Bt", "Kt", "X", "Z32", "Vt", "Z64", "RH", "U", "Ylo", "Y"]
COPIED = {"AabT": "Dt", "Aab": "O64", "S": "Sadd"}
HAT_DVE = ["b", "a", "k"]
POST_DVE = ["d", "inv0", "inv1", "inv2", "inv3", "dn", "dg", "db", "dbonus", "y"]
NBANK = 3


def at(turn, order, name):
    return turn * len(order) + order.index(name) + 1


def delta_rule(nc, ins, outs, scratch, yb):
    with ExitStack() as ctx:
        e = Env(nc, ctx, "rw")
        w2 = e.sb("w2", [P, DRW])
        g2 = e.sb("g2", [P, DRW])
        mu = e.sb("mu", [P, ZT])
        col = {n: e.sb(n, [P, HP]) for n in ("w0", "a0", "k_k", "k_a", "r_k", "lnx_g", "lnx_b")}
        kah, ka1 = e.sb("kah", [P, HP]), e.sb("ka1", [P, HP])
        masks = e.sb("masks", [P, 13, P])
        bd64 = e.sb("bd64", [P, P])
        rows8 = e.sb("rows8", [P, DB])
        seg = e.sb("seg", [P, 2, HP * TB])
        geps = e.sb("geps", [P, 1])
        w0h, a0h = e.sb("w0h", [P, HP]), e.sb("a0h", [P, HP])
        Z = e.sb("Z", [P, ZT * (TB + 1)])
        z = e.sb("z", [P, ZT * TB])
        names = ("kk", "kk2", "w", "a", "L", "Lp", "E2", "E3", "t", "kp", "kkn", "b", "bonus", "g")
        B = {n: e.sb("p_" + n, [P, HP * TB]) for n in names}
        B |= {n: e.sb("p_" + n, [P, TB]) for n in ("th", "sx")}
        B |= {"nrm": B["kk2"], "ld": B["w"], "E1": B["Lp"], "rk": B["t"], "aa": B["a"]}
        bonus_h, g_h = e.sb("bonus_h", [P, HP * TB]), e.sb("g_h", [P, HP * TB])
        pc = e.sb("pc", [P, HP, DB])
        yt, ysq = e.sb("yt", [P, HP * TB]), e.sb("ysq", [P, HP * TB])
        yd, ysd = yt, ysq
        before_smp = e.sb("before_smp", [P, ZT, DB])
        keep = e.sb("keep", [P, ZT, 1 + DB])
        cn = ("aT", "bT", "kT", "rT", "vT", "Dt", "D", "O32", "O64", "AqbT", "AakT", "AqkT", "D2", "Dt2", "D4", "Dt4", "Xt")
        M = [{n: e.sb(f"{n}{q}", [P, HP, P]) for n in cn} for q in range(Q)]
        for m in M:
            m.update(D8=m["Dt"], Z=m["D"], Kt=m["D2"], Bt=m["Dt2"], X=m["D4"], Vt=m["Dt4"], RH=m["O32"], U=m["O64"])
        S = [e.sb(f"S{q}", [P, HP, P]) for q in range(Q)]
        Sb = [M[1][n] for n in ("aT", "bT", "kT", "rT", "vT", "AqbT", "AakT", "AqkT")]
        bank = [[e.ps(f"bank{q}{i}", [P, HP, P]) for i in range(NBANK)] for q in range(Q)]
        side = [e.ps(f"side{i}", [P, HP * P]) for i in range(2)]

        par_in, z_in = e.sem("par_in"), e.sem("z_in")
        setup, zero = e.sem("setup"), e.sem("zero")
        prep_dve, prep_act, prep_pe = e.sem("prep_dve"), e.sem("prep_act"), e.sem("prep_pe")
        prep_pool, kept = e.sem("prep_pool"), e.sem("kept")
        hats_dve = e.sem("hats_dve")
        hats_pool = [e.sem(f"hats_pool{q}") for q in range(Q)]
        mm = [e.sem(f"mm{q}") for q in range(Q)]
        dve_out = [e.sem(f"dve_out{q}") for q in range(Q)]
        act_out = [e.sem(f"act_out{q}") for q in range(Q)]
        post_pe, post_act, post_dve = e.sem("post_pe"), e.sem("post_act"), e.sem("post_dve")
        keep_ready, stored = e.sem("keep_ready"), e.sem("stored")
        smp_in, smp_pe, smp_dve, smp_act = e.sem("smp_in"), e.sem("smp_pe"), e.sem("smp_dve"), e.sem("smp_act")
        hats_act = [e.sem(f"hats_act{q}") for q in range(Q)]
        BD, MD, MO32, MO64, MDT, MSU, MU, ID, SD, SDT, SSU, SU, NONE = range(13)
        FIRST, SAMPLES = 0, NB

        def is_first(t):
            return isinstance(t, int) and t == FIRST

        def is_samples(t):
            return isinstance(t, int) and t == SAMPLES

        STATE_AT = {"RH": 1, "U": 4, "S": 6, "Y": 8}

        def schedule(eng, half):
            half(FIRST, 0)
            half(FIRST, 1)
            half(1, 0)
            with eng.Fori(1, NB - 2) as t:
                half(t, 1)
                half(t + 1, 0)
            for t in (NB - 2, NB - 1):
                half(t, 1)
                half(t + 1, 0)

        def width(t):
            return TS if is_samples(t) else TB

        def chunks(t):
            return 1 if is_samples(t) else Q

        def v3(buf, W, w=None):
            return buf[:, 0:HP * W].rearrange("p (j t) -> p j t", t=W)

        def zv(i, n, W):
            return z[:].rearrange("p (j t) -> p j t", t=TB)[:, i:i + n, 0:W]

        def mask(m):
            return masks[:, m:m + 1, :].to_broadcast([P, HP, P])

        def copied(stage):
            return COPIED.get(stage, stage)

        def wait_copied(eng, q, t, name):
            name = copied(name)
            if name in DVE_OUT:
                eng.wait_ge(dve_out[q], at(t, DVE_OUT, name))
            else:
                eng.wait_ge(act_out[q], at(t, ACT_OUT, name))

        with nc.Block() as block:
            @block.sync
            def _(sp):
                for dst, name in ((w2, "w2a2"), (g2, "g2"), (mu, "mu"), (masks, "masks"), (rows8, "rows8"), (seg, "seg")):
                    sp.dma_start(dst[:], ins[name]).then_inc(par_in, 16)
                for n, dst in col.items():
                    sp.dma_start(dst[:], ins[n]).then_inc(par_in, 16)
                sp.dma_start(before_smp[:], ins["state_shift"]).then_inc(par_in, 16)
                src = scratch["zr"].rearrange("z p t -> p z t")
                Zp = Z[:].rearrange("p (z t) -> p z t", t=TB + 1)
                sp.dma_start(Zp[:, :, 1:], src[:, :, 0:TB]).then_inc(z_in, 16)
                for t in range(1, NB):
                    sp.wait_ge(prep_pool, at(t - 1, PREP_POOL, "z_v"))
                    sp.dma_start(Zp[:], src[:, :, t * TB - 1:(t + 1) * TB]).then_inc(z_in, 16)
                Zs = Z[:, 0:ZT * DB * (DS + 1)].rearrange("p (z b s) -> p z b s", b=DB, s=DS + 1)
                sp.wait_ge(prep_pool, at(NB - 1, PREP_POOL, "z_v"))
                sp.wait_ge(keep_ready, 1)
                for zt in range(ZT):
                    sp.dma_start(Zs[:, zt, :, 1:], src[:, zt, SEQ:T].rearrange("p (b s) -> p b s", b=DB)).then_inc(z_in, 16)
                sp.wait_ge(mm[1], at(NB - 1, STAGES, "Y"))
                for b in range(DB):
                    for h in HALF:
                        sp.dma_start(Sb[b][h, :, h], ins["state_rwkv"][h, b]).then_inc(smp_in, 16)
                sp.wait_ge(keep_ready, 3)
                sp.dma_start(outs["shift"], keep[:]).then_inc(stored, 16)
                sp.wait_ge(dve_out[1], at(NB - 1, DVE_OUT, "S"))
                for h in range(2):
                    sp.dma_start(outs["rwkv_p"][HALF[h]], S[0][HALF[h], :, HALF[h]]).then_inc(stored, 16)
                sp.wait_ge(smp_dve, 4 * DB)
                for b in range(DB):
                    for h in range(2):
                        sp.dma_start(outs["rwkv_s"][HALF[h], b], Sb[b][HALF[h], :, HALF[h]]).then_inc(stored, 16)
                sp.wait_ge(stored, 16 * (3 + 2 * DB))

            @block.gpsimd
            def _(pool):
                pool.memset(S[0][:], 0.0).then_inc(zero, 1)
                pool.memset(Z[:].rearrange("p (z t) -> p z t", t=TB + 1)[:, :, 0:1], 0.0).then_inc(zero, 1)
                for q in range(Q):
                    for n in ("aT", "bT", "kT", "rT", "vT"):
                        pool.memset(M[q][n][:], 0.0).then_inc(zero, 1)
                pool.memset(geps[:], GN_EPS).then_inc(zero, 1)
                pool.wait_ge(zero, 13)

                def hats(t, q):
                    W = width(t)
                    pool.wait_ge(prep_act, at(t, PREP_ACT, "e3"))
                    if not is_first(t):
                        pool.wait_ge(mm[q], at(t - 1, STAGES, "Y"))
                    cq = slice(q * C, (q + 1) * C)
                    for n, h in enumerate(HALF):
                        pool.tensor_tensor(M[q]["rT"][h, :, h], zv(0, 4, W)[h, :, cq], v3(B["E3"], W)[h, :, cq], ALU.mult).then_inc(hats_pool[q], 1)
                        pool.wait_ge(hats_pool[q], 2 * t + n + 1)

                def shift(s, part):
                    W, n = width(s), SHIFT[part]
                    rows = n.stop - n.start
                    if is_samples(s):
                        Zs = Z[:, 0:ZT * DB * (DS + 1)].rearrange("p (z b s) -> p z b s", b=DB, s=DS + 1)
                        before, row = Zs[:, n, :, 0:DS], Zs[:, n, :, 1:]
                        zz = zv(n.start, rows, W).rearrange("p z (b s) -> p z b s", b=DB, s=DS)
                    else:
                        Zp = Z[:].rearrange("p (z t) -> p z t", t=TB + 1)
                        before, row = Zp[:, n, 0:TB], Zp[:, n, 1:]
                        zz = zv(n.start, rows, W)
                    flat = zv(n.start, rows, W)
                    pool.tensor_tensor(zz, before, row, ALU.subtract).then_inc(prep_pool, 1)
                    pool.wait_ge(prep_pool, at(s, PREP_POOL, "d_" + part))
                    pool.tensor_tensor(flat, flat, bcast(mu[:, n], W), ALU.mult).then_inc(prep_pool, 1)
                    pool.wait_ge(prep_pool, at(s, PREP_POOL, "m_" + part))
                    pool.tensor_tensor(zz, zz, row, ALU.add).then_inc(prep_pool, 1)

                def shift_early(s):
                    if is_samples(s):
                        pool.wait_ge(z_in, 16 * (NB + ZT))
                        Zs = Z[:, 0:ZT * DB * (DS + 1)].rearrange("p (z b s) -> p z b s", b=DB, s=DS + 1)
                        pool.tensor_copy(Zs[:, :, :, 0], before_smp[:]).then_inc(keep_ready, 1)
                        pool.wait_ge(keep_ready, 2)
                    else:
                        pool.wait_ge(z_in, 16 * (s + 1))
                    if not is_first(s):
                        pool.wait_ge(prep_dve, at(s - 1, PREP_DVE, "bonus"))
                    shift(s, "low")
                    shift(s, "k")

                def shift_late(s):
                    if not is_first(s):
                        for q in range(Q):
                            pool.wait_ge(hats_act[q], s)
                    shift(s, "r")
                    shift(s, "v")
                    W = width(s)
                    rk = v3(B["rk"], W)
                    pool.wait_ge(prep_dve, at(s, PREP_DVE, "kp"))
                    pool.wait_ge(prep_pool, at(s, PREP_POOL, "z_v"))
                    pool.tensor_tensor(rk, zv(0, 4, W), v3(B["kp"], W), ALU.mult).then_inc(prep_pool, 1)
                    pool.wait_ge(prep_pool, at(s, PREP_POOL, "rk0"))
                    pool.tensor_tensor(rk, rk, bcast(col["r_k"][:], W), ALU.mult).then_inc(prep_pool, 1)

                def turn(t):
                    shift_early(t + 1)
                    hats(t, 1)
                    shift_late(t + 1)
                    hats(t + 1, 0)

                pool.wait_ge(par_in, 16 * 14)
                shift_early(FIRST)
                shift_late(FIRST)
                hats(FIRST, 0)
                turn(FIRST)
                with pool.Fori(1, NB - 1) as t:
                    turn(t)
                pool.tensor_copy(keep[:, :, 0:1], Z[:].rearrange("p (z t) -> p z t", t=TB + 1)[:, :, TB:TB + 1]).then_inc(keep_ready, 1)
                pool.wait_ge(keep_ready, 1)
                turn(NB - 1)
                Zs = Z[:, 0:ZT * DB * (DS + 1)].rearrange("p (z b s) -> p z b s", b=DB, s=DS + 1)
                pool.tensor_copy(keep[:, :, 1:], Zs[:, :, :, DS]).then_inc(keep_ready, 1)

            @block.vector
            def _(dve):
                dve.wait_ge(par_in, 16 * 14)
                dve.tensor_scalar(kah[:], col["k_a"][:], 0.5, None, ALU.mult).then_inc(setup, 1)
                dve.tensor_scalar(ka1[:], col["k_a"][:], -0.5, 1.0, ALU.mult, ALU.add).then_inc(setup, 1)
                dve.tensor_scalar(bd64[:], masks[:, BD, :], 1.0 / HD, None, ALU.mult).then_inc(setup, 1)
                dve.tensor_scalar(w0h[:], col["w0"][:], 0.5, None, ALU.mult).then_inc(setup, 1)
                dve.tensor_scalar(a0h[:], col["a0"][:], 0.5, None, ALU.mult).then_inc(setup, 1)
                dve.wait_ge(setup, 5)
                dve.wait_ge(zero, 13)

                def prepare(s, *steps):
                    W = width(s)
                    b = {n: v3(x, W) for n, x in B.items() if n not in ("th", "sx")}
                    k, v = zv(4, 4, W), zv(8, 4, W)

                    def mine(name):
                        dve.wait_ge(prep_dve, at(s, PREP_DVE, name))

                    def act_did(name):
                        dve.wait_ge(prep_act, at(s, PREP_ACT, name))

                    for step in steps:
                        if step == "kk":
                            dve.wait_ge(prep_pool, at(s, PREP_POOL, "z_k"))
                            dve.tensor_tensor(b["kk"], k, bcast(col["k_k"][:], W), ALU.mult).then_inc(prep_dve, 1)
                        elif step == "L":
                            act_did("wt")
                            dve.tensor_scalar(b["ld"], b["w"], -LOGW / 2, -LOGW / 2, ALU.mult, ALU.add).then_inc(prep_dve, 1)
                            mine("ld")
                            dve.tensor_tensor_scan(B["L"][:, 0:HP * W], seg[:, 1 if is_samples(s) else 0, 0:HP * W], B["ld"][:, 0:HP * W], 0.0,
                                                   ALU.mult, ALU.add).then_inc(prep_dve, 1)
                        elif step == "t":
                            act_did("at")
                            dve.tensor_tensor(b["t"], b["a"], bcast(kah[:], W), ALU.mult).then_inc(prep_dve, 1)
                            mine("t0")
                            dve.tensor_tensor(b["t"], b["t"], bcast(ka1[:], W), ALU.add).then_inc(prep_dve, 1)
                        elif step == "nmax":
                            act_did("nrm")
                            dve.tensor_scalar(b["nrm"], b["nrm"], L2_EPS, None, ALU.max).then_inc(prep_dve, 1)
                        elif step in range(HP):
                            mine("nmax")
                            dve.reciprocal(b["nrm"][:, step], b["nrm"][:, step]).then_inc(prep_dve, 1)
                        elif step == "aa":
                            mine("t0")
                            dve.tensor_scalar(b["aa"], b["a"], 0.5, 0.5, ALU.mult, ALU.add).then_inc(prep_dve, 1)
                        elif step == "sg":
                            act_did("sx")
                            dve.tensor_scalar(B["sx"][:, 0:W], B["sx"][:, 0:W], 0.5, 0.5, ALU.mult, ALU.add).then_inc(prep_dve, 1)
                        elif step == "kkn":
                            mine("inv3")
                            dve.tensor_tensor(b["kkn"], b["kk"], b["nrm"], ALU.mult).then_inc(prep_dve, 1)
                        elif step == "Lp":
                            mine("L")
                            dve.tensor_tensor(b["Lp"], b["L"], b["ld"], ALU.subtract).then_inc(prep_dve, 1)
                        elif step == "b":
                            mine("kkn")
                            dve.tensor_tensor(b["b"], b["kkn"], b["aa"], ALU.mult).then_inc(prep_dve, 1)
                        elif step == "kp":
                            mine("t1")
                            dve.tensor_tensor(b["kp"], k, b["t"], ALU.mult).then_inc(prep_dve, 1)
                        elif step == "bonus":
                            dve.wait_ge(prep_pe, at(s, PREP_PE, "bonus"))
                            if not is_first(s):
                                dve.wait_ge(kept, 2 * s)
                            dve.tensor_tensor(b["bonus"], v3(side[1], W), v, ALU.mult).then_inc(prep_dve, 1)

                def hats(t, q, *names):
                    W = width(t)
                    b = {n: v3(x, W) for n, x in B.items() if n not in ("th", "sx")}
                    cq = slice(q * C, (q + 1) * C)
                    m = M[q]
                    for name in names:
                        if name == "bT":
                            dve.wait_ge(prep_act, at(t, PREP_ACT, "e3"))
                            dve.wait_ge(prep_dve, at(t, PREP_DVE, "kp"))
                            if not is_first(t):
                                dve.wait_ge(mm[q], at(t - 1, STAGES, "Y"))
                        for h in HALF:
                            if name == "bT":
                                last = dve.tensor_tensor(m["bT"][h, :, h], b["b"][h, :, cq], b["E2"][h, :, cq], ALU.mult)
                            elif name == "aT":
                                last = dve.scalar_tensor_tensor(m["aT"][h, :, h], b["kkn"][h, :, cq], -1.0, b["E1"][h, :, cq], ALU.mult, ALU.mult)
                            else:
                                last = dve.tensor_tensor(m["kT"][h, :, h], b["kp"][h, :, cq], b["E2"][h, :, cq], ALU.mult)
                        last.then_inc(hats_dve, 1)

                def copy_out(q, t, stage):
                    m, smp = M[q], is_samples(t)
                    src = bank[q][STAGES.index(stage) % NBANK][:]
                    dve.wait_ge(mm[q], at(t, STAGES, stage))

                    def masked(name, which):
                        dve.tensor_tensor(m[name][:], src, mask(which), ALU.mult).then_inc(dve_out[q], 1)

                    if stage == "AabT":
                        masked("Dt", SDT if smp else MDT)
                        dve.wait_ge(dve_out[q], at(t, DVE_OUT, "Dt"))
                        dve.tensor_tensor(m["Xt"][:], m["Dt"][:], mask(ID), ALU.add).then_inc(dve_out[q], 1)
                    elif stage == "Aab":
                        masked("D", SD if smp else MD)
                        masked("O32", NONE if smp else MO32)
                        masked("O64", NONE if smp else MO64)
                    elif stage in ("AqbT", "AqkT"):
                        masked(stage, SU if smp else MU)
                    elif stage == "AakT":
                        masked(stage, SSU if smp else MSU)
                    elif stage in ("X2", "X3", "X4", "X32t", "X64t"):
                        dve.tensor_tensor(m["Xt"][:], src, m["Xt"][:], ALU.add).then_inc(dve_out[q], 1)
                    elif stage == "X32":
                        dve.wait_ge(act_out[q], at(t, ACT_OUT, "X"))
                        dve.tensor_tensor(m["X"][:], src, m["X"][:], ALU.add).then_inc(dve_out[q], 1)
                    elif stage == "S":
                        old, new = S[q], S[1 - q]
                        dve.tensor_tensor(new[:], src, old[:], ALU.add).then_inc(dve_out[q], 1)
                        dve.wait_ge(dve_out[q], at(t, DVE_OUT, "Sadd"))
                        dve.wait_ge(kept, 2 * t + 1)
                        dve.tensor_tensor(new[:], new[:], pc[:, :, q:q + 1].to_broadcast([P, HP, P]), ALU.mult).then_inc(dve_out[q], 1)

                def finish(t, *steps):
                    W = width(t)
                    y, d, sd = v3(yt, W), v3(yd, W), v3(ysd, W)

                    def mine(name):
                        dve.wait_ge(post_dve, at(t, POST_DVE, name))

                    for step in steps:
                        if step == "d":
                            dve.wait_ge(post_pe, 2 * t + 1)
                            dve.tensor_tensor(d, y, v3(side[1], W), ALU.subtract).then_inc(post_dve, 1)
                        elif step in range(HP):
                            dve.wait_ge(post_act, 2 * t + 2)
                            dve.reciprocal(sd[:, step], sd[:, step]).then_inc(post_dve, 1)
                        elif step == "dn":
                            mine("inv3")
                            dve.tensor_tensor(d, d, sd, ALU.mult).then_inc(post_dve, 1)
                        elif step == "dg":
                            mine("dn")
                            dve.tensor_tensor(d, d, bcast(col["lnx_g"][:], W), ALU.mult).then_inc(post_dve, 1)
                        elif step == "db":
                            mine("dg")
                            dve.tensor_tensor(d, d, bcast(col["lnx_b"][:], W), ALU.add).then_inc(post_dve, 1)
                        elif step == "dbonus":
                            mine("db")
                            dve.wait_ge(kept, 2 * t + 2)
                            dve.tensor_tensor(d, d, v3(bonus_h, W), ALU.add).then_inc(post_dve, 1)
                        elif step == "y":
                            mine("dbonus")
                            dve.tensor_tensor(yb[:, :, bass.ds(t * TB, W)], d, v3(g_h, W), ALU.mult).then_inc(post_dve, 1)

                ADD = {"AabT", "Aab", "AqbT", "AakT", "X2", "AqkT", "X3", "X4", "X32t", "X32", "X64t"}
                NEXT = [{3: ["kk"], 9: ["L", "t"], 15: ["nmax", 0], 16: [1], 19: ["aa", "sg"]},
                        {3: [2, 3], 4: ["kkn", "Lp"], 7: ["b", "kp"], 19: ["bonus"]}]
                BEFORE = [{11: ["d"]}, {8: [0, 1, 2, 3], 11: ["dn"], 13: ["dg", "db"], 14: ["dbonus", "y"]}]
                HATS = [{13: ["bT", "aT"], 14: ["kT"]}, {15: ["bT", "aT"], 16: ["kT"]}]
                REST = [step for i in BEFORE[1] for step in BEFORE[1][i]]

                def half(t, q):
                    before = (t, 0) if q else (t - 1, 1)
                    for i, stage in enumerate(INTRA):
                        if stage in ADD:
                            copy_out(q, t, stage)
                        if i == STATE_AT["S"] and not (q == 0 and is_first(t)):
                            copy_out(before[1], before[0], "S")
                        if i in HATS[q] and not is_samples(t):
                            hats(t + q, 1 - q, *HATS[q][i])
                        if i in NEXT[q] and not is_samples(t):
                            prepare(t + 1, *NEXT[q][i])
                        if i in BEFORE[q] and not is_first(t):
                            finish(t - 1, *BEFORE[q][i])

                prepare(FIRST, "kk", "L", "t", "nmax", 0, 1, "aa", "sg", 2, 3, "kkn", "Lp", "b", "kp", "bonus")
                hats(FIRST, 0, "bT", "aT", "kT")
                schedule(dve, half)
                finish(NB - 1, *REST)
                m = M[0]
                for b in range(DB):
                    if b == 0:
                        dve.wait_ge(smp_act, 3)
                        dve.wait_ge(act_out[0], at(SAMPLES, ACT_OUT, "Vt"))
                        dve.wait_ge(smp_pe, 4)
                    dve.tensor_scalar(M[1]["D2"][:], m["U"][:], rows8[:, b:b + 1], None, ALU.mult).then_inc(smp_dve, 1)
                    dve.tensor_scalar(M[1]["Dt2"][:], m["Vt"][:], rows8[:, b:b + 1], None, ALU.mult).then_inc(smp_dve, 1)
                    if b == 0:
                        dve.wait_ge(smp_in, 16 * 2 * DB)
                    dve.wait_ge(smp_pe, 5 + b)
                    dve.tensor_tensor(Sb[b][:], bank[0][b % NBANK][:], Sb[b][:], ALU.add).then_inc(smp_dve, 1)
                    dve.wait_ge(smp_dve, 4 * b + 3)
                    dve.wait_ge(kept, 2 * SAMPLES + 1)
                    dve.tensor_tensor(Sb[b][:], Sb[b][:], pc[:, :, b:b + 1].to_broadcast([P, HP, P]), ALU.mult).then_inc(smp_dve, 1)
                finish(SAMPLES, "d", *REST)

            @block.scalar
            def _(act):
                act.wait_ge(zero, 13)
                act.wait_ge(setup, 5)

                def prepare(s, *steps):
                    W = width(s)
                    b = {n: v3(x, W) for n, x in B.items() if n not in ("th", "sx")}

                    def dve_did(name):
                        act.wait_ge(prep_dve, at(s, PREP_DVE, name))

                    for step in steps:
                        if step == "th":
                            act.wait_ge(prep_pool, at(s, PREP_POOL, "z_low"))
                            act.activation(B["th"][0:HD, 0:W], zv(12, 1, W)[0:HD, 0, :], ACT.Tanh).then_inc(prep_act, 1)
                            act.activation(B["sx"][:, 0:W], zv(13, 1, W)[:, 0, :], ACT.Tanh, scale=0.5).then_inc(prep_act, 1)
                        elif step == "kk2":
                            dve_did("kk")
                            act.square(b["kk2"], b["kk"]).then_inc(prep_act, 1)
                        elif step in ("wt", "at"):
                            which, half_bias, n = ("w", w0h, 0) if step == "wt" else ("a", a0h, 1)
                            act.wait_ge(prep_pe, at(s, PREP_PE, which))
                            if not is_first(s):
                                act.wait_ge(prep_dve, at(s - 1, PREP_DVE, "b"))
                            for j in range(HP):
                                last = act.activation(b[which][:, j], v3(side[n], W)[:, j], ACT.Tanh, bias=half_bias[:, j:j + 1], scale=0.5)
                            last.then_inc(prep_act, 1)
                        elif step == "nrm":
                            act.wait_ge(prep_pe, at(s, PREP_PE, "ss"))
                            act.activation(b["nrm"], v3(side[1], W), ACT.Sqrt).then_inc(prep_act, 1)
                        elif step == "e":
                            if not is_first(s):
                                act.wait_ge(hats_pool[0], s * 2)
                                act.wait_ge(hats_pool[1], s * 2)
                                act.wait_ge(hats_dve, s * 6)
                                act.wait_ge(kept, 2 * s - 1)
                            dve_did("Lp")
                            act.activation(b["E1"], b["Lp"], ACT.Exp).then_inc(prep_act, 1)
                            act.activation(b["E2"], b["L"], ACT.Exp, scale=-1.0).then_inc(prep_act, 1)
                            act.activation(b["E3"], b["L"], ACT.Exp).then_inc(prep_act, 1)
                        elif step == "g":
                            act.wait_ge(prep_pe, at(s, PREP_PE, "g"))
                            if not is_first(s):
                                act.wait_ge(kept, 2 * s)
                            act.copy(b["g"], v3(side[0], W)).then_inc(prep_act, 1)

                def hats(t, q):
                    W = width(t)
                    act.wait_ge(prep_pool, at(t, PREP_POOL, "z_v"))
                    if not is_first(t):
                        act.wait_ge(mm[q], at(t - 1, STAGES, "Y"))
                    for h in HALF:
                        last = act.copy(M[q]["vT"][h, :, h], zv(8, 4, W)[h, :, q * C:(q + 1) * C])
                    last.then_inc(hats_act[q], 1)

                def keep_decays(t):
                    W = width(t)
                    if not is_first(t):
                        act.wait_ge(dve_out[1], at(t - 1, DVE_OUT, "S"))
                    step = DS if is_samples(t) else C
                    act.copy(pc[:, :, 0:W // step], v3(B["E3"], W)[:, :, step - 1::step]).then_inc(kept, 1)

                def keep_gate(t):
                    W = width(t)
                    act.wait_ge(prep_dve, at(t, PREP_DVE, "bonus"))
                    if not is_first(t):
                        act.wait_ge(post_dve, at(t - 1, POST_DVE, "y"))
                    act.copy(bonus_h[:, 0:HP * W], B["bonus"][:, 0:HP * W])
                    act.copy(g_h[:, 0:HP * W], B["g"][:, 0:HP * W]).then_inc(kept, 1)

                def copy_out(q, t, stage):
                    dst = {"Z32": "Z", "Z64": "Z"}.get(stage, stage)
                    act.wait_ge(mm[q], at(t, STAGES, stage))
                    act.copy(M[q][dst][:], bank[q][STAGES.index(stage) % NBANK][:]).then_inc(act_out[q], 1)

                def rows_out(q, t):
                    if q == 0 and not is_first(t):
                        act.wait_ge(post_dve, at(t - 1, POST_DVE, "y"))
                    act.wait_ge(mm[q], at(t, STAGES, "Y"))
                    src = bank[q][STAGES.index("Y") % NBANK]
                    for h in HALF:
                        act.copy(v3(yt, TB)[h, :, q * C:(q + 1) * C], src[h, :, h]).then_inc(act_out[q], 1)

                def finish(t, part):
                    W = width(t)
                    if part == 0:
                        act.wait_ge(post_dve, at(t, POST_DVE, "d"))
                        act.square(v3(ysq, W), v3(yd, W)).then_inc(post_act, 1)
                        return
                    act.wait_ge(post_pe, 2 * t + 2)
                    act.activation(v3(ysd, W), v3(side[0], W), ACT.Sqrt, bias=geps[:, 0:1]).then_inc(post_act, 1)

                PLAIN = {"D2", "Dt2", "D4", "Dt4", "D8", "Bt", "Kt", "X", "Vt", "Z32", "Z64"}
                NEXT = [{4: ["th"], 5: ["kk2"], 7: ["wt", "at"], 8: ["nrm"]}, {8: ["e"], 19: ["g"]}]
                BEFORE = [{12: 0, 16: 1}, {}]
                HATS_AT, ROWS_AT = [9, 17], [9, 16]

                def half(t, q):
                    before = (t, 0) if q else (t - 1, 1)
                    for i, stage in enumerate(INTRA):
                        if q and i == 0:
                            keep_decays(t)
                        if stage in PLAIN:
                            copy_out(q, t, stage)
                        if not (q == 0 and is_first(t)):
                            if i == STATE_AT["RH"]:
                                copy_out(before[1], before[0], "RH")
                            if i == STATE_AT["U"]:
                                copy_out(before[1], before[0], "U")
                        if q and i == ROWS_AT[1]:
                            keep_gate(t)
                        if i == ROWS_AT[q] and not (q == 0 and is_first(t)):
                            rows_out(before[1], before[0])
                        if i == HATS_AT[q] and not is_samples(t):
                            hats(t + q, 1 - q)
                        if i in NEXT[q] and not is_samples(t):
                            prepare(t + 1, *NEXT[q][i])
                        if i in BEFORE[q] and not is_first(t):
                            finish(t - 1, BEFORE[q][i])

                prepare(FIRST, "th", "kk2", "wt", "at", "nrm", "e", "g")
                hats(FIRST, 0)
                schedule(act, half)
                keep_decays(SAMPLES)
                keep_gate(SAMPLES)
                m = M[0]
                act.wait_ge(smp_pe, 1)
                act.copy(m["RH"][:], bank[1][2][:]).then_inc(smp_act, 1)
                act.wait_ge(smp_pe, 2)
                act.copy(m["Z"][:], bank[1][0][:]).then_inc(smp_act, 1)
                act.wait_ge(smp_pe, 3)
                act.copy(m["U"][:], bank[1][2][:]).then_inc(smp_act, 1)
                act.wait_ge(smp_pe, 4)
                for h in HALF:
                    last = act.copy(v3(yt, TS)[h], bank[1][1][h, :, h])
                last.then_inc(smp_act, 1)
                finish(SAMPLES, 0)
                finish(SAMPLES, 1)

            @block.tensor
            def _(pe):
                pe.wait_ge(par_in, 16 * 14)
                pe.wait_ge(setup, 5)
                pe.wait_ge(zero, 13)
                ident = masks[:, ID, :]

                def prepare(s, *steps):
                    W = width(s)

                    def low_rank(bank_, w, x):
                        for j in range(HP):
                            last = pe.matmul(v3(bank_, W)[:, j, :], w[:, j * P:(j + 1) * P], x, start=True, stop=True)
                        last.then_inc(prep_pe, 1)

                    def dve_did(name):
                        pe.wait_ge(prep_dve, at(s, PREP_DVE, name))

                    def act_did(name):
                        pe.wait_ge(prep_act, at(s, PREP_ACT, name))

                    for step in steps:
                        if step == "w":
                            act_did("th")
                            if not is_first(s):
                                pe.wait_ge(prep_act, at(s - 1, PREP_ACT, "g"))
                                pe.wait_ge(prep_dve, at(s - 1, PREP_DVE, "bonus"))
                            low_rank(side[0], w2[0:HD, :], B["th"][0:HD, 0:W])
                            low_rank(side[1], w2[HD:P, :], zv(12, 1, W)[HD:P, 0, :])
                        elif step == "ss":
                            act_did("at")
                            pe.matmul(side[1][:, 0:HP * W], masks[:, BD, :], B["kk2"][:, 0:HP * W], start=True, stop=True).then_inc(prep_pe, 1)
                        elif step == "g":
                            act_did("wt")
                            dve_did("sg")
                            if not (is_first(s) or (isinstance(s, int) and s == 1)):
                                pe.wait_ge(post_act, 2 * (s - 1))
                            low_rank(side[0], g2[:], B["sx"][:, 0:W])
                        elif step == "bonus":
                            act_did("nrm")
                            pe.wait_ge(prep_pool, at(s, PREP_POOL, "rk"))
                            if not (is_first(s) or (isinstance(s, int) and s == 1)):
                                pe.wait_ge(post_dve, at(s - 2, POST_DVE, "d"))
                            pe.matmul(side[1][:, 0:HP * W], masks[:, BD, :], B["rk"][:, 0:HP * W], start=True, stop=True).then_inc(prep_pe, 1)

                LAST_IN_BANK = ["S", "Y", "U"]

                def product(q, t, stage, operands, after=(), transpose=False):
                    i = STAGES.index(stage)
                    names = [copied(n) for n in after] + ([copied(STAGES[i - NBANK])] if i >= NBANK else [])
                    for sem, order in ((dve_out[q], DVE_OUT), (act_out[q], ACT_OUT)):
                        mine = [n for n in names if n in order]
                        if mine:
                            pe.wait_ge(sem, at(t, order, max(mine, key=order.index)))
                    if i < NBANK and not is_first(t):
                        wait_copied(pe, q, t - 1, LAST_IN_BANK[i])
                    out = bank[q][STAGES.index(stage) % NBANK]
                    for j in range(HP):
                        for n, (l, r) in enumerate(operands):
                            if transpose:
                                last = pe.transpose(out[:, j, :], l[:, j, :], ident)
                            else:
                                last = pe.matmul(out[:, j, :], l[:, j, :], r[:, j, :], start=(n == 0), stop=(n == len(operands) - 1))
                    last.then_inc(mm[q], 1)

                def intra(q, t, stage):
                    m = M[q]
                    dve_hats = 6 * t + 3 * q
                    if stage == "AabT":
                        pe.wait_ge(hats_dve, dve_hats + 2)
                        product(q, t, stage, [(m["bT"], m["aT"])])
                    elif stage == "Aab":
                        product(q, t, stage, [(m["aT"], m["bT"])])
                    elif stage == "AqbT":
                        pe.wait_ge(hats_pool[q], 2 * t + 2)
                        product(q, t, stage, [(m["bT"], m["rT"])])
                    elif stage == "D2":
                        product(q, t, stage, [(m["Dt"], m["D"])], after=["Dt", "D"])
                    elif stage == "Dt2":
                        product(q, t, stage, [(m["D"], m["Dt"])])
                    elif stage == "AakT":
                        pe.wait_ge(hats_dve, dve_hats + 3)
                        product(q, t, stage, [(m["kT"], m["aT"])])
                    elif stage == "D4":
                        product(q, t, stage, [(m["Dt2"], m["D2"])], after=["D2", "Dt2"])
                    elif stage == "Dt4":
                        product(q, t, stage, [(m["D2"], m["Dt2"])])
                    elif stage == "X2":
                        product(q, t, stage, [(m["D2"], m["Xt"])], after=["Xt"])
                    elif stage == "AqkT":
                        product(q, t, stage, [(m["kT"], m["rT"])])
                    elif stage == "D8":
                        product(q, t, stage, [(m["Dt4"], m["D4"])], after=["D4", "Dt4"])
                    elif stage == "X3":
                        product(q, t, stage, [(m["D4"], m["Xt"])], after=["X2"])
                    elif stage == "Bt":
                        product(q, t, stage, [(m["bT"], None)], transpose=True)
                    elif stage == "X4":
                        product(q, t, stage, [(m["D8"], m["Xt"])], after=["D8", "X3"])
                    elif stage == "Kt":
                        product(q, t, stage, [(m["kT"], None)], transpose=True)
                    elif stage == "X":
                        product(q, t, stage, [(m["Xt"], None)], after=["X4"], transpose=True)
                    elif stage == "Vt":
                        pe.wait_ge(hats_act[q], t + 1)
                        product(q, t, stage, [(m["vT"], None)], transpose=True)
                    elif stage == "Z32":
                        product(q, t, stage, [(m["O32"], m["Xt"])], after=["O32"])
                    elif stage == "X32t":
                        product(q, t, stage, [(m["X"], m["Z"])], after=["X", "Z32"])
                    elif stage == "X32":
                        product(q, t, stage, [(m["Z"], m["X"])])
                    elif stage == "Z64":
                        product(q, t, stage, [(m["O64"], m["Xt"])], after=["X32t"])
                    elif stage == "X64t":
                        product(q, t, stage, [(m["X"], m["Z"])], after=["X32", "Z64"])

                def with_state(q, t, stage):
                    m = M[q]
                    if stage == "RH":
                        if q == 1:
                            pe.wait_ge(dve_out[0], at(t, DVE_OUT, "S"))
                        elif not is_first(t):
                            pe.wait_ge(dve_out[1], at(t - 1, DVE_OUT, "S"))
                        product(q, t, stage, [(m["aT"], S[q]), (m["AakT"], m["Vt"])], after=["AakT", "Vt"])
                    elif stage == "U":
                        product(q, t, stage, [(m["Xt"], m["RH"])], after=["X64t", "RH"])
                    elif stage == "S":
                        product(q, t, stage, [(m["Bt"], m["U"]), (m["Kt"], m["Vt"])], after=["Bt", "Kt", "U"])
                    elif stage == "Y":
                        product(q, t, stage, [(S[q], m["rT"]), (m["U"], m["AqbT"]), (m["Vt"], m["AqkT"])], after=["AqbT", "AqkT"])

                def finish(t, part):
                    W = width(t)
                    if part == 1:
                        pe.wait_ge(post_act, 2 * t + 1)
                        if isinstance(t, int) and t == NB - 1:
                            pe.wait_ge(prep_act, at(SAMPLES, PREP_ACT, "g"))
                        pe.matmul(side[0][:, 0:HP * W], bd64[:], ysq[:, 0:HP * W], start=True, stop=True).then_inc(post_pe, 1)
                        return
                    if is_samples(t):
                        pe.wait_ge(smp_act, 4)
                    else:
                        for q in range(Q):
                            pe.wait_ge(act_out[q], at(t, ACT_OUT, "Y"))
                    if is_samples(t):
                        pe.wait_ge(post_dve, at(NB - 1, POST_DVE, "d"))
                        pe.wait_ge(post_act, 2 * NB)
                    elif isinstance(t, int) and t == NB - 1:
                        pe.wait_ge(prep_dve, at(SAMPLES, PREP_DVE, "bonus"))
                    else:
                        pe.wait_ge(prep_act, at(t + 2, PREP_ACT, "nrm"))
                    pe.matmul(side[1][:, 0:HP * W], bd64[:], yt[:, 0:HP * W], start=True, stop=True).then_inc(post_pe, 1)

                NEXT = [{5: ["w"], 7: ["ss"]}, {3: ["g"], 17: ["bonus"]}]
                BEFORE = [{11: 0, 14: 1}, {}]

                def half(t, q):
                    before = (t, 0) if q else (t - 1, 1)
                    for i, stage in enumerate(INTRA):
                        intra(q, t, stage)
                        if not (q == 0 and is_first(t)):
                            for step, after in STATE_AT.items():
                                if i == after:
                                    with_state(before[1], before[0], step)
                        if i in NEXT[q] and not is_samples(t):
                            prepare(t + 1, *NEXT[q][i])
                        if i in BEFORE[q] and not is_first(t):
                            finish(t - 1, BEFORE[q][i])

                prepare(FIRST, "w", "ss", "g", "bonus")
                schedule(pe, half)
                m = M[0]
                tok_of = lambda ap, j, b: ap[:, j, :].rearrange("p (h b s) -> p h b s", h=2, b=DB)[:, :, b, :]
                pe.wait_ge(smp_in, 16 * 2 * DB)
                wait_copied(pe, 1, NB - 1, "S")
                wait_copied(pe, 1, NB - 1, "Y")
                for j in range(HP):
                    for b in range(DB):
                        last = pe.matmul(tok_of(bank[1][2], j, b), Sb[b][:, j, :], tok_of(m["aT"], j, b), start=True, stop=True)
                last.then_inc(smp_pe, 1)
                pe.wait_ge(smp_act, 1)
                wait_copied(pe, 0, SAMPLES, "AakT")
                wait_copied(pe, 0, SAMPLES, "Vt")
                for j in range(HP):
                    pe.matmul(bank[1][0][:, j, :], m["RH"][:, j, :], ident, start=True, stop=False)
                    last = pe.matmul(bank[1][0][:, j, :], m["AakT"][:, j, :], m["Vt"][:, j, :], start=False, stop=True)
                last.then_inc(smp_pe, 1)
                pe.wait_ge(smp_act, 2)
                wait_copied(pe, 0, SAMPLES, "X64t")
                for j in range(HP):
                    last = pe.matmul(bank[1][2][:, j, :], m["Xt"][:, j, :], m["Z"][:, j, :], start=True, stop=True)
                last.then_inc(smp_pe, 1)
                pe.wait_ge(smp_act, 3)
                wait_copied(pe, 0, SAMPLES, "AqkT")
                for j in range(HP):
                    pe.matmul(bank[1][1][:, j, :], m["U"][:, j, :], m["AqbT"][:, j, :], start=True, stop=False)
                    pe.matmul(bank[1][1][:, j, :], m["Vt"][:, j, :], m["AqkT"][:, j, :], start=False, stop=False)
                    for b in range(DB):
                        last = pe.matmul(tok_of(bank[1][1], j, b), Sb[b][:, j, :], tok_of(m["rT"], j, b), start=False, stop=(b == DB - 1))
                last.then_inc(smp_pe, 1)
                wait_copied(pe, 0, SAMPLES, "Kt")
                wait_copied(pe, 0, SAMPLES, "Z64")
                for b in range(DB):
                    pe.wait_ge(smp_dve, 4 * b + 2)
                    for j in range(HP):
                        pe.matmul(bank[0][b % NBANK][:, j, :], m["Bt"][:, j, :], M[1]["D2"][:, j, :], start=True, stop=False)
                        last = pe.matmul(bank[0][b % NBANK][:, j, :], m["Kt"][:, j, :], M[1]["Dt2"][:, j, :], start=False, stop=True)
                    last.then_inc(smp_pe, 1)
                finish(SAMPLES, 0)
                finish(SAMPLES, 1)


def rwkv_masks():
    import numpy as np
    i = np.arange(P)
    h, t = i // HD, i % HD
    head = h[:, None] == h[None, :]
    low, up = t[:, None] > t[None, :], t[:, None] < t[None, :]
    eq = t[:, None] == t[None, :]
    same = lambda n: head & (t[:, None] // n == t[None, :] // n)
    cross = lambda n: same(2 * n) & (t[:, None] // n > t[None, :] // n)
    ms = [head, same(16) & low, cross(16), cross(32), same(16) & up, head & up, head & (up | eq), head & eq,
          same(DS) & low, same(DS) & up, same(DS) & up, same(DS) & (up | eq), np.zeros((P, P), bool)]
    return np.stack(ms, 1).astype(np.float32)


def sample_rows():
    import numpy as np
    return (np.arange(P)[:, None] % HD // DS == np.arange(DB)[None]).astype(np.float32)


def chunk_starts():
    import numpy as np
    a = np.ones((P, 2, HP * TB), np.float32)
    a[:, 0, ::C] = 0
    a[:, 1, ::DS] = 0
    return a


NG_ = 32
GC = 16
NS = 64
L = P // GC
NJ = NG_ // 2
NBL = SEQ // L
NBS = DB
NBT = NBL + NBS
BI = 16
TWO_PI = 2 * math.pi
PI_A = 6.28125
PI_B = TWO_PI - PI_A
ROUND = 1.5 * 2 ** 23
BELOW_PI = 3.1415925


def state_space(nc, ins, outs, u):
    with ExitStack() as ctx:
        e = Env(nc, ctx, "ss")
        lr, li, dt = (e.sb(n, [P, NJ]) for n in ("lr", "li", "dt"))
        Br, Bi, Cr, Ci = (e.sb(n, [P, NJ, GC]) for n in ("Br", "Bi", "Cr", "Ci"))
        d = e.sb("d", [P, NG_])
        ident = e.sb("ident", [P, P])
        h0 = [e.sb(n, [P, NJ, NBS]) for n in ("h0r", "h0i")]
        wglu, bglu = e.sb("wglu", [P, KU, DSSM]), e.sb("bglu", [P, KU])
        small = {n: e.sb(n, [P, NJ]) for n in ("th", "mag", "k", "rs", "rc", "sin", "cos", "den", "nr", "fr", "fi", "x1", "x2")}
        Ap = [e.sb(n, [P, L + 1, NJ]) for n in ("Apr", "Api")]
        Qp = [e.sb(n, [P, BI + 1, NJ]) for n in ("Qpr", "Qpi")]
        Bb = [e.sb(n, [P, NJ, GC]) for n in ("Bbr", "Bbi")]
        CA = [e.sb(n, [P, NJ, L + 1, GC]) for n in ("CAr", "CAn")]
        RT = [e.sb(n, [P, NJ, P]) for n in ("RTr", "RTi")]
        Tm = e.sb("Tm", [P, NG_, P])
        U = e.sb("U", [P, NG_, NBT])
        H = [e.sb(n, [P, NJ, NBL + 1]) for n in ("Hr", "Hi")]
        HS = [e.sb(n, [P, NJ, NBS]) for n in ("HSr", "HSi")]
        rows = e.sb("rows", [P, NG_ * P])
        G = [e.sb(n, [P, NJ, BI]) for n in ("Gr", "Gi")]
        tmp = [e.sb(f"tmp{i}", [P, NJ, BI]) for i in range(4)]
        sg = e.sb("sg", [P, KU, TW])
        endp = [e.sb(n, [P, NJ]) for n in ("endr", "endi")]
        R = [U[:].rearrange("p g n -> p (g n)")[:, i * NJ * P:(i + 1) * NJ * P].rearrange("p (j s c) -> p j s c", s=L, c=GC) for i in range(2)]
        big = [H[i][:].rearrange("p j n -> p (j n)")[:, 0:NJ * (L + 1) * GC].rearrange("p (j t c) -> p j t c", t=L + 1, c=GC) for i in range(2)]
        Ks = rows[0:GC, :].rearrange("p (g x) -> p g x", x=P)
        dtmp = U[:].rearrange("p g n -> p (g n)")[:, 0:NG_ * P].rearrange("p (g x) -> p g x", x=P)
        bk = [e.ps(f"bk{i}", [P, 512]) for i in range(8)]

        par_in, zero, chain = e.sem("par_in"), e.sem("zero"), e.sem("chain")
        dt_ready, mag_ready, sc_ready = e.sem("dt_ready"), e.sem("mag_ready"), e.sem("sc_ready")
        arg_ready, red_ready = e.sem("arg_ready"), e.sem("red_ready")
        k_ready, r_ready = e.sem("k_ready"), e.sem("r_ready")
        k_mm, k_out, t_moved, t_ready = e.sem("k_mm"), e.sem("k_out"), e.sem("t_moved"), e.sem("t_ready")
        r_mm, r_out = e.sem("r_mm"), e.sem("r_out")
        u_mm, u_act, u_dve = e.sem("u_mm"), e.sem("u_act"), e.sem("u_dve")
        b_mm, b_act, b_dve = e.sem("b_mm"), e.sem("b_act"), e.sem("b_dve")
        h_ready, end_ready = e.sem("h_ready"), e.sem("end_ready")
        y_mm, y_out, x_mm, x_out = e.sem("y_mm"), e.sem("y_out"), e.sem("x_mm"), e.sem("x_out")
        g_mm, g_sig, g_out = e.sem("g_mm"), e.sem("g_sig"), e.sem("g_out")
        stored = e.sem("stored")
        NPAR = 16

        LOTS = [(0, P, 0), (P, P, P * L), (NBL, NBS, SEQ)]
        NK = NG_ // 4
        NR = 2 * NJ // 4
        UF, UG = KU * 2, NG_ // 4
        UL = UF + UG

        def groups(i):
            first = 8 * (i // 2) + i % 2
            return slice(first, first + 7, 2)

        with nc.Block() as block:
            @block.sync
            def _(sp):
                for dst, n in ((lr, "lam_re"), (li, "lam_im"), (dt, "log_dt"), (Br, "b_re"), (Bi, "b_im"), (Cr, "c_re"), (Ci, "c_im"),
                               (d, "ssm_d"), (ident, "ident"), (h0[0], "h0_re"), (h0[1], "h0_im"), (bglu, "b_glu")):
                    sp.dma_start(dst[:], ins[n]).then_inc(par_in, 16)
                for k in range(KU):
                    sp.dma_start(wglu[:, k, :], ins["w_glu"][k]).then_inc(par_in, 16)
                sp.wait_ge(k_out, NK)
                sp.wait_ge(zero, 3)
                for s in range(L):
                    sp.dma_start(Tm[s * GC:(s + 1) * GC, :, s * GC:P], Ks[:, :, 0:P - s * GC]).then_inc(t_moved, 16)
                sp.wait_ge(end_ready, 2)
                for i, n in enumerate(("re", "im")):
                    sp.dma_start(outs[f"ssm_{n}_p"], endp[i][:]).then_inc(stored, 16)
                    sp.dma_start(outs[f"ssm_{n}_s"], HS[i][:]).then_inc(stored, 16)
                sp.wait_ge(stored, 64)

            @block.gpsimd
            def _(pool):
                pool.memset(Tm[:], 0.0).then_inc(zero, 1)
                pool.memset(Ap[0][:, 0, :], 1.0).then_inc(zero, 1)
                pool.memset(Ap[1][:, 0, :], 0.0).then_inc(zero, 1)

            def u_copy(eng, lot, f, n, b0):
                i = lot * UL + f
                eng.wait_ge(u_mm, i + 1)
                src = bk[i % 8]
                if f < UF:
                    ct, half = f // 2, f % 2
                    dst = rows[0:n, :].rearrange("p (g s c) -> p g s c", s=L, c=GC)[:, 8 * ct:8 * ct + 8, 4 * half:4 * half + 4, :]
                    src = src[0:n, :].rearrange("p (s g c) -> p g s c", s=4, c=GC)
                else:
                    g = 4 * (f - UF)
                    dst = U[:, g:g + 4, b0:b0 + n]
                    src = src[:, 0:4 * n].rearrange("p (g n) -> p g n", g=4)
                if f % 2:
                    eng.tensor_copy(dst, src).then_inc(u_dve, 1)
                else:
                    eng.copy(dst, src).then_inc(u_act, 1)

            @block.scalar
            def _(act):
                act.wait_ge(par_in, 16 * NPAR)
                act.activation(dt[:], dt[:], ACT.Exp).then_inc(dt_ready, 1)
                act.wait_ge(mag_ready, 1)
                act.activation(small["mag"][:], small["mag"][:], ACT.Exp).then_inc(sc_ready, 1)
                act.wait_ge(arg_ready, 1)
                act.activation(small["sin"][:], small["rs"][:], ACT.Sin).then_inc(sc_ready, 1)
                act.activation(small["cos"][:], small["rc"][:], ACT.Sin).then_inc(sc_ready, 1)
                for i in range(NK):
                    act.wait_ge(k_mm, i + 1)
                    act.copy(Ks[:, groups(i), :], bk[i % 4][0:GC, :].rearrange("p (g x) -> p g x", x=P)).then_inc(k_out, 1)
                for i in range(NR):
                    act.wait_ge(r_mm, i + 1)
                    act.copy(RT[i // (NJ // 4)][:, 4 * (i % (NJ // 4)):4 * (i % (NJ // 4)) + 4, :],
                             bk[4 + i % 4][:].rearrange("p (j x) -> p j x", x=P)).then_inc(r_out, 1)
                act.wait_ge(t_moved, 16 * L)
                for lot, (b0, n, _) in enumerate(LOTS):
                    for f in range(0, UL, 2):
                        u_copy(act, lot, f, n, b0)
                for j in range(NJ):
                    act.wait_ge(b_mm, 2 * j + 1)
                    src = bk[(2 * j) % 8]
                    act.copy(H[0][:, j, 1:], src[:, 0:NBL])
                    act.copy(HS[0][:, j, :], src[:, NBL:NBT]).then_inc(b_act, 1)
                for lot, (b0, n, _) in enumerate(LOTS):
                    for q in range(UG):
                        i = lot * UG + q
                        act.wait_ge(y_mm, i + 1)
                        if q == 0 and lot:
                            act.wait_ge(x_mm, UF * lot)
                        out = rows[0:n, :].rearrange("p (t g c) -> p g t c", t=L, c=GC)[:, groups(q)]
                        act.activation(out, bk[i % 4][0:n, :].rearrange("p (g t c) -> p g t c", t=L, c=GC), ACT.Gelu_apprx_tanh).then_inc(y_out, 1)
                for n in range(NT):
                    for m in range(KU):
                        i = n * KU + m
                        act.wait_ge(g_mm, i + 1)
                        if m == 0 and n:
                            act.wait_ge(g_out, n)
                        act.activation(sg[:, m, :], bk[i % 4][:, 0:TW], ACT.Sigmoid, bias=bglu[:, m:m + 1]).then_inc(g_sig, 1)

            @block.vector
            def _(dve):
                count = [0]

                def link(ins):
                    count[0] += 1
                    ins.then_inc(chain, 1)
                    dve.wait_ge(chain, count[0])

                def tt(out, a, b, op):
                    link(dve.tensor_tensor(out, a, b, op))

                def ts(out, a, s1, s2, o1, o2=None):
                    link(dve.tensor_scalar(out, a, s1, s2, o1, *([o2] if o2 else [])))

                def cmul(out, a, b, t):
                    tt(t[0], a[0], b[0], ALU.mult)
                    tt(t[1], a[1], b[1], ALU.mult)
                    tt(t[2], a[0], b[1], ALU.mult)
                    tt(t[3], a[1], b[0], ALU.mult)
                    tt(out[0], t[0], t[1], ALU.subtract)
                    tt(out[1], t[2], t[3], ALU.add)

                s = {n: x[:] for n, x in small.items()}

                def reduced(out, x):
                    ts(s["k"], x, 1 / TWO_PI, ROUND, ALU.mult, ALU.add)
                    ts(s["k"], s["k"], -ROUND, None, ALU.add)
                    link(dve.scalar_tensor_tensor(out, s["k"], -PI_A, x, ALU.mult, ALU.add))
                    link(dve.scalar_tensor_tensor(out, s["k"], -PI_B, out, ALU.mult, ALU.add))
                    ts(out, out, BELOW_PI, -BELOW_PI, ALU.min, ALU.max)

                dve.wait_ge(par_in, 16 * NPAR)
                dve.wait_ge(dt_ready, 1)
                tt(s["th"], li[:], dt[:], ALU.mult)
                dve.tensor_tensor(s["mag"], lr[:], dt[:], ALU.mult).then_inc(mag_ready, 1)
                reduced(s["rs"], s["th"])
                ts(s["x1"], s["rs"], math.pi / 2, None, ALU.add)
                reduced(s["rc"], s["x1"])
                dve.sem_inc(arg_ready, 1)
                dve.wait_ge(sc_ready, 3)
                dve.wait_ge(zero, 3)
                tt(Ap[0][:, 1], s["mag"], s["cos"], ALU.mult)
                tt(Ap[1][:, 1], s["mag"], s["sin"], ALU.mult)
                tt(s["x1"], lr[:], lr[:], ALU.mult)
                tt(s["x2"], li[:], li[:], ALU.mult)
                tt(s["den"], s["x1"], s["x2"], ALU.add)
                link(dve.reciprocal(s["den"], s["den"]))
                ts(s["nr"], Ap[0][:, 1], -1.0, None, ALU.add)
                tt(s["x1"], s["nr"], lr[:], ALU.mult)
                tt(s["x2"], Ap[1][:, 1], li[:], ALU.mult)
                tt(s["fr"], s["x1"], s["x2"], ALU.add)
                tt(s["fr"], s["fr"], s["den"], ALU.mult)
                tt(s["x1"], Ap[1][:, 1], lr[:], ALU.mult)
                tt(s["x2"], s["nr"], li[:], ALU.mult)
                tt(s["fi"], s["x1"], s["x2"], ALU.subtract)
                tt(s["fi"], s["fi"], s["den"], ALU.mult)
                t4 = [x[:] for x in tmp]
                cmul([x[:] for x in Bb], [bcast(s["fr"], GC), bcast(s["fi"], GC)], [Br[:], Bi[:]], t4)

                def powers(X, top):
                    n = 1
                    while n < top:
                        w = min(n, top - n)
                        last = [x[:, n:n + 1, :].to_broadcast([P, w, NJ]) for x in X]
                        t = [x[:].rearrange("p j b -> p b j")[:, 0:w, :] for x in tmp]
                        cmul([x[:, n + 1:n + 1 + w, :] for x in X], [x[:, 1:1 + w, :] for x in X], last, t)
                        n += w

                powers(Ap, L)
                at_ = [x[:].rearrange("p t j -> p j t").unsqueeze(3).to_broadcast([P, NJ, L + 1, GC]) for x in Ap]
                c_ = [x[:].unsqueeze(2).to_broadcast([P, NJ, L + 1, GC]) for x in (Cr, Ci)]
                tt(big[0], at_[0], c_[0], ALU.mult)
                tt(big[1], at_[1], c_[1], ALU.mult)
                tt(CA[0][:], big[0], big[1], ALU.subtract)
                tt(big[0], at_[0], c_[1], ALU.mult)
                tt(big[1], at_[1], c_[0], ALU.mult)
                tt(CA[1][:], big[0], big[1], ALU.add)
                dve.tensor_scalar(CA[1][:], CA[1][:], -1.0, None, ALU.mult).then_inc(k_ready, 1)
                for q in range(L):
                    a = [bcast(x[:, L - 1 - q, :], GC) for x in Ap]
                    cmul([R[0][:, :, q, :], R[1][:, :, q, :]], a, [x[:] for x in Bb], t4)
                dve.sem_inc(r_ready, 1)
                for i in range(2):
                    link(dve.tensor_copy(Qp[i][:, 1, :], Ap[i][:, L, :]))
                powers(Qp, BI)
                dve.wait_ge(t_moved, 16 * L)
                dve.wait_ge(r_mm, NR)
                tt(dtmp, ident[:].unsqueeze(1).to_broadcast([P, NG_, P]), bcast(d[:], P), ALU.mult)
                link(dve.tensor_tensor(Tm[:], Tm[:], dtmp, ALU.add))
                dve.sem_inc(t_ready, 1)
                for lot, (b0, n, _) in enumerate(LOTS):
                    for f in range(1, UL, 2):
                        u_copy(dve, lot, f, n, b0)
                for i in range(2):
                    link(dve.memset(H[i][:, :, 0:1], 0.0))
                for j in range(NJ):
                    dve.wait_ge(b_mm, 2 * j + 2)
                    src = bk[(2 * j + 1) % 8]
                    dve.tensor_copy(H[1][:, j, 1:], src[:, 0:NBL])
                    dve.tensor_copy(HS[1][:, j, :], src[:, NBL:NBT]).then_inc(b_dve, 1)
                dve.wait_ge(b_act, NJ)
                dve.wait_ge(b_dve, NJ)

                def add_product(x, a, b, t):
                    tt(t[0], a[0], b[0], ALU.mult)
                    tt(t[1], a[1], b[1], ALU.mult)
                    tt(t[2], a[0], b[1], ALU.mult)
                    tt(t[3], a[1], b[0], ALU.mult)
                    tt(x[0], x[0], t[0], ALU.add)
                    tt(x[1], x[1], t[2], ALU.add)
                    tt(x[0], x[0], t[1], ALU.subtract)
                    tt(x[1], x[1], t[3], ALU.add)

                def run(i):
                    return [x[:, :, 1 + i:1 + i + BI * (BI - 1) + 1:BI] for x in H]

                a8 = [bcast(x[:, 1, :], BI) for x in Qp]
                for i in range(1, BI):
                    add_product(run(i), a8, run(i - 1), t4)
                ends = run(BI - 1)
                for i in range(2):
                    link(dve.memset(G[i][:, :, 0:1], 0.0))
                    link(dve.tensor_copy(G[i][:, :, 1:], ends[i][:, :, 0:BI - 1]))
                a128 = [x[:, BI, :] for x in Qp]
                tj = [x[:, :, 0] for x in tmp]
                for b in range(1, BI):
                    add_product([x[:, :, b] for x in G], a128, [x[:, :, b - 1] for x in G], tj)
                for i in range(BI):
                    add_product(run(i), [bcast(x[:, i + 1, :], BI) for x in Qp], [x[:] for x in G], t4)
                dve.sem_inc(h_ready, 1)
                a8s = [bcast(x[:, 1, :], NBS) for x in Qp]
                add_product([x[:] for x in HS], a8s, [x[:] for x in h0], [x[:, :, 0:NBS] for x in tmp])
                for i in range(2):
                    dve.tensor_copy(endp[i][:], H[i][:, :, NBL]).then_inc(end_ready, 1)
                for lot, (b0, n, t0) in enumerate(LOTS):
                    for f in range(UF):
                        i = lot * UF + f
                        ct, half = f // 2, f % 2
                        dve.wait_ge(x_mm, i + 1)
                        dst = u[:, ct, t0:t0 + n * L].rearrange("p (n t) -> p t n", t=L)[:, 4 * half:4 * half + 4, :]
                        dve.tensor_copy(dst, bk[4 + i % 4][:, 0:4 * n].rearrange("p (t n) -> p t n", t=4)).then_inc(x_out, 1)
                for n in range(NT):
                    dve.wait_ge(g_sig, KU * (n + 1))
                    dve.tensor_tensor(u[:, :, tok(n)], u[:, :, tok(n)], sg[:], ALU.mult).then_inc(g_out, 1)

            @block.tensor
            def _(pe):
                pe.wait_ge(par_in, 16 * NPAR)
                pe.wait_ge(k_ready, 1)
                for i in range(NK):
                    if i >= 4:
                        pe.wait_ge(k_out, i - 3)
                    for n4, g in enumerate(range(NG_)[groups(i)]):
                        j, h = g // 2, slice(NS * (g % 2), NS * (g % 2) + NS)
                        out = bk[i % 4][0:GC, n4 * P:(n4 + 1) * P]
                        for n in range(2):
                            last = pe.matmul(out, Bb[n][h, j, :], CA[n][h, j, 0:L, :], start=(n == 0), stop=(n == 1))
                    last.then_inc(k_mm, 1)
                pe.wait_ge(r_ready, 1)
                for i in range(NR):
                    if i >= 4:
                        pe.wait_ge(r_out, i - 3)
                    x, j0 = i // (NJ // 4), 4 * (i % (NJ // 4))
                    for j in range(j0, j0 + 4):
                        last = pe.transpose(bk[4 + i % 4][:, (j - j0) * P:(j - j0 + 1) * P], R[x][:, j].rearrange("p s c -> p (s c)"), ident[:])
                    last.then_inc(r_mm, 1)
                pe.wait_ge(k_out, NK)
                pe.wait_ge(r_out, NR)
                pe.wait_ge(t_ready, 1)
                for lot, (b0, n, t0) in enumerate(LOTS):
                    for f in range(UL):
                        i = lot * UL + f
                        if i >= 8:
                            pe.wait_ge(u_dve if f % 2 else u_act, (i - 8) // 2 + 1)
                        if f < UF:
                            ct, half = f // 2, f % 2
                            for k in range(4):
                                first = t0 + 4 * half + k
                                last = pe.transpose(bk[i % 8][0:n, k * P:(k + 1) * P], u[:, ct, first:first + L * (n - 1) + 1:L], ident[:])
                        else:
                            if f == UF:
                                pe.wait_ge(u_act, (lot * UL + UF) // 2)
                                pe.wait_ge(u_dve, (lot * UL + UF) // 2)
                            for k in range(4):
                                g = 4 * (f - UF) + k
                                last = pe.transpose(bk[i % 8][:, k * n:(k + 1) * n], rows[0:n, g * P:(g + 1) * P], ident[0:n, 0:n])
                        last.then_inc(u_mm, 1)
                pe.wait_ge(u_act, len(LOTS) * UL // 2)
                pe.wait_ge(u_dve, len(LOTS) * UL // 2)
                for i in range(2 * NJ):
                    j, x = i // 2, i % 2
                    if i >= 8:
                        pe.wait_ge((b_act, b_dve)[x], j - 3)
                    for h in range(2):
                        last = pe.matmul(bk[i % 8][NS * h:NS * h + NS, 0:NBT], RT[x][:, j, NS * h:NS * h + NS], U[:, 2 * j + h, :], start=True, stop=True)
                    last.then_inc(b_mm, 1)
                pe.wait_ge(h_ready, 1)
                for lot, (b0, n, t0) in enumerate(LOTS):
                    for q in range(UG):
                        i = lot * UG + q
                        if i >= 4:
                            pe.wait_ge(y_out, i - 3)
                        for n4, g in enumerate(range(NG_)[groups(q)]):
                            j, h = g // 2, slice(NS * (g % 2), NS * (g % 2) + NS)
                            out = bk[i % 4][0:n, n4 * P:(n4 + 1) * P]
                            pe.matmul(out, U[:, g, b0:b0 + n], Tm[:, g, :], start=True, stop=False)
                            for x in range(2):
                                state = h0[x][h, j, :] if b0 == NBL else H[x][h, j, b0:b0 + n]
                                last = pe.matmul(out, state, CA[x][h, j, 1:, :], start=False, stop=(x == 1))
                        last.then_inc(y_mm, 1)
                    pe.wait_ge(y_out, (lot + 1) * UG)
                    for f in range(UF):
                        i = lot * UF + f
                        ct, half = f // 2, f % 2
                        if i >= 4:
                            pe.wait_ge(x_out, i - 3)
                        for k in range(4):
                            c = (4 * half + k) * DSSM + ct * P
                            last = pe.transpose(bk[4 + i % 4][:, k * n:(k + 1) * n], rows[0:n, c:c + P], ident[0:n, 0:n])
                        last.then_inc(x_mm, 1)
                pe.wait_ge(x_out, UF * len(LOTS))
                for n in range(NT):
                    for m in range(KU):
                        i = n * KU + m
                        if i >= 4:
                            pe.wait_ge(g_sig, i - 3)
                        for k in range(KU):
                            last = pe.matmul(bk[i % 4][:, 0:TW], wglu[:, k, m * P:(m + 1) * P], u[:, k, tok(n)], start=(k == 0), stop=(k == KU - 1))
                        last.then_inc(g_mm, 1)


class Tiles:

    def __init__(self, parts):
        self.parts = parts

    def __getitem__(self, at_):
        p, k, t = at_
        return self.parts[k // KU][p, k % KU, t]


def hybrid_layer(nc, ins, outs, scratch):
    with ExitStack() as ctx:
        u = ctx.enter_context(nc.sbuf_tensor("mix_a", [P, KU, T], F32))
        project_in(nc, ins, scratch, u)
        state_space(nc, ins, outs, u)
        yb = ctx.enter_context(nc.sbuf_tensor("mix_b", [P, KR, T], F32))
        delta_rule(nc, ins, outs, scratch, yb)
        hT = ctx.enter_context(nc.sbuf_tensor("h", [P, KD, T], F32))
        mix_out(nc, ins, (u, yb), hT, Tiles((u, yb)))
        conv_ffn(nc, ins, outs, hT, Tiles((u, yb)))
        gated_embedding(nc, ins, outs, hT, (u, yb))


def kernel(**inputs):
    import numpy as np
    import concourse.bacc as _bacc
    from concourse import mybir as _mybir
    from concourse.bass_utils import run_bass_kernel_spmd as _run

    a = {k: np.asarray(v) for k, v in inputs.items()}

    def tiles(rows):
        return rows.T.reshape(-1, P, rows.shape[0]).transpose(1, 0, 2)

    def columns(v):
        return v.reshape(-1, P).T

    def states(v):
        v = v.reshape(NJ, 2, NS, -1).transpose(1, 2, 0, 3).reshape(P, NJ, -1)
        return v[:, :, 0] if v.shape[2] == 1 else v

    def both(prompt, sample):
        return tiles(np.concatenate([prompt.reshape(SEQ, -1), sample.reshape(TS_ALL, -1)], 0))

    TS_ALL = DB * DS
    w_up = a["w_up"][0].reshape(KD, P, 2 * FF).transpose(1, 0, 2)
    arrays = {
        "xT": both(a["x_prompt"], a["x_sample"]),
        "pT": both(a["p_prompt"], a["p_sample"]),
        "norm1_g": columns(a["norm1_g"]), "norm2_g": columns(a["norm2_g"]), "final_g": columns(a["final_g"]),
        "w_in": a["w_in"].reshape(KD, P, -1), "w_out": a["w_out"].reshape(KD, P, D),
        "w_val": w_up[:, :, 0:FF], "w_gate": w_up[:, :, FF:], "w_down": a["w_down"].reshape(KF, P, D),
        "conv_wb": np.concatenate([a["conv_w"][0], a["conv_b"]], 0).reshape(CONV + 1, KF, P).transpose(2, 1, 0),
        "state_conv": a["state_conv"].reshape(DB, 2, KF, P).transpose(3, 2, 0, 1),
        "w_pg": a["w_pg"].reshape(KD, P, D), "w_ple": a["w_ple"].reshape(KP, P, D),
        "w2a2": np.concatenate([a["rwkv_w2"][0], a["rwkv_a2"][0]], 0), "g2": a["rwkv_g2"][0], "mu": columns(a["shift_mu"]),
        "masks": rwkv_masks(), "seg": chunk_starts(), "rows8": sample_rows(),
        "state_rwkv": a["state_rwkv"].reshape(DB, HP, 2, HD, HD).transpose(2, 4, 0, 1, 3).reshape(P, DB, HP, HD),
        "state_shift": a["state_shift"].reshape(DB, ZT, P).transpose(2, 1, 0),
        "lam_re": states(a["ssm_lam_re"]), "lam_im": states(a["ssm_lam_im"]),
        "log_dt": states(np.repeat(a["ssm_log_dt"][0][:, None], NS, 1)),
        "b_re": states(a["ssm_b_re"]), "b_im": states(a["ssm_b_im"]),
        "c_re": states(a["ssm_c_re"][0].transpose(0, 2, 1)), "c_im": states(a["ssm_c_im"][0].transpose(0, 2, 1)),
        "ssm_d": np.tile(a["ssm_d"].reshape(NG_, GC).T, (L, 1)), "ident": np.eye(P, dtype=np.float32),
        "h0_re": states(a["state_ssm_re"][0].transpose(1, 2, 0)), "h0_im": states(a["state_ssm_im"][0].transpose(1, 2, 0)),
        "w_glu": a["ssm_w_glu"].reshape(KU, P, DSSM), "b_glu": columns(a["ssm_b_glu"]),
    }
    for n in ("w0", "a0", "k_k", "k_a", "r_k", "lnx_g", "lnx_b"):
        arrays[n] = columns(a["rwkv_" + n])
    arrays = {k: np.ascontiguousarray(v) for k, v in arrays.items()}
    shapes = {
        "yT": (P, KD, T), "ssm_re_p": (P, NJ), "ssm_im_p": (P, NJ), "ssm_re_s": (P, NJ, DB), "ssm_im_s": (P, NJ, DB),
        "rwkv_p": (P, HP, HD), "rwkv_s": (P, DB, HP, HD), "shift": (P, ZT, 1 + DB), "conv_p": (P, KF, 2), "conv_s": (P, KF, DB, 2),
    }
    nc = _bacc.Bacc("TRN2", target_bir_lowering=False, num_devices=1)
    ins = {k: nc.dram_tensor(f"in_{k}", v.shape, _mybir.dt.from_np(v.dtype), kind="ExternalInput").ap() for k, v in arrays.items()}
    outs = {k: nc.dram_tensor(f"out_{k}", v, F32, kind="ExternalOutput").ap() for k, v in shapes.items()}
    scratch = {"zr": nc.dram_tensor("scratch_zr", (ZT, P, T), F32, kind="Internal").ap()}
    hybrid_layer(nc, ins, outs, scratch)
    r = _run(nc, [{f"in_{k}": v for k, v in arrays.items()}], core_ids=[0]).results[0]
    o = {k: r[f"out_{k}"] for k in shapes}

    def from_states(v):
        return v.reshape(2, NS, NJ, -1).transpose(3, 2, 0, 1).reshape(1, -1, NG_, NS)

    y = o["yT"].transpose(2, 1, 0).reshape(T, D)
    shift = o["shift"].transpose(2, 1, 0).reshape(1 + DB, -1)
    return (
        y[None, 0:SEQ], y[SEQ:].reshape(DB, DS, D),
        from_states(o["ssm_re_p"]), from_states(o["ssm_im_p"]),
        o["rwkv_p"].reshape(2, HD, HP, HD).transpose(2, 0, 3, 1).reshape(1, 1, 2 * HP, HD, HD),
        shift[None, 0:1], o["conv_p"].transpose(2, 1, 0).reshape(1, 1, 2, FF),
        from_states(o["ssm_re_s"]), from_states(o["ssm_im_s"]),
        o["rwkv_s"].reshape(2, HD, DB, HP, HD).transpose(2, 3, 0, 4, 1).reshape(1, DB, 2 * HP, HD, HD),
        shift[None, 1:], o["conv_s"].transpose(2, 3, 1, 0).reshape(1, DB, 2, FF),
    )
```

```python
import math
from contextlib import ExitStack

import concourse.bass as bass
from concourse import mybir

P = 128
F32 = mybir.dt.float32
F32R = mybir.dt.float32r
I32 = mybir.dt.int32
ALU = mybir.AluOpType
ACT = mybir.ActivationFunctionType
AX = mybir.AxisListType

D = 1024
KD = D // P
SEQ, DB, DS = 2048, 8, 8
T = SEQ + DB * DS
TW = 352
NT = T // TW
DSSM, DRW = 512, 512
KU, KR = DSSM // P, DRW // P
ZT = 14
KIN = KU + ZT
FF = 2816
KF = FF // P
PLE = 256
KP = PLE // P
CONV = 3
RMS_EPS, GN_EPS, L2_EPS = 1e-6, 64e-5, 1e-12
LASTP = SEQ - (NT - 1) * TW


class Env:

    def __init__(self, nc, ctx, tag):
        self.nc, self.ctx, self.tag = nc, ctx, tag

    def sb(self, name, shape, dt=F32):
        return self.ctx.enter_context(self.nc.sbuf_tensor(f"{self.tag}_{name}", shape, dt))

    def ps(self, name, shape):
        return self.ctx.enter_context(self.nc.psum_tensor(f"{self.tag}_{name}", shape, F32))

    def sem(self, name):
        return self.ctx.enter_context(self.nc.semaphore(f"{self.tag}_{name}"))


def bcast(ap, n):
    p, a = ap.shape
    return ap.unsqueeze(2).to_broadcast([p, a, n])


def tok(n):
    return slice(n * TW, (n + 1) * TW)


def project_in(nc, ins, scratch, u):
    with ExitStack() as ctx:
        e = Env(nc, ctx, "in")
        WM = 3
        w = e.sb("w", [P, KD, KIN * P])
        xn = e.sb("xn", [P, KD, T])
        sq = e.sb("sq", [P, KD, TW])
        ssum = e.sb("ssum", [P, TW])
        rms = e.sb("rms", [P, TW])
        zout = e.sb("zout", [P, ZT, TW])
        g = e.sb("g", [P, KD])
        eps = e.sb("eps", [P, 1])
        ones = e.sb("ones", [P, P])
        pn = e.ps("pn", [P, 512])
        pp = [e.ps(f"pp{i}", [P, 512]) for i in range(6)]
        x_in = [e.sem(f"x_in{n}") for n in range(NT)]
        w_in = [e.sem(f"w_in{j}") for j in range(KIN // WM)]
        g_in = e.sem("g_in")
        const_ready = e.sem("const_ready")
        sq_ready, ssum_ready, ms_ready = e.sem("sq_ready"), e.sem("ssum_ready"), e.sem("ms_ready")
        rms_ready, inv_ready, xn_ready = e.sem("rms_ready"), e.sem("inv_ready"), e.sem("xn_ready")
        proj_ready = e.sem("proj_ready")
        act_out, dve_out = e.sem("act_out"), e.sem("dve_out")
        z_stored = [e.sem(f"z_stored{h}") for h in range(2)]
        HZ = ZT // 2
        SQUARE_AT, SUM_AT, MEAN_AT, ROOT_AT, INVERSE_AT = 2, 5, 8, 10, 11
        DVE_M = [m for m in range(KIN) if m % 2]
        ACT_M = [m for m in range(KIN) if m % 2 == 0]

        def at(n, per, c):
            return n * per + c

        def cols(n):
            return bass.ds(n * TW, TW)

        def tiles(eng, body):
            body(0, True)
            for n in range(2, NT):
                eng.wait_ge(x_in[n], 16)
            with eng.Fori(1, NT - 1) as n:
                body(n, True)
            body(NT - 1, False)

        with nc.Block() as block:
            @block.sync
            def _(sp):
                for n in range(NT):
                    sp.dma_start(xn[:, :, tok(n)], ins["xT"][:, :, tok(n)]).then_inc(x_in[n], 16)
                    if n == 0:
                        sp.dma_start(g[:], ins["norm1_g"]).then_inc(g_in, 16)
                        src = ins["w_in"].rearrange("k p c -> p k c")
                        for j in range(KIN // WM):
                            cols = slice(j * WM * P, (j + 1) * WM * P)
                            sp.dma_start(w[:, :, cols], src[:, :, cols]).then_inc(w_in[j], 16)
                dst = scratch["zr"].rearrange("z p t -> p z t")
                for n in range(NT):
                    for h in range(2):
                        last = KU + (h + 1) * HZ
                        sp.wait_ge(act_out, n * len(ACT_M) + sum(m < last for m in ACT_M))
                        sp.wait_ge(dve_out, n * len(DVE_M) + sum(m < last for m in DVE_M))
                        sp.dma_start(dst[:, h * HZ:(h + 1) * HZ, tok(n)],
                                     zout[:, h * HZ:(h + 1) * HZ, :]).then_inc(z_stored[h], 16)
                for h in range(2):
                    sp.wait_ge(z_stored[h], 16 * (NT + 1))

            @block.gpsimd
            def _(pool):
                pool.memset(ones[:], 1.0 / D).then_inc(const_ready, 1)
                pool.memset(eps[:], RMS_EPS).then_inc(const_ready, 1)
                for h in range(2):
                    pool.sem_inc(z_stored[h], 16)

            def copy_out(eng, n, m, out_sem):
                eng.wait_ge(proj_ready, n * KIN + m + 1)
                if m < KU:
                    dst = u[:, m, bass.ds(n * TW, TW)]
                else:
                    if (m - KU) % HZ < 2:
                        eng.wait_ge(z_stored[(m - KU) // HZ], 16 * (n + 1))
                    dst = zout[:, m - KU, :]
                src = pp[m % 6][:, 0:TW]
                if eng is nc.scalar or eng.engine == nc.scalar.engine:
                    eng.copy(dst, src).then_inc(out_sem, 1)
                else:
                    eng.tensor_copy(dst, src).then_inc(out_sem, 1)

            @block.scalar
            def _(act):
                act.wait_ge(const_ready, 2)

                def square(n):
                    if isinstance(n, int) and n < 2:
                        act.wait_ge(x_in[n], 16)
                    if not (isinstance(n, int) and n == 0):
                        act.wait_ge(ssum_ready, n)
                    act.square(sq[:], xn[:, :, cols(n)]).then_inc(sq_ready, 1)

                def root(n):
                    act.wait_ge(ms_ready, n + 1)
                    if not (isinstance(n, int) and n == 0):
                        act.wait_ge(xn_ready, at(n, KD, 0))
                    act.activation(rms[:], pn[:, 0:TW], ACT.Sqrt, bias=eps[:, 0:1]).then_inc(rms_ready, 1)

                def tile(n, more):
                    for m in ACT_M:
                        copy_out(act, n, m, act_out)
                        if more and m == SQUARE_AT:
                            square(n + 1)
                        if more and m == ROOT_AT:
                            root(n + 1)

                square(0)
                root(0)
                tiles(act, tile)

            @block.vector
            def _(dve):
                dve.wait_ge(g_in, 16)

                def norm_sum(n):
                    dve.wait_ge(sq_ready, n + 1)
                    if not (isinstance(n, int) and n == 0):
                        dve.wait_ge(ms_ready, n)
                    dve.tensor_reduce(ssum[:], sq[:].rearrange("p k t -> p t k"), AX.X, ALU.add).then_inc(ssum_ready, 1)

                def inverse(n):
                    dve.wait_ge(rms_ready, n + 1)
                    dve.reciprocal(rms[:], rms[:]).then_inc(inv_ready, 1)

                def norm_apply(n, ks):
                    dve.wait_ge(inv_ready, n + 1)
                    for k in ks:
                        xk = xn[:, k, cols(n)]
                        dve.scalar_tensor_tensor(xk, xk, g[:, k:k + 1], rms[:], ALU.mult, ALU.mult).then_inc(xn_ready, 1)

                def tile(n, more):
                    for m in DVE_M:
                        copy_out(dve, n, m, dve_out)
                        if not more:
                            continue
                        if m == SUM_AT:
                            norm_sum(n + 1)
                        if m == INVERSE_AT:
                            inverse(n + 1)
                        if m > INVERSE_AT:
                            i = (m - INVERSE_AT) // 2 - 1
                            norm_apply(n + 1, range(4 * i, min(4 * i + 4, KD)))

                norm_sum(0)
                inverse(0)
                norm_apply(0, range(KD))
                tiles(dve, tile)

            @block.tensor
            def _(pe):
                pe.wait_ge(const_ready, 2)

                def mean_square(n):
                    pe.wait_ge(ssum_ready, n + 1)
                    if not (isinstance(n, int) and n == 0):
                        pe.wait_ge(rms_ready, n)
                    pe.matmul(pn[:, 0:TW], ones[:], ssum[:], start=True, stop=True).then_inc(ms_ready, 1)

                def tile(n, more):
                    first = isinstance(n, int) and n == 0
                    for m in range(KIN):
                        back = len(pp)
                        if not first or m >= back:
                            q, r = (n, m - back) if m >= back else (n - 1, m - back + KIN)
                            sem, lot = (act_out, ACT_M) if r in ACT_M else (dve_out, DVE_M)
                            pe.wait_ge(sem, q * len(lot) + lot.index(r) + 1)
                        if first and m % WM == 0:
                            pe.wait_ge(w_in[m // WM], 16)
                        for k in range(KD):
                            if m == 0:
                                pe.wait_ge(xn_ready, at(n, KD, k + 1))
                            mm = pe.matmul(pp[m % back][:, 0:TW], w[:, k, m * P:(m + 1) * P], xn[:, k, cols(n)],
                                           start=(k == 0), stop=(k == KD - 1))
                        mm.then_inc(proj_ready, 1)
                        if more and m == MEAN_AT:
                            mean_square(n + 1)

                mean_square(0)
                tiles(pe, tile)


def mix_out(nc, ins, y, hT, rstd):
    with ExitStack() as ctx:
        e = Env(nc, ctx, "mo")
        w = e.sb("w", [P, KD, D])
        sq = e.sb("sq", [P, KD, TW])
        ssum = e.sb("ssum", [P, TW])
        rms = e.sb("rms", [P, TW])
        eps = e.sb("eps", [P, 1])
        ones = e.sb("ones", [P, P])
        pn = [e.ps(f"pn{i}", [P, 512]) for i in range(2)]
        pp = [e.ps(f"pp{i}", [P, 512]) for i in range(6)]
        x_in = [e.sem(f"x_in{n}") for n in range(NT)]
        w_in = [e.sem(f"w_in{k}") for k in range(KD // 2)]
        const_ready = e.sem("const_ready")
        out_ready, h_ready = e.sem("out_ready"), e.sem("h_ready")
        sq_ready, ssum_ready, ms_ready = e.sem("sq_ready"), e.sem("ssum_ready"), e.sem("ms_ready")
        rms_ready, inv_ready = e.sem("rms_ready"), e.sem("inv_ready")

        with nc.Block() as block:
            @block.sync
            def _(sp):
                for k in range(KD):
                    if k % 2 == 0:
                        sp.dma_start(w[:, k:k + 2, :], ins["w_out"][k:k + 2].rearrange("k p d -> p k d")).then_inc(w_in[k // 2], 16)
                    if k < NT:
                        sp.dma_start(hT[:, :, tok(k)], ins["xT"][:, :, tok(k)]).then_inc(x_in[k], 16)

            @block.gpsimd
            def _(pool):
                pool.memset(ones[:], 1.0 / D).then_inc(const_ready, 1)
                pool.memset(eps[:], RMS_EPS).then_inc(const_ready, 1)

            @block.scalar
            def _(act):
                act.wait_ge(const_ready, 2)
                for n in range(NT):
                    act.wait_ge(h_ready, KD * (n + 1))
                    if n:
                        act.wait_ge(ssum_ready, n)
                    act.square(sq[:], hT[:, :, tok(n)]).then_inc(sq_ready, 1)
                    act.wait_ge(ms_ready, n + 1)
                    if n:
                        act.wait_ge(inv_ready, n)
                    act.activation(rms[:], pn[n % 2][:, 0:TW], ACT.Sqrt, bias=eps[:, 0:1]).then_inc(rms_ready, 1)

            @block.vector
            def _(dve):
                def residual(n):
                    dve.wait_ge(x_in[n], 16)
                    for m in range(KD):
                        i = n * KD + m
                        dve.wait_ge(out_ready, i + 1)
                        hm = hT[:, m, tok(n)]
                        dve.tensor_tensor(hm, pp[i % 6][:, 0:TW], hm, ALU.add).then_inc(h_ready, 1)

                def norm_sum(n):
                    dve.wait_ge(sq_ready, n + 1)
                    if n:
                        dve.wait_ge(ms_ready, n)
                    dve.tensor_reduce(ssum[:], sq[:].rearrange("p k t -> p t k"), AX.X, ALU.add).then_inc(ssum_ready, 1)

                def norm_apply(n):
                    dve.wait_ge(rms_ready, n + 1)
                    dve.reciprocal(rstd[:, tok(n)], rms[:]).then_inc(inv_ready, 1)

                for n in range(NT):
                    residual(n)
                    norm_sum(n)
                    norm_apply(n)

            @block.tensor
            def _(pe):
                pe.wait_ge(const_ready, 2)

                def mean_square(n):
                    pe.wait_ge(ssum_ready, n + 1)
                    if n >= 2:
                        pe.wait_ge(rms_ready, n - 1)
                    pe.matmul(pn[n % 2][:, 0:TW], ones[:], ssum[:], start=True, stop=True).then_inc(ms_ready, 1)

                for n in range(NT):
                    for m in range(KD):
                        i = n * KD + m
                        if i >= 6:
                            pe.wait_ge(h_ready, i - 5)
                        for k in range(KD):
                            if i == 0 and k % 2 == 0:
                                pe.wait_ge(w_in[k // 2], 16)
                            mm = pe.matmul(pp[i % 6][:, 0:TW], w[:, k, m * P:(m + 1) * P], y[k // KU][:, k % KU, tok(n)],
                                           start=(k == 0), stop=(k == KD - 1))
                        mm.then_inc(out_ready, 1)
                        if m == 4 and n:
                            mean_square(n - 1)
                mean_square(NT - 1)


def wait_count(eng, sem, turn, per, c):
    if isinstance(turn, int):
        if turn * per + c > 0:
            eng.wait_ge(sem, turn * per + c)
    else:
        eng.wait_ge(sem, turn * per + c)


def conv_ffn(nc, ins, outs, hT, rstd):
    G = 2
    NG = KF // G
    THIRDS = 3
    NS = NT // THIRDS
    TT = NS * TW
    GB = DS + 2
    NF = G * NS
    ND = NS * KD
    DOWN_AT = [1, 2]
    NX = NS * KD
    with ExitStack() as ctx:
        e = Env(nc, ctx, "ff")

        def both(name, shape):
            return e.sb(name + "_hi", shape, F32R), e.sb(name + "_lo", shape, F32R)

        wg = [both(f"wg{q}", [P, KD, P]) for q in range(G)]
        wv = [both(f"wv{q}", [P, KD, P]) for q in range(G)]
        wd = [both(f"wd{q}", [P, D]) for q in range(G)]
        raw = [e.sb(f"raw{i}", [P, KD, P]) for i in range(2)]
        xn = both("xn", [P, KD, TT])
        f = both("f", [P, G, TT])
        x = e.sb("x", [P, 2, TW])
        fr = e.sb("fr", [P, 2, TW])
        g2 = e.sb("g2", [P, KD])
        gp = e.sb("gp", [P, 2 + TT])
        gs = e.sb("gs", [P, DB, GB])
        cv = e.sb("cv", [P, 2, TW])
        sg = e.sb("sg", [P, 2, TW])
        cw = e.sb("cw", [P, KF, 4])
        taps = e.sb("taps", [P, G, 4])
        st = e.sb("st", [P, KF, DB, 2])
        carry = e.sb("carry", [P, KF, 2])
        keep_s = e.sb("keep_s", [P, KF, DB, 2])
        pg = [e.ps(f"pg{i}", [P, 512]) for i in range(2)]
        pv = [e.ps(f"pv{i}", [P, 512]) for i in range(2)]
        pd = [e.ps(f"pd{i}", [P, 512]) for i in range(4)]
        raw_in = [e.sem(f"raw_in{i}") for i in range(2)]
        par_in = e.sem("par_in")
        zero_ready = e.sem("zero_ready")
        w_hi, w_lo = e.sem("w_hi"), e.sem("w_lo")
        x_ready, x_hi, x_lo = e.sem("x_ready"), e.sem("x_hi"), e.sem("x_lo")
        gate_mm, val_mm, down_mm = e.sem("gate_mm"), e.sem("val_mm"), e.sem("down_mm")
        gate_out = e.sem("gate_out")
        taps_ready, carried, st_put = e.sem("taps_ready"), e.sem("carried"), e.sem("st_put")
        tap0, tap1, conv_ready = e.sem("tap0"), e.sem("tap1"), e.sem("conv_ready")
        silu_ready, f_ready, f_hi, f_lo = e.sem("silu_ready"), e.sem("f_ready"), e.sem("f_hi"), e.sem("f_lo")
        h_ready = e.sem("h_ready")
        kept, stored = e.sem("kept"), e.sem("stored")

        WEIGHTS = [wg[0], wv[0], wg[1], wv[1], wd[0], wd[1]]
        NW = len(WEIGHTS)

        def three(l, r):
            return [(l[0], r[0]), (l[0], r[1]), (l[1], r[0])]

        def thirds(eng, body):
            for s in range(THIRDS):
                body(s, s * NG, 0, False)
                with eng.Fori(1, NG - 1) as g:
                    body(s, g + s * NG, g, False)
                body(s, (s + 1) * NG - 1, NG - 1, True)

        with nc.Block() as block:
            @block.sync
            def _(sp):
                sp.dma_start(g2[:], ins["norm2_g"]).then_inc(par_in, 16)
                sp.dma_start(cw[:], ins["conv_wb"]).then_inc(par_in, 16)
                sp.dma_start(st[:], ins["state_conv"]).then_inc(par_in, 16)
                for t in range(THIRDS * NG):
                    for j in range(NW):
                        ff = G * (t % NG) + (j // 2 if j < 2 * G else j - 2 * G)
                        if NW * t + j >= 2:
                            sp.wait_ge(w_lo, NW * t + j - 1)
                        src = ins["w_down"][ff].rearrange("p (k t) -> p k t", t=P) if j >= 2 * G else ins[("w_gate", "w_val")[j % 2]][:, :, ff * P:(ff + 1) * P]
                        sp.dma_start(raw[j % 2][:], src).then_inc(raw_in[j % 2], 16)
                sp.wait_ge(kept, THIRDS * KF)
                sp.dma_start(outs["conv_p"], carry[:]).then_inc(stored, 16)
                sp.dma_start(outs["conv_s"], keep_s[:]).then_inc(stored, 16)
                sp.wait_ge(stored, 32)

            @block.gpsimd
            def _(pool):
                pool.memset(gp[:, 0:2], 0.0).then_inc(zero_ready, 1)

            @block.scalar
            def _(act):
                act.wait_ge(zero_ready, 1)

                def weights_hi(t, j):
                    wait_count(act, raw_in[j % 2], t, 16 * NW // 2, 16 * (j // 2 + 1))
                    if j < 2 * G:
                        wait_count(act, (gate_mm, val_mm)[j % 2], t, NF, (j // 2 + 1) * NS - NF)
                    else:
                        wait_count(act, down_mm, t, ND, 0)
                    out = WEIGHTS[j][0][:]
                    act.copy(out if j < 2 * G else out.rearrange("p (k t) -> p k t", t=P), raw[j % 2][:]).then_inc(w_hi, 1)

                def rows_hi(s, j):
                    n, k = j // KD, j % KD
                    act.wait_ge(x_ready, NX * s + j + 1)
                    act.copy(xn[0][:, k, tok(n)], x[:, j % 2, :]).then_inc(x_hi, 1)

                def turn(s, t, g, last):
                    def f_part(i):
                        wait_count(act, f_ready, t, NF, i + 1)
                        act.copy(f[0][:, i // NS, tok(i % NS)], fr[:, i % 2, :]).then_inc(f_hi, 1)

                    for i in range(NF):
                        n, b = i % NS, i % 2
                        wait_count(act, gate_mm, t, NF, i + 1)
                        wait_count(act, conv_ready, t, NF, i // NS * NS)
                        if s < THIRDS - 1 or n < NS - 1:
                            act.copy(gp[:, 2 + n * TW:2 + (n + 1) * TW], pg[b][:, 0:TW]).then_inc(gate_out, 1)
                        else:
                            act.copy(gp[:, 2 + n * TW:2 + n * TW + LASTP], pg[b][:, 0:LASTP])
                            act.copy(gs[:, :, 2:GB], pg[b][:, LASTP:TW].rearrange("p (b s) -> p b s", b=DB)).then_inc(gate_out, 1)
                        if i:
                            f_part(i - 1)
                        wait_count(act, conv_ready, t, NF, i + 1)
                        wait_count(act, f_ready, t, NF, i - 1)
                        act.activation(sg[:, b, :], cv[:, b, :], ACT.Silu).then_inc(silu_ready, 1)
                        if i in DOWN_AT:
                            weights_hi(t, 2 * G + DOWN_AT.index(i))
                    f_part(NF - 1)
                    if last and s == THIRDS - 1:
                        return
                    if last:
                        for j in range(NX):
                            rows_hi(s + 1, j)
                            if j % 4 == 3:
                                weights_hi(t + 1, j // 4)
                    else:
                        for j in range(2 * G):
                            weights_hi(t + 1, j)

                for j in range(NX):
                    rows_hi(0, j)
                    if j % 2 and j // 2 < 2 * G:
                        weights_hi(0, j // 2)
                thirds(act, turn)

            @block.vector
            def _(dve):
                dve.wait_ge(par_in, 48)

                def weights_lo(t, j):
                    wait_count(dve, w_hi, t, NW, j + 1)
                    hi, lo = [w[:] if j < 2 * G else w[:].rearrange("p (k t) -> p k t", t=P) for w in WEIGHTS[j]]
                    dve.tensor_tensor(lo, raw[j % 2][:], hi.bitcast(F32), ALU.subtract).then_inc(w_lo, 1)

                def rows(s, j):
                    n, k = j // KD, j % KD
                    at_ = tok(s * NS + n)
                    if NX * s + j >= 2:
                        dve.wait_ge(x_lo, NX * s + j - 1)
                    dve.scalar_tensor_tensor(x[:, j % 2, :], hT[:, k, at_], g2[:, k:k + 1], rstd[:, at_], ALU.mult, ALU.mult).then_inc(x_ready, 1)

                def rows_lo(s, j):
                    n, k = j // KD, j % KD
                    dve.wait_ge(x_hi, NX * s + j + 1)
                    dve.tensor_tensor(xn[1][:, k, tok(n)], x[:, j % 2, :], xn[0][:, k, tok(n)].bitcast(F32), ALU.subtract).then_inc(x_lo, 1)

                def turn(s, t, g, last):
                    for q in range(G):
                        ff = g * G + q
                        dve.tensor_copy(taps[:, q, :], cw[:, bass.ds(ff, 1), :].rearrange("p a c -> p (a c)")).then_inc(taps_ready, 1)

                    def f_part(i):
                        at_ = (slice(None), i // NS, tok(i % NS))
                        wait_count(dve, f_hi, t, NF, i + 1)
                        dve.tensor_tensor(f[1][at_], fr[:, i % 2, :], f[0][at_].bitcast(F32), ALU.subtract).then_inc(f_lo, 1)

                    for i in range(NF):
                        q, n, b = i // NS, i % NS, i % 2
                        tap = [taps[:, q, j:j + 1] for j in range(4)]
                        ff = bass.ds(g * G + q, 1)
                        if n == 0 and s:
                            dve.tensor_copy(gp[:, 0:2], carry[:, ff, :].rearrange("p a s -> p (a s)")).then_inc(carried, 1)
                            wait_count(dve, carried, t - NG, G, q + 1)
                        smp = s == THIRDS - 1 and n == NS - 1
                        if smp:
                            dve.tensor_copy(gs[:, :, 0:2], st[:, ff, :, :].rearrange("p a b s -> p (a b) s")).then_inc(st_put, 1)
                            wait_count(dve, st_put, t - (THIRDS - 1) * NG, G, q + 1)
                        if i == 0:
                            wait_count(dve, taps_ready, t, G, G)
                        wait_count(dve, gate_out, t, NF, i + 1)
                        wait_count(dve, silu_ready, t, NF, i - 1)
                        c = cv[:, b, :]
                        rows_ = [(c, lambda j: gp[:, n * TW + j:n * TW + j + TW])]
                        if smp:
                            rows_ = [(c[:, 0:LASTP], lambda j: gp[:, n * TW + j:n * TW + j + LASTP]),
                                     (c[:, LASTP:TW].rearrange("p (b s) -> p b s", b=DB), lambda j: gs[:, :, j:j + DS])]
                        for out, row in rows_:
                            end = dve.tensor_scalar(out, row(2), tap[2], tap[3], ALU.mult, ALU.add)
                        end.then_inc(tap0, 1)
                        if n == NS - 1:
                            rest = LASTP if smp else TW
                            last_rows = dve.tensor_copy(carry[:, ff, :].rearrange("p a s -> p (a s)"), gp[:, n * TW + rest:n * TW + rest + 2])
                            if smp:
                                last_rows = dve.tensor_copy(keep_s[:, ff, :, :].rearrange("p a b s -> p (a b) s"), gs[:, :, DS:GB])
                            last_rows.then_inc(kept, 1)
                        wait_count(dve, tap0, t, NF, i + 1)
                        for out, row in rows_:
                            end = dve.scalar_tensor_tensor(out, row(1), tap[1], out, ALU.mult, ALU.add)
                        end.then_inc(tap1, 1)
                        wait_count(dve, tap1, t, NF, i + 1)
                        for out, row in rows_:
                            end = dve.scalar_tensor_tensor(out, row(0), tap[0], out, ALU.mult, ALU.add)
                        end.then_inc(conv_ready, 1)
                        if i:
                            f_part(i - 1)
                        wait_count(dve, silu_ready, t, NF, i + 1)
                        wait_count(dve, val_mm, t, NF, i + 1)
                        wait_count(dve, f_lo, t, NF, i - 1)
                        dve.tensor_tensor(fr[:, b, :], pv[b][:, 0:TW], sg[:, b, :], ALU.mult).then_inc(f_ready, 1)
                        if i in DOWN_AT:
                            weights_lo(t, 2 * G + DOWN_AT.index(i))
                    f_part(NF - 1)
                    for i in range(ND):
                        n, m = i // KD, i % KD
                        wait_count(dve, down_mm, t, ND, i + 1)
                        hm = hT[:, m, tok(s * NS + n)]
                        dve.tensor_tensor(hm, pd[i % 4][:, 0:TW], hm, ALU.add).then_inc(h_ready, 1)
                        if last and s == THIRDS - 1:
                            continue
                        if last:
                            if i == 0:
                                rows(s + 1, 0)
                            if i + 1 < NX:
                                rows(s + 1, i + 1)
                            rows_lo(s + 1, i)
                        if i % 4 == 3:
                            weights_lo(t + 1, i // 4)

                rows(0, 0)
                for j in range(NX):
                    if j + 1 < NX:
                        rows(0, j + 1)
                    rows_lo(0, j)
                    if j % 2 and j // 2 < 2 * G:
                        weights_lo(0, j // 2)
                thirds(dve, turn)

            @block.tensor
            def _(pe):
                def turn(s, t, g, last):
                    def up(out, w, n):
                        for k in range(KD):
                            if k_wait:
                                pe.wait_ge(x_lo, NX * s + n * KD + k + 1)
                            for j, (l, r) in enumerate(three([a[:, k, :] for a in w], [a[:, k, tok(n)] for a in xn])):
                                mm = pe.matmul(out[:, 0:TW], l, r, start=(k == 0 and j == 0), stop=(k == KD - 1 and j == 2))
                        return mm

                    for i in range(NF):
                        q, n, b = i // NS, i % NS, i % 2
                        k_wait = isinstance(g, int) and g == 0 and q == 0
                        if n == 0:
                            wait_count(pe, w_lo, t, NW, 2 * q + 1)
                        wait_count(pe, gate_out, t, NF, i - 1)
                        up(pg[b], wg[q], n).then_inc(gate_mm, 1)
                        if n == 0:
                            wait_count(pe, w_lo, t, NW, 2 * q + 2)
                        wait_count(pe, f_ready, t, NF, i - 1)
                        k_wait = False
                        up(pv[b], wv[q], n).then_inc(val_mm, 1)
                    wait_count(pe, w_lo, t, NW, NW)
                    for i in range(ND):
                        n, m = i // KD, i % KD
                        if m == 0:
                            wait_count(pe, f_lo, t, NF, NF - NS + n + 1)
                        wait_count(pe, h_ready, t, ND, i - 3)
                        for q in range(G):
                            for j, (l, r) in enumerate(three([a[:, m * P:(m + 1) * P] for a in wd[q]], [a[:, q, tok(n)] for a in f])):
                                mm = pe.matmul(pd[i % 4][:, 0:TW], l, r, start=(q == 0 and j == 0), stop=(q == G - 1 and j == 2))
                        mm.then_inc(down_mm, 1)
                thirds(pe, turn)


def gated_embedding(nc, ins, outs, hT):
    SQUARE_AT, MEAN_AT, ROOT_AT = 0, 2, 3
    with ExitStack() as ctx:
        e = Env(nc, ctx, "pe")
        h3 = e.sb("h3", [P, 2, KD, TW])
        wpg = e.sb("wpg", [P, KD, D])
        wple = e.sb("wple", [P, KP, D])
        pt = e.sb("pt", [P, KP, T])
        sig = e.sb("sig", [P, 2, TW])
        sq = e.sb("sq", [P, KD, TW])
        ssum = e.sb("ssum", [P, TW])
        rms = e.sb("rms", [P, TW])
        g = e.sb("g", [P, KD])
        eps = e.sb("eps", [P, 1])
        ones = e.sb("ones", [P, P])
        pn = [e.ps(f"pn{i}", [P, 512]) for i in range(2)]
        pg = [e.ps(f"pg{i}", [P, 512]) for i in range(3)]
        pl = [e.ps(f"pl{i}", [P, 512]) for i in range(3)]
        w_in = [e.sem(f"w_in{k}") for k in range(KD // 2)]
        ple_in, p_in, g_in, const_ready = e.sem("ple_in"), e.sem("p_in"), e.sem("g_in"), e.sem("const_ready")
        gate_mm, ple_mm = e.sem("gate_mm"), e.sem("ple_mm")
        sig_ready, prod_ready, h_ready = e.sem("sig_ready"), e.sem("prod_ready"), e.sem("h_ready")
        sq_ready, ssum_ready, ms_ready = e.sem("sq_ready"), e.sem("ssum_ready"), e.sem("ms_ready")
        rms_ready, inv_ready, y_ready = e.sem("rms_ready"), e.sem("inv_ready"), e.sem("y_ready")
        y_stored = [e.sem(f"y_stored{b}") for b in range(2)]

        with nc.Block() as block:
            @block.sync
            def _(sp):
                for k in range(0, KD, 2):
                    sp.dma_start(wpg[:, k:k + 2, :], ins["w_pg"][k:k + 2].rearrange("k p d -> p k d")).then_inc(w_in[k // 2], 16)
                for k in range(KP):
                    sp.dma_start(wple[:, k, :], ins["w_ple"][k]).then_inc(ple_in, 16)
                sp.dma_start(pt[:], ins["pT"]).then_inc(p_in, 16)
                sp.dma_start(g[:], ins["final_g"]).then_inc(g_in, 16)
                for n in range(NT):
                    sp.wait_ge(y_ready, KD * (n + 1))
                    sp.dma_start(outs["yT"][:, :, tok(n)], h3[:, n % 2]).then_inc(y_stored[n % 2], 16)
                for b in range(2):
                    sp.wait_ge(y_stored[b], 16 * (NT // 2))

            @block.gpsimd
            def _(pool):
                pool.memset(ones[:], 1.0 / D).then_inc(const_ready, 1)
                pool.memset(eps[:], RMS_EPS).then_inc(const_ready, 1)

            @block.scalar
            def _(act):
                act.wait_ge(const_ready, 2)

                def square(n):
                    act.wait_ge(h_ready, KD * (n + 1))
                    if n:
                        act.wait_ge(ssum_ready, n)
                    act.square(sq[:], h3[:, n % 2]).then_inc(sq_ready, 1)

                def root(n):
                    act.wait_ge(ms_ready, n + 1)
                    if n:
                        act.wait_ge(y_ready, KD * n)
                    act.activation(rms[:], pn[n % 2][:, 0:TW], ACT.Sqrt, bias=eps[:, 0:1]).then_inc(rms_ready, 1)

                for n in range(NT):
                    for m in range(KD):
                        i = n * KD + m
                        act.wait_ge(gate_mm, i + 1)
                        if i >= 2:
                            act.wait_ge(prod_ready, i - 1)
                        act.activation(sig[:, i % 2, :], pg[i % 3][:, 0:TW], ACT.Sigmoid).then_inc(sig_ready, 1)
                        if n and m == SQUARE_AT:
                            square(n - 1)
                        if n and m == ROOT_AT:
                            root(n - 1)
                square(NT - 1)
                root(NT - 1)

            @block.vector
            def _(dve):
                dve.wait_ge(g_in, 16)

                def norm_sum(n):
                    dve.wait_ge(sq_ready, n + 1)
                    if n:
                        dve.wait_ge(ms_ready, n)
                    dve.tensor_reduce(ssum[:], sq[:].rearrange("p k t -> p t k"), AX.X, ALU.add).then_inc(ssum_ready, 1)

                def inverse(n):
                    dve.wait_ge(rms_ready, n + 1)
                    dve.reciprocal(rms[:], rms[:]).then_inc(inv_ready, 1)

                def norm_apply(n, ks):
                    dve.wait_ge(inv_ready, n + 1)
                    for k in ks:
                        y = h3[:, n % 2, k, :]
                        dve.scalar_tensor_tensor(y, y, g[:, k:k + 1], rms[:], ALU.mult, ALU.mult).then_inc(y_ready, 1)

                for n in range(NT):
                    b = n % 2
                    if n >= 2:
                        dve.wait_ge(y_stored[b], 16 * (n // 2))
                    for m in range(KD):
                        i = n * KD + m
                        dve.wait_ge(sig_ready, i + 1)
                        dve.wait_ge(ple_mm, i + 1)
                        s = sig[:, i % 2, :]
                        dve.tensor_tensor(h3[:, b, m, :], pl[i % 3][:, 0:TW], s, ALU.mult).then_inc(prod_ready, 1)
                        dve.wait_ge(prod_ready, i + 1)
                        dve.tensor_tensor(h3[:, b, m, :], h3[:, b, m, :], hT[:, m, tok(n)], ALU.add).then_inc(h_ready, 1)
                        if n and m == SQUARE_AT:
                            norm_sum(n - 1)
                        if n and m == ROOT_AT:
                            inverse(n - 1)
                        if n and m > ROOT_AT:
                            norm_apply(n - 1, range(3 * (m - ROOT_AT - 1), min(3 * (m - ROOT_AT), KD)))
                norm_sum(NT - 1)
                inverse(NT - 1)
                norm_apply(NT - 1, range(KD))

            @block.tensor
            def _(pe):
                pe.wait_ge(const_ready, 2)
                pe.wait_ge(ple_in, 16 * KP)
                pe.wait_ge(p_in, 16)

                def mean_square(n):
                    pe.wait_ge(ssum_ready, n + 1)
                    if n >= 2:
                        pe.wait_ge(rms_ready, n - 1)
                    pe.matmul(pn[n % 2][:, 0:TW], ones[:], ssum[:], start=True, stop=True).then_inc(ms_ready, 1)

                for n in range(NT):
                    for m in range(KD):
                        i = n * KD + m
                        if i >= 3:
                            pe.wait_ge(prod_ready, i - 2)
                        for k in range(KD):
                            if i == 0 and k % 2 == 0:
                                pe.wait_ge(w_in[k // 2], 16)
                            mm = pe.matmul(pg[i % 3][:, 0:TW], wpg[:, k, m * P:(m + 1) * P], hT[:, k, tok(n)], start=(k == 0), stop=(k == KD - 1))
                        mm.then_inc(gate_mm, 1)
                        for k in range(KP):
                            mm = pe.matmul(pl[i % 3][:, 0:TW], wple[:, k, m * P:(m + 1) * P], pt[:, k, tok(n)], start=(k == 0), stop=(k == KP - 1))
                        mm.then_inc(ple_mm, 1)
                        if m == MEAN_AT and n:
                            mean_square(n - 1)
                mean_square(NT - 1)


C = 64
Q = 2
TB = C * Q
NB = SEQ // TB
TS = DB * DS
HP = 4
HD = 64
LOGW = math.exp(-0.5)
HALF = [slice(0, HD), slice(HD, P)]

PREP_POOL = [step + part for part in ("low", "k", "r", "v") for step in ("d_", "m_", "z_")] + ["rk0", "rk"]
PREP_DVE = ["kk", "ld", "L", "t0", "t1", "nmax", "inv0", "inv1", "aa", "sg", "inv2", "inv3", "kkn", "Lp", "b", "kp", "bonus"]
PREP_ACT = ["th", "sx", "kk2", "wt", "at", "nrm", "e1", "e2", "e3", "g"]
PREP_PE = ["w", "a", "ss", "g", "bonus"]
SHIFT = {"low": slice(12, 14), "k": slice(4, 8), "r": slice(0, 4), "v": slice(8, 12)}
STAGES = ["AabT", "Aab", "AqbT", "D2", "Dt2", "AakT", "D4", "Dt4", "X2", "D8", "X3", "Bt", "X4", "Kt", "X", "Z32", "Vt",
          "X32t", "X32", "Z64", "AqkT", "X64t", "RH", "U", "S", "Y"]
INTRA = STAGES[:22]
DVE_OUT = ["Dt", "Xt", "D", "O32", "O64", "AqbT", "AakT", "X2", "X3", "X4", "X32t", "X32", "AqkT", "X64t", "Sadd", "S"]
ACT_OUT = ["D2", "Dt2", "D4", "Dt4", "D8", "Bt", "Kt", "X", "Z32", "Vt", "Z64", "RH", "U", "Ylo", "Y"]
COPIED = {"AabT": "Dt", "Aab": "O64", "S": "Sadd"}
HAT_DVE = ["b", "a", "k"]
POST_DVE = ["d", "inv0", "inv1", "inv2", "inv3", "dn", "dg", "db", "dbonus", "y"]
NBANK = 3


def at(turn, order, name):
    return turn * len(order) + order.index(name) + 1


def delta_rule(nc, ins, outs, scratch, yb):
    with ExitStack() as ctx:
        e = Env(nc, ctx, "rw")
        w2 = e.sb("w2", [P, DRW])
        g2 = e.sb("g2", [P, DRW])
        mu = e.sb("mu", [P, ZT])
        col = {n: e.sb(n, [P, HP]) for n in ("w0", "a0", "k_k", "k_a", "r_k", "lnx_g", "lnx_b")}
        kah, ka1 = e.sb("kah", [P, HP]), e.sb("ka1", [P, HP])
        masks = e.sb("masks", [P, 13, P])
        bd64 = e.sb("bd64", [P, P])
        rows8 = e.sb("rows8", [P, DB])
        seg = e.sb("seg", [P, 2, HP * TB])
        geps = e.sb("geps", [P, 1])
        w0h, a0h = e.sb("w0h", [P, HP]), e.sb("a0h", [P, HP])
        Z = e.sb("Z", [P, ZT * (TB + 1)])
        z = e.sb("z", [P, ZT * TB])
        names = ("kk", "kk2", "w", "a", "L", "Lp", "E2", "E3", "t", "kp", "kkn", "b", "bonus", "g")
        B = {n: e.sb("p_" + n, [P, HP * TB]) for n in names}
        B |= {n: e.sb("p_" + n, [P, TB]) for n in ("th", "sx")}
        B |= {"nrm": B["kk2"], "ld": B["w"], "E1": B["Lp"], "rk": B["t"], "aa": B["a"]}
        bonus_h, g_h = e.sb("bonus_h", [P, HP * TB]), e.sb("g_h", [P, HP * TB])
        pc = e.sb("pc", [P, HP, DB])
        yt, ysq = e.sb("yt", [P, HP * TB]), e.sb("ysq", [P, HP * TB])
        yd, ysd = yt, ysq
        before_smp = e.sb("before_smp", [P, ZT, DB])
        keep = e.sb("keep", [P, ZT, 1 + DB])
        cn = ("aT", "bT", "kT", "rT", "vT", "Dt", "D", "O32", "O64", "AqbT", "AakT", "AqkT", "D2", "Dt2", "D4", "Dt4", "Xt")
        M = [{n: e.sb(f"{n}{q}", [P, HP, P]) for n in cn} for q in range(Q)]
        for m in M:
            m.update(D8=m["Dt"], Z=m["D"], Kt=m["D2"], Bt=m["Dt2"], X=m["D4"], Vt=m["Dt4"], RH=m["O32"], U=m["O64"])
        S = [e.sb(f"S{q}", [P, HP, P]) for q in range(Q)]
        Sb = [M[1][n] for n in ("aT", "bT", "kT", "rT", "vT", "AqbT", "AakT", "AqkT")]
        bank = [[e.ps(f"bank{q}{i}", [P, HP, P]) for i in range(NBANK)] for q in range(Q)]
        side = [e.ps(f"side{i}", [P, HP * P]) for i in range(2)]

        par_in, mu_in, z_in = e.sem("par_in"), e.sem("mu_in"), e.sem("z_in")
        NPAR = 13
        setup, zero = e.sem("setup"), e.sem("zero")
        prep_dve, prep_act, prep_pe = e.sem("prep_dve"), e.sem("prep_act"), e.sem("prep_pe")
        prep_pool, kept = e.sem("prep_pool"), e.sem("kept")
        hats_dve = e.sem("hats_dve")
        hats_pool = [e.sem(f"hats_pool{q}") for q in range(Q)]
        mm = [e.sem(f"mm{q}") for q in range(Q)]
        dve_out = [e.sem(f"dve_out{q}") for q in range(Q)]
        act_out = [e.sem(f"act_out{q}") for q in range(Q)]
        post_pe, post_act, post_dve = e.sem("post_pe"), e.sem("post_act"), e.sem("post_dve")
        keep_ready, stored = e.sem("keep_ready"), e.sem("stored")
        smp_in, smp_pe, smp_dve, smp_act = e.sem("smp_in"), e.sem("smp_pe"), e.sem("smp_dve"), e.sem("smp_act")
        hats_act = [e.sem(f"hats_act{q}") for q in range(Q)]
        BD, MD, MO32, MO64, MDT, MSU, MU, ID, SD, SDT, SSU, SU, NONE = range(13)
        FIRST, SAMPLES = 0, NB

        def is_first(t):
            return isinstance(t, int) and t == FIRST

        def is_samples(t):
            return isinstance(t, int) and t == SAMPLES

        STATE_AT = {"RH": 1, "U": 4, "S": 6, "Y": 8}

        def schedule(eng, half):
            half(FIRST, 0)
            half(FIRST, 1)
            half(1, 0)
            with eng.Fori(1, NB - 2) as t:
                half(t, 1)
                half(t + 1, 0)
            for t in (NB - 2, NB - 1):
                half(t, 1)
                half(t + 1, 0)

        def width(t):
            return TS if is_samples(t) else TB

        def chunks(t):
            return 1 if is_samples(t) else Q

        def v3(buf, W, w=None):
            return buf[:, 0:HP * W].rearrange("p (j t) -> p j t", t=W)

        def zv(i, n, W):
            return z[:].rearrange("p (j t) -> p j t", t=TB)[:, i:i + n, 0:W]

        def mask(m):
            return masks[:, m:m + 1, :].to_broadcast([P, HP, P])

        def copied(stage):
            return COPIED.get(stage, stage)

        def wait_copied(eng, q, t, name):
            name = copied(name)
            if name in DVE_OUT:
                eng.wait_ge(dve_out[q], at(t, DVE_OUT, name))
            else:
                eng.wait_ge(act_out[q], at(t, ACT_OUT, name))

        with nc.Block() as block:
            @block.sync
            def _(sp):
                src = scratch["zr"].rearrange("z p t -> p z t")
                Zp = Z[:].rearrange("p (z t) -> p z t", t=TB + 1)
                sp.dma_start(mu[:], ins["mu"]).then_inc(mu_in, 16)
                sp.dma_start(Zp[:, :, 1:], src[:, :, 0:TB]).then_inc(z_in, 16)
                for dst, name in ((w2, "w2a2"), (g2, "g2"), (masks, "masks"), (rows8, "rows8"), (seg, "seg")):
                    sp.dma_start(dst[:], ins[name]).then_inc(par_in, 16)
                for n, dst in col.items():
                    sp.dma_start(dst[:], ins[n]).then_inc(par_in, 16)
                sp.dma_start(before_smp[:], ins["state_shift"]).then_inc(par_in, 16)
                for t in range(1, NB):
                    sp.wait_ge(prep_pool, at(t - 1, PREP_POOL, "z_v"))
                    sp.dma_start(Zp[:], src[:, :, t * TB - 1:(t + 1) * TB]).then_inc(z_in, 16)
                Zs = Z[:, 0:ZT * DB * (DS + 1)].rearrange("p (z b s) -> p z b s", b=DB, s=DS + 1)
                sp.wait_ge(prep_pool, at(NB - 1, PREP_POOL, "z_v"))
                sp.wait_ge(keep_ready, 1)
                for zt in range(ZT):
                    sp.dma_start(Zs[:, zt, :, 1:], src[:, zt, SEQ:T].rearrange("p (b s) -> p b s", b=DB)).then_inc(z_in, 16)
                sp.wait_ge(mm[1], at(NB - 1, STAGES, "Y"))
                for b in range(DB):
                    for h in HALF:
                        sp.dma_start(Sb[b][h, :, h], ins["state_rwkv"][h, b]).then_inc(smp_in, 16)
                sp.wait_ge(keep_ready, 3)
                sp.dma_start(outs["shift"], keep[:]).then_inc(stored, 16)
                sp.wait_ge(dve_out[1], at(NB - 1, DVE_OUT, "S"))
                for h in range(2):
                    sp.dma_start(outs["rwkv_p"][HALF[h]], S[0][HALF[h], :, HALF[h]]).then_inc(stored, 16)
                sp.wait_ge(smp_dve, 4 * DB)
                for b in range(DB):
                    for h in range(2):
                        sp.dma_start(outs["rwkv_s"][HALF[h], b], Sb[b][HALF[h], :, HALF[h]]).then_inc(stored, 16)
                sp.wait_ge(stored, 16 * (3 + 2 * DB))

            @block.gpsimd
            def _(pool):
                pool.memset(S[0][:], 0.0).then_inc(zero, 1)
                pool.memset(Z[:].rearrange("p (z t) -> p z t", t=TB + 1)[:, :, 0:1], 0.0).then_inc(zero, 1)
                for q in range(Q):
                    for n in ("aT", "bT", "kT", "rT", "vT"):
                        pool.memset(M[q][n][:], 0.0).then_inc(zero, 1)
                pool.memset(geps[:], GN_EPS).then_inc(zero, 1)
                pool.wait_ge(zero, 13)

                def hats(t, q):
                    W = width(t)
                    pool.wait_ge(prep_act, at(t, PREP_ACT, "e3"))
                    if not is_first(t):
                        pool.wait_ge(mm[q], at(t - 1, STAGES, "Y"))
                    cq = slice(q * C, (q + 1) * C)
                    for n, h in enumerate(HALF):
                        pool.tensor_tensor(M[q]["rT"][h, :, h], zv(0, 4, W)[h, :, cq], v3(B["E3"], W)[h, :, cq], ALU.mult).then_inc(hats_pool[q], 1)
                        pool.wait_ge(hats_pool[q], 2 * t + n + 1)

                def shift(s, part):
                    W, n = width(s), SHIFT[part]
                    rows = n.stop - n.start
                    if is_samples(s):
                        Zs = Z[:, 0:ZT * DB * (DS + 1)].rearrange("p (z b s) -> p z b s", b=DB, s=DS + 1)
                        before, row = Zs[:, n, :, 0:DS], Zs[:, n, :, 1:]
                        zz = zv(n.start, rows, W).rearrange("p z (b s) -> p z b s", b=DB, s=DS)
                    else:
                        Zp = Z[:].rearrange("p (z t) -> p z t", t=TB + 1)
                        before, row = Zp[:, n, 0:TB], Zp[:, n, 1:]
                        zz = zv(n.start, rows, W)
                    flat = zv(n.start, rows, W)
                    pool.tensor_tensor(zz, before, row, ALU.subtract).then_inc(prep_pool, 1)
                    pool.wait_ge(prep_pool, at(s, PREP_POOL, "d_" + part))
                    pool.tensor_tensor(flat, flat, bcast(mu[:, n], W), ALU.mult).then_inc(prep_pool, 1)
                    pool.wait_ge(prep_pool, at(s, PREP_POOL, "m_" + part))
                    pool.tensor_tensor(zz, zz, row, ALU.add).then_inc(prep_pool, 1)

                def shift_early(s):
                    if is_samples(s):
                        pool.wait_ge(z_in, 16 * (NB + ZT))
                        Zs = Z[:, 0:ZT * DB * (DS + 1)].rearrange("p (z b s) -> p z b s", b=DB, s=DS + 1)
                        pool.tensor_copy(Zs[:, :, :, 0], before_smp[:]).then_inc(keep_ready, 1)
                        pool.wait_ge(keep_ready, 2)
                    else:
                        pool.wait_ge(z_in, 16 * (s + 1))
                    if not is_first(s):
                        pool.wait_ge(prep_dve, at(s - 1, PREP_DVE, "bonus"))
                    shift(s, "low")
                    shift(s, "k")

                def shift_late(s):
                    if not is_first(s):
                        for q in range(Q):
                            pool.wait_ge(hats_act[q], s)
                    shift(s, "r")
                    shift(s, "v")
                    W = width(s)
                    rk = v3(B["rk"], W)
                    pool.wait_ge(prep_dve, at(s, PREP_DVE, "kp"))
                    pool.wait_ge(prep_pool, at(s, PREP_POOL, "z_v"))
                    pool.tensor_tensor(rk, zv(0, 4, W), v3(B["kp"], W), ALU.mult).then_inc(prep_pool, 1)
                    pool.wait_ge(prep_pool, at(s, PREP_POOL, "rk0"))
                    pool.tensor_tensor(rk, rk, bcast(col["r_k"][:], W), ALU.mult).then_inc(prep_pool, 1)

                def turn(t):
                    shift_early(t + 1)
                    hats(t, 1)
                    shift_late(t + 1)
                    hats(t + 1, 0)

                pool.wait_ge(mu_in, 16)
                shift_early(FIRST)
                pool.wait_ge(par_in, 16 * NPAR)
                shift_late(FIRST)
                hats(FIRST, 0)
                turn(FIRST)
                with pool.Fori(1, NB - 1) as t:
                    turn(t)
                pool.tensor_copy(keep[:, :, 0:1], Z[:].rearrange("p (z t) -> p z t", t=TB + 1)[:, :, TB:TB + 1]).then_inc(keep_ready, 1)
                pool.wait_ge(keep_ready, 1)
                turn(NB - 1)
                Zs = Z[:, 0:ZT * DB * (DS + 1)].rearrange("p (z b s) -> p z b s", b=DB, s=DS + 1)
                pool.tensor_copy(keep[:, :, 1:], Zs[:, :, :, DS]).then_inc(keep_ready, 1)

            @block.vector
            def _(dve):
                dve.wait_ge(par_in, 16 * NPAR)
                dve.tensor_scalar(kah[:], col["k_a"][:], 0.5, None, ALU.mult).then_inc(setup, 1)
                dve.tensor_scalar(ka1[:], col["k_a"][:], -0.5, 1.0, ALU.mult, ALU.add).then_inc(setup, 1)
                dve.tensor_scalar(bd64[:], masks[:, BD, :], 1.0 / HD, None, ALU.mult).then_inc(setup, 1)
                dve.tensor_scalar(w0h[:], col["w0"][:], 0.5, None, ALU.mult).then_inc(setup, 1)
                dve.tensor_scalar(a0h[:], col["a0"][:], 0.5, None, ALU.mult).then_inc(setup, 1)
                dve.wait_ge(setup, 5)
                dve.wait_ge(zero, 13)

                def prepare(s, *steps):
                    W = width(s)
                    b = {n: v3(x, W) for n, x in B.items() if n not in ("th", "sx")}
                    k, v = zv(4, 4, W), zv(8, 4, W)

                    def mine(name):
                        dve.wait_ge(prep_dve, at(s, PREP_DVE, name))

                    def act_did(name):
                        dve.wait_ge(prep_act, at(s, PREP_ACT, name))

                    for step in steps:
                        if step == "kk":
                            dve.wait_ge(prep_pool, at(s, PREP_POOL, "z_k"))
                            dve.tensor_tensor(b["kk"], k, bcast(col["k_k"][:], W), ALU.mult).then_inc(prep_dve, 1)
                        elif step == "L":
                            act_did("wt")
                            dve.tensor_scalar(b["ld"], b["w"], -LOGW / 2, -LOGW / 2, ALU.mult, ALU.add).then_inc(prep_dve, 1)
                            mine("ld")
                            dve.tensor_tensor_scan(B["L"][:, 0:HP * W], seg[:, 1 if is_samples(s) else 0, 0:HP * W], B["ld"][:, 0:HP * W], 0.0,
                                                   ALU.mult, ALU.add).then_inc(prep_dve, 1)
                        elif step == "t":
                            act_did("at")
                            dve.tensor_tensor(b["t"], b["a"], bcast(kah[:], W), ALU.mult).then_inc(prep_dve, 1)
                            mine("t0")
                            dve.tensor_tensor(b["t"], b["t"], bcast(ka1[:], W), ALU.add).then_inc(prep_dve, 1)
                        elif step == "nmax":
                            act_did("nrm")
                            dve.tensor_scalar(b["nrm"], b["nrm"], L2_EPS, None, ALU.max).then_inc(prep_dve, 1)
                        elif step in range(HP):
                            mine("nmax")
                            dve.reciprocal(b["nrm"][:, step], b["nrm"][:, step]).then_inc(prep_dve, 1)
                        elif step == "aa":
                            mine("t0")
                            dve.tensor_scalar(b["aa"], b["a"], 0.5, 0.5, ALU.mult, ALU.add).then_inc(prep_dve, 1)
                        elif step == "sg":
                            act_did("sx")
                            dve.tensor_scalar(B["sx"][:, 0:W], B["sx"][:, 0:W], 0.5, 0.5, ALU.mult, ALU.add).then_inc(prep_dve, 1)
                        elif step == "kkn":
                            mine("inv3")
                            dve.tensor_tensor(b["kkn"], b["kk"], b["nrm"], ALU.mult).then_inc(prep_dve, 1)
                        elif step == "Lp":
                            mine("L")
                            dve.tensor_tensor(b["Lp"], b["L"], b["ld"], ALU.subtract).then_inc(prep_dve, 1)
                        elif step == "b":
                            mine("kkn")
                            dve.tensor_tensor(b["b"], b["kkn"], b["aa"], ALU.mult).then_inc(prep_dve, 1)
                        elif step == "kp":
                            mine("t1")
                            dve.tensor_tensor(b["kp"], k, b["t"], ALU.mult).then_inc(prep_dve, 1)
                        elif step == "bonus":
                            dve.wait_ge(prep_pe, at(s, PREP_PE, "bonus"))
                            if not is_first(s):
                                dve.wait_ge(kept, 2 * s)
                            dve.tensor_tensor(b["bonus"], v3(side[1], W), v, ALU.mult).then_inc(prep_dve, 1)

                def hats(t, q, *names):
                    W = width(t)
                    b = {n: v3(x, W) for n, x in B.items() if n not in ("th", "sx")}
                    cq = slice(q * C, (q + 1) * C)
                    m = M[q]
                    for name in names:
                        if name == "bT":
                            dve.wait_ge(prep_act, at(t, PREP_ACT, "e3"))
                            dve.wait_ge(prep_dve, at(t, PREP_DVE, "kp"))
                            if not is_first(t):
                                dve.wait_ge(mm[q], at(t - 1, STAGES, "Y"))
                        for h in HALF:
                            if name == "bT":
                                last = dve.tensor_tensor(m["bT"][h, :, h], b["b"][h, :, cq], b["E2"][h, :, cq], ALU.mult)
                            elif name == "aT":
                                last = dve.scalar_tensor_tensor(m["aT"][h, :, h], b["kkn"][h, :, cq], -1.0, b["E1"][h, :, cq], ALU.mult, ALU.mult)
                            else:
                                last = dve.tensor_tensor(m["kT"][h, :, h], b["kp"][h, :, cq], b["E2"][h, :, cq], ALU.mult)
                        last.then_inc(hats_dve, 1)

                def copy_out(q, t, stage):
                    m, smp = M[q], is_samples(t)
                    src = bank[q][STAGES.index(stage) % NBANK][:]
                    dve.wait_ge(mm[q], at(t, STAGES, stage))

                    def masked(name, which):
                        dve.tensor_tensor(m[name][:], src, mask(which), ALU.mult).then_inc(dve_out[q], 1)

                    if stage == "AabT":
                        masked("Dt", SDT if smp else MDT)
                        dve.wait_ge(dve_out[q], at(t, DVE_OUT, "Dt"))
                        dve.tensor_tensor(m["Xt"][:], m["Dt"][:], mask(ID), ALU.add).then_inc(dve_out[q], 1)
                    elif stage == "Aab":
                        masked("D", SD if smp else MD)
                        masked("O32", NONE if smp else MO32)
                        masked("O64", NONE if smp else MO64)
                    elif stage in ("AqbT", "AqkT"):
                        masked(stage, SU if smp else MU)
                    elif stage == "AakT":
                        masked(stage, SSU if smp else MSU)
                    elif stage in ("X2", "X3", "X4", "X32t", "X64t"):
                        dve.tensor_tensor(m["Xt"][:], src, m["Xt"][:], ALU.add).then_inc(dve_out[q], 1)
                    elif stage == "X32":
                        dve.wait_ge(act_out[q], at(t, ACT_OUT, "X"))
                        dve.tensor_tensor(m["X"][:], src, m["X"][:], ALU.add).then_inc(dve_out[q], 1)
                    elif stage == "S":
                        old, new = S[q], S[1 - q]
                        dve.tensor_tensor(new[:], src, old[:], ALU.add).then_inc(dve_out[q], 1)
                        dve.wait_ge(dve_out[q], at(t, DVE_OUT, "Sadd"))
                        dve.wait_ge(kept, 2 * t + 1)
                        dve.tensor_tensor(new[:], new[:], pc[:, :, q:q + 1].to_broadcast([P, HP, P]), ALU.mult).then_inc(dve_out[q], 1)

                def finish(t, *steps):
                    W = width(t)
                    y, d, sd = v3(yt, W), v3(yd, W), v3(ysd, W)

                    def mine(name):
                        dve.wait_ge(post_dve, at(t, POST_DVE, name))

                    for step in steps:
                        if step == "d":
                            dve.wait_ge(post_pe, 2 * t + 1)
                            dve.tensor_tensor(d, y, v3(side[1], W), ALU.subtract).then_inc(post_dve, 1)
                        elif step in range(HP):
                            dve.wait_ge(post_act, 2 * t + 2)
                            dve.reciprocal(sd[:, step], sd[:, step]).then_inc(post_dve, 1)
                        elif step == "dn":
                            mine("inv3")
                            dve.tensor_tensor(d, d, sd, ALU.mult).then_inc(post_dve, 1)
                        elif step == "dg":
                            mine("dn")
                            dve.tensor_tensor(d, d, bcast(col["lnx_g"][:], W), ALU.mult).then_inc(post_dve, 1)
                        elif step == "db":
                            mine("dg")
                            dve.tensor_tensor(d, d, bcast(col["lnx_b"][:], W), ALU.add).then_inc(post_dve, 1)
                        elif step == "dbonus":
                            mine("db")
                            dve.wait_ge(kept, 2 * t + 2)
                            dve.tensor_tensor(d, d, v3(bonus_h, W), ALU.add).then_inc(post_dve, 1)
                        elif step == "y":
                            mine("dbonus")
                            dve.tensor_tensor(yb[:, :, bass.ds(t * TB, W)], d, v3(g_h, W), ALU.mult).then_inc(post_dve, 1)

                ADD = {"AabT", "Aab", "AqbT", "AakT", "X2", "AqkT", "X3", "X4", "X32t", "X32", "X64t"}
                NEXT = [{3: ["kk"], 9: ["L", "t"], 15: ["nmax", 0], 16: [1], 19: ["aa", "sg"]},
                        {3: [2, 3], 4: ["kkn", "Lp"], 7: ["b", "kp"], 19: ["bonus"]}]
                BEFORE = [{11: ["d"]}, {8: [0, 1, 2, 3], 11: ["dn"], 13: ["dg", "db"], 14: ["dbonus", "y"]}]
                HATS = [{13: ["bT", "aT"], 14: ["kT"]}, {15: ["bT", "aT"], 16: ["kT"]}]
                REST = [step for i in BEFORE[1] for step in BEFORE[1][i]]

                def half(t, q):
                    before = (t, 0) if q else (t - 1, 1)
                    for i, stage in enumerate(INTRA):
                        if stage in ADD:
                            copy_out(q, t, stage)
                        if i == STATE_AT["S"] and not (q == 0 and is_first(t)):
                            copy_out(before[1], before[0], "S")
                        if i in HATS[q] and not is_samples(t):
                            hats(t + q, 1 - q, *HATS[q][i])
                        if i in NEXT[q] and not is_samples(t):
                            prepare(t + 1, *NEXT[q][i])
                        if i in BEFORE[q] and not is_first(t):
                            finish(t - 1, *BEFORE[q][i])

                prepare(FIRST, "kk", "L", "t", "nmax", 0, 1, "aa", "sg", 2, 3, "kkn", "Lp", "b", "kp", "bonus")
                hats(FIRST, 0, "bT", "aT", "kT")
                schedule(dve, half)
                finish(NB - 1, *REST)
                m = M[0]
                for b in range(DB):
                    if b == 0:
                        dve.wait_ge(smp_act, 3)
                        dve.wait_ge(act_out[0], at(SAMPLES, ACT_OUT, "Vt"))
                        dve.wait_ge(smp_pe, 4)
                    dve.tensor_scalar(M[1]["D2"][:], m["U"][:], rows8[:, b:b + 1], None, ALU.mult).then_inc(smp_dve, 1)
                    dve.tensor_scalar(M[1]["Dt2"][:], m["Vt"][:], rows8[:, b:b + 1], None, ALU.mult).then_inc(smp_dve, 1)
                    if b == 0:
                        dve.wait_ge(smp_in, 16 * 2 * DB)
                    dve.wait_ge(smp_pe, 5 + b)
                    dve.tensor_tensor(Sb[b][:], bank[0][b % NBANK][:], Sb[b][:], ALU.add).then_inc(smp_dve, 1)
                    dve.wait_ge(smp_dve, 4 * b + 3)
                    dve.wait_ge(kept, 2 * SAMPLES + 1)
                    dve.tensor_tensor(Sb[b][:], Sb[b][:], pc[:, :, b:b + 1].to_broadcast([P, HP, P]), ALU.mult).then_inc(smp_dve, 1)
                finish(SAMPLES, "d", *REST)

            @block.scalar
            def _(act):
                act.wait_ge(zero, 13)
                act.wait_ge(setup, 5)

                def prepare(s, *steps):
                    W = width(s)
                    b = {n: v3(x, W) for n, x in B.items() if n not in ("th", "sx")}

                    def dve_did(name):
                        act.wait_ge(prep_dve, at(s, PREP_DVE, name))

                    for step in steps:
                        if step == "th":
                            act.wait_ge(prep_pool, at(s, PREP_POOL, "z_low"))
                            act.activation(B["th"][0:HD, 0:W], zv(12, 1, W)[0:HD, 0, :], ACT.Tanh).then_inc(prep_act, 1)
                            act.activation(B["sx"][:, 0:W], zv(13, 1, W)[:, 0, :], ACT.Tanh, scale=0.5).then_inc(prep_act, 1)
                        elif step == "kk2":
                            dve_did("kk")
                            act.square(b["kk2"], b["kk"]).then_inc(prep_act, 1)
                        elif step in ("wt", "at"):
                            which, half_bias, n = ("w", w0h, 0) if step == "wt" else ("a", a0h, 1)
                            act.wait_ge(prep_pe, at(s, PREP_PE, which))
                            if not is_first(s):
                                act.wait_ge(prep_dve, at(s - 1, PREP_DVE, "b"))
                            for j in range(HP):
                                last = act.activation(b[which][:, j], v3(side[n], W)[:, j], ACT.Tanh, bias=half_bias[:, j:j + 1], scale=0.5)
                            last.then_inc(prep_act, 1)
                        elif step == "nrm":
                            act.wait_ge(prep_pe, at(s, PREP_PE, "ss"))
                            act.activation(b["nrm"], v3(side[1], W), ACT.Sqrt).then_inc(prep_act, 1)
                        elif step == "e":
                            if not is_first(s):
                                act.wait_ge(hats_pool[0], s * 2)
                                act.wait_ge(hats_pool[1], s * 2)
                                act.wait_ge(hats_dve, s * 6)
                                act.wait_ge(kept, 2 * s - 1)
                            dve_did("Lp")
                            act.activation(b["E1"], b["Lp"], ACT.Exp).then_inc(prep_act, 1)
                            act.activation(b["E2"], b["L"], ACT.Exp, scale=-1.0).then_inc(prep_act, 1)
                            act.activation(b["E3"], b["L"], ACT.Exp).then_inc(prep_act, 1)
                        elif step == "g":
                            act.wait_ge(prep_pe, at(s, PREP_PE, "g"))
                            if not is_first(s):
                                act.wait_ge(kept, 2 * s)
                            act.copy(b["g"], v3(side[0], W)).then_inc(prep_act, 1)

                def hats(t, q):
                    W = width(t)
                    act.wait_ge(prep_pool, at(t, PREP_POOL, "z_v"))
                    if not is_first(t):
                        act.wait_ge(mm[q], at(t - 1, STAGES, "Y"))
                    for h in HALF:
                        last = act.copy(M[q]["vT"][h, :, h], zv(8, 4, W)[h, :, q * C:(q + 1) * C])
                    last.then_inc(hats_act[q], 1)

                def keep_decays(t):
                    W = width(t)
                    if not is_first(t):
                        act.wait_ge(dve_out[1], at(t - 1, DVE_OUT, "S"))
                    step = DS if is_samples(t) else C
                    act.copy(pc[:, :, 0:W // step], v3(B["E3"], W)[:, :, step - 1::step]).then_inc(kept, 1)

                def keep_gate(t):
                    W = width(t)
                    act.wait_ge(prep_dve, at(t, PREP_DVE, "bonus"))
                    if not is_first(t):
                        act.wait_ge(post_dve, at(t - 1, POST_DVE, "y"))
                    act.copy(bonus_h[:, 0:HP * W], B["bonus"][:, 0:HP * W])
                    act.copy(g_h[:, 0:HP * W], B["g"][:, 0:HP * W]).then_inc(kept, 1)

                def copy_out(q, t, stage):
                    dst = {"Z32": "Z", "Z64": "Z"}.get(stage, stage)
                    act.wait_ge(mm[q], at(t, STAGES, stage))
                    act.copy(M[q][dst][:], bank[q][STAGES.index(stage) % NBANK][:]).then_inc(act_out[q], 1)

                def rows_out(q, t):
                    if q == 0 and not is_first(t):
                        act.wait_ge(post_dve, at(t - 1, POST_DVE, "y"))
                    act.wait_ge(mm[q], at(t, STAGES, "Y"))
                    src = bank[q][STAGES.index("Y") % NBANK]
                    for h in HALF:
                        act.copy(v3(yt, TB)[h, :, q * C:(q + 1) * C], src[h, :, h]).then_inc(act_out[q], 1)

                def finish(t, part):
                    W = width(t)
                    if part == 0:
                        act.wait_ge(post_dve, at(t, POST_DVE, "d"))
                        act.square(v3(ysq, W), v3(yd, W)).then_inc(post_act, 1)
                        return
                    act.wait_ge(post_pe, 2 * t + 2)
                    act.activation(v3(ysd, W), v3(side[0], W), ACT.Sqrt, bias=geps[:, 0:1]).then_inc(post_act, 1)

                PLAIN = {"D2", "Dt2", "D4", "Dt4", "D8", "Bt", "Kt", "X", "Vt", "Z32", "Z64"}
                NEXT = [{4: ["th"], 5: ["kk2"], 7: ["wt", "at"], 8: ["nrm"]}, {8: ["e"], 19: ["g"]}]
                BEFORE = [{12: 0, 16: 1}, {}]
                HATS_AT, ROWS_AT = [9, 17], [9, 16]

                def half(t, q):
                    before = (t, 0) if q else (t - 1, 1)
                    for i, stage in enumerate(INTRA):
                        if q and i == 0:
                            keep_decays(t)
                        if stage in PLAIN:
                            copy_out(q, t, stage)
                        if not (q == 0 and is_first(t)):
                            if i == STATE_AT["RH"]:
                                copy_out(before[1], before[0], "RH")
                            if i == STATE_AT["U"]:
                                copy_out(before[1], before[0], "U")
                        if q and i == ROWS_AT[1]:
                            keep_gate(t)
                        if i == ROWS_AT[q] and not (q == 0 and is_first(t)):
                            rows_out(before[1], before[0])
                        if i == HATS_AT[q] and not is_samples(t):
                            hats(t + q, 1 - q)
                        if i in NEXT[q] and not is_samples(t):
                            prepare(t + 1, *NEXT[q][i])
                        if i in BEFORE[q] and not is_first(t):
                            finish(t - 1, BEFORE[q][i])

                prepare(FIRST, "th", "kk2", "wt", "at", "nrm", "e", "g")
                hats(FIRST, 0)
                schedule(act, half)
                keep_decays(SAMPLES)
                keep_gate(SAMPLES)
                m = M[0]
                act.wait_ge(smp_pe, 1)
                act.copy(m["RH"][:], bank[1][2][:]).then_inc(smp_act, 1)
                act.wait_ge(smp_pe, 2)
                act.copy(m["Z"][:], bank[1][0][:]).then_inc(smp_act, 1)
                act.wait_ge(smp_pe, 3)
                act.copy(m["U"][:], bank[1][2][:]).then_inc(smp_act, 1)
                act.wait_ge(smp_pe, 4)
                for h in HALF:
                    last = act.copy(v3(yt, TS)[h], bank[1][1][h, :, h])
                last.then_inc(smp_act, 1)
                finish(SAMPLES, 0)
                finish(SAMPLES, 1)

            @block.tensor
            def _(pe):
                pe.wait_ge(par_in, 16 * NPAR)
                pe.wait_ge(setup, 5)
                pe.wait_ge(zero, 13)
                ident = masks[:, ID, :]

                def prepare(s, *steps):
                    W = width(s)

                    def low_rank(bank_, w, x):
                        for j in range(HP):
                            last = pe.matmul(v3(bank_, W)[:, j, :], w[:, j * P:(j + 1) * P], x, start=True, stop=True)
                        last.then_inc(prep_pe, 1)

                    def dve_did(name):
                        pe.wait_ge(prep_dve, at(s, PREP_DVE, name))

                    def act_did(name):
                        pe.wait_ge(prep_act, at(s, PREP_ACT, name))

                    for step in steps:
                        if step == "w":
                            act_did("th")
                            if not is_first(s):
                                pe.wait_ge(prep_act, at(s - 1, PREP_ACT, "g"))
                                pe.wait_ge(prep_dve, at(s - 1, PREP_DVE, "bonus"))
                            low_rank(side[0], w2[0:HD, :], B["th"][0:HD, 0:W])
                            low_rank(side[1], w2[HD:P, :], zv(12, 1, W)[HD:P, 0, :])
                        elif step == "ss":
                            act_did("at")
                            pe.matmul(side[1][:, 0:HP * W], masks[:, BD, :], B["kk2"][:, 0:HP * W], start=True, stop=True).then_inc(prep_pe, 1)
                        elif step == "g":
                            act_did("wt")
                            dve_did("sg")
                            if not (is_first(s) or (isinstance(s, int) and s == 1)):
                                pe.wait_ge(post_act, 2 * (s - 1))
                            low_rank(side[0], g2[:], B["sx"][:, 0:W])
                        elif step == "bonus":
                            act_did("nrm")
                            pe.wait_ge(prep_pool, at(s, PREP_POOL, "rk"))
                            if not (is_first(s) or (isinstance(s, int) and s == 1)):
                                pe.wait_ge(post_dve, at(s - 2, POST_DVE, "d"))
                            pe.matmul(side[1][:, 0:HP * W], masks[:, BD, :], B["rk"][:, 0:HP * W], start=True, stop=True).then_inc(prep_pe, 1)

                LAST_IN_BANK = ["S", "Y", "U"]

                def product(q, t, stage, operands, after=(), transpose=False):
                    i = STAGES.index(stage)
                    names = [copied(n) for n in after] + ([copied(STAGES[i - NBANK])] if i >= NBANK else [])
                    for sem, order in ((dve_out[q], DVE_OUT), (act_out[q], ACT_OUT)):
                        mine = [n for n in names if n in order]
                        if mine:
                            pe.wait_ge(sem, at(t, order, max(mine, key=order.index)))
                    if i < NBANK and not is_first(t):
                        wait_copied(pe, q, t - 1, LAST_IN_BANK[i])
                    out = bank[q][STAGES.index(stage) % NBANK]
                    for j in range(HP):
                        for n, (l, r) in enumerate(operands):
                            if transpose:
                                last = pe.transpose(out[:, j, :], l[:, j, :], ident)
                            else:
                                last = pe.matmul(out[:, j, :], l[:, j, :], r[:, j, :], start=(n == 0), stop=(n == len(operands) - 1))
                    last.then_inc(mm[q], 1)

                def intra(q, t, stage):
                    m = M[q]
                    dve_hats = 6 * t + 3 * q
                    if stage == "AabT":
                        pe.wait_ge(hats_dve, dve_hats + 2)
                        product(q, t, stage, [(m["bT"], m["aT"])])
                    elif stage == "Aab":
                        product(q, t, stage, [(m["aT"], m["bT"])])
                    elif stage == "AqbT":
                        pe.wait_ge(hats_pool[q], 2 * t + 2)
                        product(q, t, stage, [(m["bT"], m["rT"])])
                    elif stage == "D2":
                        product(q, t, stage, [(m["Dt"], m["D"])], after=["Dt", "D"])
                    elif stage == "Dt2":
                        product(q, t, stage, [(m["D"], m["Dt"])])
                    elif stage == "AakT":
                        pe.wait_ge(hats_dve, dve_hats + 3)
                        product(q, t, stage, [(m["kT"], m["aT"])])
                    elif stage == "D4":
                        product(q, t, stage, [(m["Dt2"], m["D2"])], after=["D2", "Dt2"])
                    elif stage == "Dt4":
                        product(q, t, stage, [(m["D2"], m["Dt2"])])
                    elif stage == "X2":
                        product(q, t, stage, [(m["D2"], m["Xt"])], after=["Xt"])
                    elif stage == "AqkT":
                        product(q, t, stage, [(m["kT"], m["rT"])])
                    elif stage == "D8":
                        product(q, t, stage, [(m["Dt4"], m["D4"])], after=["D4", "Dt4"])
                    elif stage == "X3":
                        product(q, t, stage, [(m["D4"], m["Xt"])], after=["X2"])
                    elif stage == "Bt":
                        product(q, t, stage, [(m["bT"], None)], transpose=True)
                    elif stage == "X4":
                        product(q, t, stage, [(m["D8"], m["Xt"])], after=["D8", "X3"])
                    elif stage == "Kt":
                        product(q, t, stage, [(m["kT"], None)], transpose=True)
                    elif stage == "X":
                        product(q, t, stage, [(m["Xt"], None)], after=["X4"], transpose=True)
                    elif stage == "Vt":
                        pe.wait_ge(hats_act[q], t + 1)
                        product(q, t, stage, [(m["vT"], None)], transpose=True)
                    elif stage == "Z32":
                        product(q, t, stage, [(m["O32"], m["Xt"])], after=["O32"])
                    elif stage == "X32t":
                        product(q, t, stage, [(m["X"], m["Z"])], after=["X", "Z32"])
                    elif stage == "X32":
                        product(q, t, stage, [(m["Z"], m["X"])])
                    elif stage == "Z64":
                        product(q, t, stage, [(m["O64"], m["Xt"])], after=["X32t"])
                    elif stage == "X64t":
                        product(q, t, stage, [(m["X"], m["Z"])], after=["X32", "Z64"])

                def with_state(q, t, stage):
                    m = M[q]
                    if stage == "RH":
                        if q == 1:
                            pe.wait_ge(dve_out[0], at(t, DVE_OUT, "S"))
                        elif not is_first(t):
                            pe.wait_ge(dve_out[1], at(t - 1, DVE_OUT, "S"))
                        product(q, t, stage, [(m["aT"], S[q]), (m["AakT"], m["Vt"])], after=["AakT", "Vt"])
                    elif stage == "U":
                        product(q, t, stage, [(m["Xt"], m["RH"])], after=["X64t", "RH"])
                    elif stage == "S":
                        product(q, t, stage, [(m["Bt"], m["U"]), (m["Kt"], m["Vt"])], after=["Bt", "Kt", "U"])
                    elif stage == "Y":
                        product(q, t, stage, [(S[q], m["rT"]), (m["U"], m["AqbT"]), (m["Vt"], m["AqkT"])], after=["AqbT", "AqkT"])

                def finish(t, part):
                    W = width(t)
                    if part == 1:
                        pe.wait_ge(post_act, 2 * t + 1)
                        if isinstance(t, int) and t == NB - 1:
                            pe.wait_ge(prep_act, at(SAMPLES, PREP_ACT, "g"))
                        pe.matmul(side[0][:, 0:HP * W], bd64[:], ysq[:, 0:HP * W], start=True, stop=True).then_inc(post_pe, 1)
                        return
                    if is_samples(t):
                        pe.wait_ge(smp_act, 4)
                    else:
                        for q in range(Q):
                            pe.wait_ge(act_out[q], at(t, ACT_OUT, "Y"))
                    if is_samples(t):
                        pe.wait_ge(post_dve, at(NB - 1, POST_DVE, "d"))
                        pe.wait_ge(post_act, 2 * NB)
                    elif isinstance(t, int) and t == NB - 1:
                        pe.wait_ge(prep_dve, at(SAMPLES, PREP_DVE, "bonus"))
                    else:
                        pe.wait_ge(prep_act, at(t + 2, PREP_ACT, "nrm"))
                    pe.matmul(side[1][:, 0:HP * W], bd64[:], yt[:, 0:HP * W], start=True, stop=True).then_inc(post_pe, 1)

                NEXT = [{6: ["w"], 8: ["ss"]}, {3: ["g"], 17: ["bonus"]}]
                BEFORE = [{11: 0, 14: 1}, {}]

                def half(t, q):
                    before = (t, 0) if q else (t - 1, 1)
                    for i, stage in enumerate(INTRA):
                        intra(q, t, stage)
                        if not (q == 0 and is_first(t)):
                            for step, after in STATE_AT.items():
                                if i == after:
                                    with_state(before[1], before[0], step)
                        if i in NEXT[q] and not is_samples(t):
                            prepare(t + 1, *NEXT[q][i])
                        if i in BEFORE[q] and not is_first(t):
                            finish(t - 1, BEFORE[q][i])

                prepare(FIRST, "w", "ss", "g", "bonus")
                schedule(pe, half)
                m = M[0]
                tok_of = lambda ap, j, b: ap[:, j, :].rearrange("p (h b s) -> p h b s", h=2, b=DB)[:, :, b, :]
                pe.wait_ge(smp_in, 16 * 2 * DB)
                wait_copied(pe, 1, NB - 1, "S")
                wait_copied(pe, 1, NB - 1, "Y")
                for j in range(HP):
                    for b in range(DB):
                        last = pe.matmul(tok_of(bank[1][2], j, b), Sb[b][:, j, :], tok_of(m["aT"], j, b), start=True, stop=True)
                last.then_inc(smp_pe, 1)
                pe.wait_ge(smp_act, 1)
                wait_copied(pe, 0, SAMPLES, "AakT")
                wait_copied(pe, 0, SAMPLES, "Vt")
                for j in range(HP):
                    pe.matmul(bank[1][0][:, j, :], m["RH"][:, j, :], ident, start=True, stop=False)
                    last = pe.matmul(bank[1][0][:, j, :], m["AakT"][:, j, :], m["Vt"][:, j, :], start=False, stop=True)
                last.then_inc(smp_pe, 1)
                pe.wait_ge(smp_act, 2)
                wait_copied(pe, 0, SAMPLES, "X64t")
                for j in range(HP):
                    last = pe.matmul(bank[1][2][:, j, :], m["Xt"][:, j, :], m["Z"][:, j, :], start=True, stop=True)
                last.then_inc(smp_pe, 1)
                pe.wait_ge(smp_act, 3)
                wait_copied(pe, 0, SAMPLES, "AqkT")
                for j in range(HP):
                    pe.matmul(bank[1][1][:, j, :], m["U"][:, j, :], m["AqbT"][:, j, :], start=True, stop=False)
                    pe.matmul(bank[1][1][:, j, :], m["Vt"][:, j, :], m["AqkT"][:, j, :], start=False, stop=False)
                    for b in range(DB):
                        last = pe.matmul(tok_of(bank[1][1], j, b), Sb[b][:, j, :], tok_of(m["rT"], j, b), start=False, stop=(b == DB - 1))
                last.then_inc(smp_pe, 1)
                wait_copied(pe, 0, SAMPLES, "Kt")
                wait_copied(pe, 0, SAMPLES, "Z64")
                for b in range(DB):
                    pe.wait_ge(smp_dve, 4 * b + 2)
                    for j in range(HP):
                        pe.matmul(bank[0][b % NBANK][:, j, :], m["Bt"][:, j, :], M[1]["D2"][:, j, :], start=True, stop=False)
                        last = pe.matmul(bank[0][b % NBANK][:, j, :], m["Kt"][:, j, :], M[1]["Dt2"][:, j, :], start=False, stop=True)
                    last.then_inc(smp_pe, 1)
                finish(SAMPLES, 0)
                finish(SAMPLES, 1)


def rwkv_masks():
    import numpy as np
    i = np.arange(P)
    h, t = i // HD, i % HD
    head = h[:, None] == h[None, :]
    low, up = t[:, None] > t[None, :], t[:, None] < t[None, :]
    eq = t[:, None] == t[None, :]
    same = lambda n: head & (t[:, None] // n == t[None, :] // n)
    cross = lambda n: same(2 * n) & (t[:, None] // n > t[None, :] // n)
    ms = [head, same(16) & low, cross(16), cross(32), same(16) & up, head & up, head & (up | eq), head & eq,
          same(DS) & low, same(DS) & up, same(DS) & up, same(DS) & (up | eq), np.zeros((P, P), bool)]
    return np.stack(ms, 1).astype(np.float32)


def sample_rows():
    import numpy as np
    return (np.arange(P)[:, None] % HD // DS == np.arange(DB)[None]).astype(np.float32)


def chunk_starts():
    import numpy as np
    a = np.ones((P, 2, HP * TB), np.float32)
    a[:, 0, ::C] = 0
    a[:, 1, ::DS] = 0
    return a


NG_ = 32
GC = 16
NS = 64
L = P // GC
NJ = NG_ // 2
NBL = SEQ // L
NBS = DB
NBT = NBL + NBS
BI = 16
TWO_PI = 2 * math.pi
PI_A = 6.28125
PI_B = TWO_PI - PI_A
ROUND = 1.5 * 2 ** 23
BELOW_PI = 3.1415925


def state_space(nc, ins, outs, u):
    with ExitStack() as ctx:
        e = Env(nc, ctx, "ss")
        lr, li, dt = (e.sb(n, [P, NJ]) for n in ("lr", "li", "dt"))
        Br, Bi, Cr, Ci = (e.sb(n, [P, NJ, GC]) for n in ("Br", "Bi", "Cr", "Ci"))
        d = e.sb("d", [P, NG_])
        ident = e.sb("ident", [P, P])
        h0 = [e.sb(n, [P, NJ, NBS]) for n in ("h0r", "h0i")]
        wglu, bglu = e.sb("wglu", [P, KU, DSSM]), e.sb("bglu", [P, KU])
        small = {n: e.sb(n, [P, NJ]) for n in ("th", "mag", "k", "rs", "rc", "sin", "cos", "den", "nr", "fr", "fi", "x1", "x2")}
        Ap = [e.sb(n, [P, L + 1, NJ]) for n in ("Apr", "Api")]
        Qp = [e.sb(n, [P, BI + 1, NJ]) for n in ("Qpr", "Qpi")]
        Bb = [e.sb(n, [P, NJ, GC]) for n in ("Bbr", "Bbi")]
        CA = [e.sb(n, [P, NJ, L + 1, GC]) for n in ("CAr", "CAn")]
        RT = [e.sb(n, [P, NJ, P]) for n in ("RTr", "RTi")]
        Tm = e.sb("Tm", [P, NG_, P])
        U = e.sb("U", [P, NG_, NBT])
        H = [e.sb(n, [P, NJ, NBL + 1]) for n in ("Hr", "Hi")]
        HS = [e.sb(n, [P, NJ, NBS]) for n in ("HSr", "HSi")]
        rows = e.sb("rows", [P, NG_ * P])
        G = [e.sb(n, [P, NJ, BI]) for n in ("Gr", "Gi")]
        tmp = [e.sb(f"tmp{i}", [P, NJ, BI]) for i in range(4)]
        sg = e.sb("sg", [P, KU, TW])
        endp = [e.sb(n, [P, NJ]) for n in ("endr", "endi")]
        Rb = H[0][:].rearrange("p j n -> p (j n)")[:, 0:2 * NJ * P]
        R = [Rb[:, i * NJ * P:(i + 1) * NJ * P].rearrange("p (j s c) -> p j s c", s=L, c=GC) for i in range(2)]
        big = [H[i][:].rearrange("p j n -> p (j n)")[:, 0:NJ * (L + 1) * GC].rearrange("p (j t c) -> p j t c", t=L + 1, c=GC) for i in range(2)]
        Ks = H[1][0:GC].rearrange("p j n -> p (j n)")[:, 0:NG_ * P].rearrange("p (g x) -> p g x", x=P)
        dtmp = Rb.rearrange("p (g x) -> p g x", x=P)
        bk = [e.ps(f"bk{i}", [P, 512]) for i in range(8)]

        par_in, zero, chain = e.sem("par_in"), e.sem("zero"), e.sem("chain")
        dt_ready, mag_ready, sc_ready = e.sem("dt_ready"), e.sem("mag_ready"), e.sem("sc_ready")
        arg_ready, red_ready = e.sem("arg_ready"), e.sem("red_ready")
        k_ready, r_ready = e.sem("k_ready"), e.sem("r_ready")
        k_mm, k_out, t_moved, t_ready = e.sem("k_mm"), e.sem("k_out"), e.sem("t_moved"), e.sem("t_ready")
        r_mm, r_out = e.sem("r_mm"), e.sem("r_out")
        u_mm, u_out = e.sem("u_mm"), e.sem("u_out")
        b_mm, b_act, b_dve = e.sem("b_mm"), e.sem("b_act"), e.sem("b_dve")
        h_ready, end_ready = e.sem("h_ready"), e.sem("end_ready")
        y_mm, y_out, x_mm, x_out = e.sem("y_mm"), e.sem("y_out"), e.sem("x_mm"), e.sem("x_out")
        g_mm, g_sig, g_out = e.sem("g_mm"), e.sem("g_sig"), e.sem("g_out")
        stored, glu_in = e.sem("stored"), e.sem("glu_in")
        NPAR = 12

        LOTS = [(0, P, 0), (P, P, P * L), (NBL, NBS, SEQ)]
        NK = NG_ // 4
        NR = 2 * NJ // 4
        UF, UG = KU * 2, NG_ // 4
        UL = UF + UG

        def groups(i):
            first = 8 * (i // 2) + i % 2
            return slice(first, first + 7, 2)

        with nc.Block() as block:
            @block.sync
            def _(sp):
                for dst, n in ((lr, "lam_re"), (li, "lam_im"), (dt, "log_dt"), (Br, "b_re"), (Bi, "b_im"), (Cr, "c_re"), (Ci, "c_im"),
                               (d, "ssm_d"), (ident, "ident"), (h0[0], "h0_re"), (h0[1], "h0_im"), (bglu, "b_glu")):
                    sp.dma_start(dst[:], ins[n]).then_inc(par_in, 16)
                for k in range(KU):
                    sp.dma_start(wglu[:, k, :], ins["w_glu"][k]).then_inc(glu_in, 16)
                sp.wait_ge(k_out, NK)
                sp.wait_ge(zero, 3)
                for s in range(L):
                    sp.dma_start(Tm[s * GC:(s + 1) * GC, :, s * GC:P], Ks[:, :, 0:P - s * GC]).then_inc(t_moved, 16)
                sp.wait_ge(end_ready, 2)
                for i, n in enumerate(("re", "im")):
                    sp.dma_start(outs[f"ssm_{n}_p"], endp[i][:]).then_inc(stored, 16)
                    sp.dma_start(outs[f"ssm_{n}_s"], HS[i][:]).then_inc(stored, 16)
                sp.wait_ge(stored, 64)

            @block.gpsimd
            def _(pool):
                pool.memset(Tm[:], 0.0).then_inc(zero, 1)
                pool.memset(Ap[0][:, 0, :], 1.0).then_inc(zero, 1)
                pool.memset(Ap[1][:, 0, :], 0.0).then_inc(zero, 1)

            def u_copy(eng, lot, f, n, b0):
                i = lot * UL + f
                eng.wait_ge(u_mm, i + 1)
                src = bk[i % 8]
                if f < UF:
                    ct, half = f // 2, f % 2
                    dst = rows[0:n, :].rearrange("p (g s c) -> p g s c", s=L, c=GC)[:, 8 * ct:8 * ct + 8, 4 * half:4 * half + 4, :]
                    src = src[0:n, :].rearrange("p (s g c) -> p g s c", s=4, c=GC)
                else:
                    g = 4 * (f - UF)
                    dst = U[:, g:g + 4, b0:b0 + n]
                    src = src[:, 0:4 * n].rearrange("p (g n) -> p g n", g=4)
                eng.copy(dst, src).then_inc(u_out, 1)

            @block.scalar
            def _(act):
                act.wait_ge(par_in, 16 * NPAR)
                act.activation(dt[:], dt[:], ACT.Exp).then_inc(dt_ready, 1)
                act.wait_ge(mag_ready, 1)
                act.activation(small["mag"][:], small["mag"][:], ACT.Exp).then_inc(sc_ready, 1)
                act.wait_ge(arg_ready, 1)
                act.activation(small["sin"][:], small["rs"][:], ACT.Sin).then_inc(sc_ready, 1)
                act.activation(small["cos"][:], small["rc"][:], ACT.Sin).then_inc(sc_ready, 1)
                for lot, (b0, n, _) in enumerate(LOTS):
                    for f in range(UL):
                        u_copy(act, lot, f, n, b0)
                for i in range(NK):
                    act.wait_ge(k_mm, i + 1)
                    act.copy(Ks[:, groups(i), :], bk[i % 4][0:GC, :].rearrange("p (g x) -> p g x", x=P)).then_inc(k_out, 1)
                for i in range(NR):
                    act.wait_ge(r_mm, i + 1)
                    act.copy(RT[i // (NJ // 4)][:, 4 * (i % (NJ // 4)):4 * (i % (NJ // 4)) + 4, :],
                             bk[4 + i % 4][:].rearrange("p (j x) -> p j x", x=P)).then_inc(r_out, 1)
                for j in range(NJ):
                    act.wait_ge(b_mm, 2 * j + 1)
                    src = bk[(2 * j) % 8]
                    act.copy(H[0][:, j, 1:], src[:, 0:NBL])
                    act.copy(HS[0][:, j, :], src[:, NBL:NBT]).then_inc(b_act, 1)
                for lot, (b0, n, _) in enumerate(LOTS):
                    for q in range(UG):
                        i = lot * UG + q
                        act.wait_ge(y_mm, i + 1)
                        if q == 0 and lot:
                            act.wait_ge(x_mm, UF * lot)
                        out = rows[0:n, :].rearrange("p (t g c) -> p g t c", t=L, c=GC)[:, groups(q)]
                        act.activation(out, bk[i % 4][0:n, :].rearrange("p (g t c) -> p g t c", t=L, c=GC), ACT.Gelu_apprx_tanh).then_inc(y_out, 1)
                for n in range(NT):
                    for m in range(KU):
                        i = n * KU + m
                        act.wait_ge(g_mm, i + 1)
                        if m == 0 and n:
                            act.wait_ge(g_out, n)
                        act.activation(sg[:, m, :], bk[i % 4][:, 0:TW], ACT.Sigmoid, bias=bglu[:, m:m + 1]).then_inc(g_sig, 1)

            @block.vector
            def _(dve):
                count = [0]

                def link(ins):
                    count[0] += 1
                    ins.then_inc(chain, 1)
                    dve.wait_ge(chain, count[0])

                def tt(out, a, b, op):
                    link(dve.tensor_tensor(out, a, b, op))

                def ts(out, a, s1, s2, o1, o2=None):
                    link(dve.tensor_scalar(out, a, s1, s2, o1, *([o2] if o2 else [])))

                def cmul(out, a, b, t):
                    tt(t[0], a[0], b[0], ALU.mult)
                    tt(t[1], a[1], b[1], ALU.mult)
                    tt(t[2], a[0], b[1], ALU.mult)
                    tt(t[3], a[1], b[0], ALU.mult)
                    tt(out[0], t[0], t[1], ALU.subtract)
                    tt(out[1], t[2], t[3], ALU.add)

                s = {n: x[:] for n, x in small.items()}

                def reduced(out, x):
                    ts(s["k"], x, 1 / TWO_PI, ROUND, ALU.mult, ALU.add)
                    ts(s["k"], s["k"], -ROUND, None, ALU.add)
                    link(dve.scalar_tensor_tensor(out, s["k"], -PI_A, x, ALU.mult, ALU.add))
                    link(dve.scalar_tensor_tensor(out, s["k"], -PI_B, out, ALU.mult, ALU.add))
                    ts(out, out, BELOW_PI, -BELOW_PI, ALU.min, ALU.max)

                dve.wait_ge(par_in, 16 * NPAR)
                dve.wait_ge(dt_ready, 1)
                tt(s["th"], li[:], dt[:], ALU.mult)
                dve.tensor_tensor(s["mag"], lr[:], dt[:], ALU.mult).then_inc(mag_ready, 1)
                reduced(s["rs"], s["th"])
                ts(s["x1"], s["rs"], math.pi / 2, None, ALU.add)
                reduced(s["rc"], s["x1"])
                dve.sem_inc(arg_ready, 1)
                dve.wait_ge(sc_ready, 3)
                dve.wait_ge(zero, 3)
                tt(Ap[0][:, 1], s["mag"], s["cos"], ALU.mult)
                tt(Ap[1][:, 1], s["mag"], s["sin"], ALU.mult)
                tt(s["x1"], lr[:], lr[:], ALU.mult)
                tt(s["x2"], li[:], li[:], ALU.mult)
                tt(s["den"], s["x1"], s["x2"], ALU.add)
                link(dve.reciprocal(s["den"], s["den"]))
                ts(s["nr"], Ap[0][:, 1], -1.0, None, ALU.add)
                tt(s["x1"], s["nr"], lr[:], ALU.mult)
                tt(s["x2"], Ap[1][:, 1], li[:], ALU.mult)
                tt(s["fr"], s["x1"], s["x2"], ALU.add)
                tt(s["fr"], s["fr"], s["den"], ALU.mult)
                tt(s["x1"], Ap[1][:, 1], lr[:], ALU.mult)
                tt(s["x2"], s["nr"], li[:], ALU.mult)
                tt(s["fi"], s["x1"], s["x2"], ALU.subtract)
                tt(s["fi"], s["fi"], s["den"], ALU.mult)
                t4 = [x[:] for x in tmp]
                cmul([x[:] for x in Bb], [bcast(s["fr"], GC), bcast(s["fi"], GC)], [Br[:], Bi[:]], t4)

                def powers(X, top):
                    n = 1
                    while n < top:
                        w = min(n, top - n)
                        last = [x[:, n:n + 1, :].to_broadcast([P, w, NJ]) for x in X]
                        t = [x[:].rearrange("p j b -> p b j")[:, 0:w, :] for x in tmp]
                        cmul([x[:, n + 1:n + 1 + w, :] for x in X], [x[:, 1:1 + w, :] for x in X], last, t)
                        n += w

                powers(Ap, L)
                at_ = [x[:].rearrange("p t j -> p j t").unsqueeze(3).to_broadcast([P, NJ, L + 1, GC]) for x in Ap]
                c_ = [x[:].unsqueeze(2).to_broadcast([P, NJ, L + 1, GC]) for x in (Cr, Ci)]
                tt(big[0], at_[0], c_[0], ALU.mult)
                tt(big[1], at_[1], c_[1], ALU.mult)
                tt(CA[0][:], big[0], big[1], ALU.subtract)
                tt(big[0], at_[0], c_[1], ALU.mult)
                tt(big[1], at_[1], c_[0], ALU.mult)
                tt(CA[1][:], big[0], big[1], ALU.add)
                dve.tensor_scalar(CA[1][:], CA[1][:], -1.0, None, ALU.mult).then_inc(k_ready, 1)
                for q in range(L):
                    a = [bcast(x[:, L - 1 - q, :], GC) for x in Ap]
                    cmul([R[0][:, :, q, :], R[1][:, :, q, :]], a, [x[:] for x in Bb], t4)
                dve.sem_inc(r_ready, 1)
                for i in range(2):
                    link(dve.tensor_copy(Qp[i][:, 1, :], Ap[i][:, L, :]))
                powers(Qp, BI)
                dve.wait_ge(t_moved, 16 * L)
                dve.wait_ge(r_mm, NR)
                tt(dtmp, ident[:].unsqueeze(1).to_broadcast([P, NG_, P]), bcast(d[:], P), ALU.mult)
                link(dve.tensor_tensor(Tm[:], Tm[:], dtmp, ALU.add))
                dve.sem_inc(t_ready, 1)
                for i in range(2):
                    link(dve.memset(H[i][:, :, 0:1], 0.0))
                for j in range(NJ):
                    dve.wait_ge(b_mm, 2 * j + 2)
                    src = bk[(2 * j + 1) % 8]
                    dve.tensor_copy(H[1][:, j, 1:], src[:, 0:NBL])
                    dve.tensor_copy(HS[1][:, j, :], src[:, NBL:NBT]).then_inc(b_dve, 1)
                dve.wait_ge(b_act, NJ)
                dve.wait_ge(b_dve, NJ)

                def add_product(x, a, b, t):
                    tt(t[0], a[0], b[0], ALU.mult)
                    tt(t[1], a[1], b[1], ALU.mult)
                    tt(t[2], a[0], b[1], ALU.mult)
                    tt(t[3], a[1], b[0], ALU.mult)
                    tt(x[0], x[0], t[0], ALU.add)
                    tt(x[1], x[1], t[2], ALU.add)
                    tt(x[0], x[0], t[1], ALU.subtract)
                    tt(x[1], x[1], t[3], ALU.add)

                def run(i):
                    return [x[:, :, 1 + i:1 + i + BI * (BI - 1) + 1:BI] for x in H]

                a8 = [bcast(x[:, 1, :], BI) for x in Qp]
                for i in range(1, BI):
                    add_product(run(i), a8, run(i - 1), t4)
                ends = run(BI - 1)
                for i in range(2):
                    link(dve.memset(G[i][:, :, 0:1], 0.0))
                    link(dve.tensor_copy(G[i][:, :, 1:], ends[i][:, :, 0:BI - 1]))
                a128 = [x[:, BI, :] for x in Qp]
                tj = [x[:, :, 0] for x in tmp]
                for b in range(1, BI):
                    add_product([x[:, :, b] for x in G], a128, [x[:, :, b - 1] for x in G], tj)
                for r in range(BI):
                    blocks = [x[:, :, 1 + r * BI:1 + (r + 1) * BI] for x in H]
                    add_product(blocks, [x[:, 1:, :].rearrange("p i j -> p j i") for x in Qp], [bcast(x[:, :, r], BI) for x in G], t4)
                    if r % (BI // 2) == BI // 2 - 1:
                        dve.sem_inc(h_ready, 1)
                a8s = [bcast(x[:, 1, :], NBS) for x in Qp]
                add_product([x[:] for x in HS], a8s, [x[:] for x in h0], [x[:, :, 0:NBS] for x in tmp])
                for i in range(2):
                    dve.tensor_copy(endp[i][:], H[i][:, :, NBL]).then_inc(end_ready, 1)
                for lot, (b0, n, t0) in enumerate(LOTS):
                    for f in range(UF):
                        i = lot * UF + f
                        ct, half = f // 2, f % 2
                        dve.wait_ge(x_mm, i + 1)
                        dst = u[:, ct, t0:t0 + n * L].rearrange("p (n t) -> p t n", t=L)[:, 4 * half:4 * half + 4, :]
                        dve.tensor_copy(dst, bk[4 + i % 4][:, 0:4 * n].rearrange("p (t n) -> p t n", t=4)).then_inc(x_out, 1)
                for n in range(NT):
                    dve.wait_ge(g_sig, KU * (n + 1))
                    dve.tensor_tensor(u[:, :, tok(n)], u[:, :, tok(n)], sg[:], ALU.mult).then_inc(g_out, 1)

            @block.tensor
            def _(pe):
                pe.wait_ge(par_in, 16 * NPAR)
                for lot, (b0, n, t0) in enumerate(LOTS):
                    for f in range(UL):
                        i = lot * UL + f
                        if i >= 8:
                            pe.wait_ge(u_out, i - 7)
                        if f < UF:
                            ct, half = f // 2, f % 2
                            for k in range(4):
                                first = t0 + 4 * half + k
                                last = pe.transpose(bk[i % 8][0:n, k * P:(k + 1) * P], u[:, ct, first:first + L * (n - 1) + 1:L], ident[:])
                        else:
                            if f == UF:
                                pe.wait_ge(u_out, lot * UL + UF)
                            for k in range(4):
                                g = 4 * (f - UF) + k
                                last = pe.transpose(bk[i % 8][:, k * n:(k + 1) * n], rows[0:n, g * P:(g + 1) * P], ident[0:n, 0:n])
                        last.then_inc(u_mm, 1)
                pe.wait_ge(u_out, len(LOTS) * UL)
                pe.wait_ge(k_ready, 1)
                for i in range(NK):
                    if i >= 4:
                        pe.wait_ge(k_out, i - 3)
                    for n4, g in enumerate(range(NG_)[groups(i)]):
                        j, h = g // 2, slice(NS * (g % 2), NS * (g % 2) + NS)
                        out = bk[i % 4][0:GC, n4 * P:(n4 + 1) * P]
                        for n in range(2):
                            last = pe.matmul(out, Bb[n][h, j, :], CA[n][h, j, 0:L, :], start=(n == 0), stop=(n == 1))
                    last.then_inc(k_mm, 1)
                pe.wait_ge(r_ready, 1)
                for i in range(NR):
                    if i >= 4:
                        pe.wait_ge(r_out, i - 3)
                    x, j0 = i // (NJ // 4), 4 * (i % (NJ // 4))
                    for j in range(j0, j0 + 4):
                        last = pe.transpose(bk[4 + i % 4][:, (j - j0) * P:(j - j0 + 1) * P], R[x][:, j].rearrange("p s c -> p (s c)"), ident[:])
                    last.then_inc(r_mm, 1)
                pe.wait_ge(k_out, NK)
                pe.wait_ge(r_out, NR)
                pe.wait_ge(t_ready, 1)
                for i in range(2 * NJ):
                    j, x = i // 2, i % 2
                    if i >= 8:
                        pe.wait_ge((b_act, b_dve)[x], j - 3)
                    for h in range(2):
                        last = pe.matmul(bk[i % 8][NS * h:NS * h + NS, 0:NBT], RT[x][:, j, NS * h:NS * h + NS], U[:, 2 * j + h, :], start=True, stop=True)
                    last.then_inc(b_mm, 1)
                for lot, (b0, n, t0) in enumerate(LOTS):
                    if lot < 2:
                        pe.wait_ge(h_ready, lot + 1)
                    for q in range(UG):
                        i = lot * UG + q
                        if i >= 4:
                            pe.wait_ge(y_out, i - 3)
                        for n4, g in enumerate(range(NG_)[groups(q)]):
                            j, h = g // 2, slice(NS * (g % 2), NS * (g % 2) + NS)
                            out = bk[i % 4][0:n, n4 * P:(n4 + 1) * P]
                            pe.matmul(out, U[:, g, b0:b0 + n], Tm[:, g, :], start=True, stop=False)
                            for x in range(2):
                                state = h0[x][h, j, :] if b0 == NBL else H[x][h, j, b0:b0 + n]
                                last = pe.matmul(out, state, CA[x][h, j, 1:, :], start=False, stop=(x == 1))
                        last.then_inc(y_mm, 1)
                    pe.wait_ge(y_out, (lot + 1) * UG)
                    for f in range(UF):
                        i = lot * UF + f
                        ct, half = f // 2, f % 2
                        if i >= 4:
                            pe.wait_ge(x_out, i - 3)
                        for k in range(4):
                            c = (4 * half + k) * DSSM + ct * P
                            last = pe.transpose(bk[4 + i % 4][:, k * n:(k + 1) * n], rows[0:n, c:c + P], ident[0:n, 0:n])
                        last.then_inc(x_mm, 1)
                pe.wait_ge(x_out, UF * len(LOTS))
                pe.wait_ge(glu_in, 16 * KU)
                for n in range(NT):
                    for m in range(KU):
                        i = n * KU + m
                        if i >= 4:
                            pe.wait_ge(g_sig, i - 3)
                        for k in range(KU):
                            last = pe.matmul(bk[i % 4][:, 0:TW], wglu[:, k, m * P:(m + 1) * P], u[:, k, tok(n)], start=(k == 0), stop=(k == KU - 1))
                        last.then_inc(g_mm, 1)


def hybrid_layer(nc, ins, outs, scratch):
    with ExitStack() as ctx:
        def late(name, shape):
            return ctx.enter_context(nc.sbuf_tensor(name, shape, F32, side="right"))

        with ExitStack() as mixing:
            u = mixing.enter_context(nc.sbuf_tensor("mix_a", [P, KU, T], F32))
            project_in(nc, ins, scratch, u)
            state_space(nc, ins, outs, u)
            yb = mixing.enter_context(nc.sbuf_tensor("mix_b", [P, KR, T], F32))
            delta_rule(nc, ins, outs, scratch, yb)
            hT, rstd = late("h", [P, KD, T]), late("rstd", [P, T])
            mix_out(nc, ins, (u, yb), hT, rstd)
        conv_ffn(nc, ins, outs, hT, rstd)
        gated_embedding(nc, ins, outs, hT)


def kernel(**inputs):
    import numpy as np
    import concourse.bacc as _bacc
    from concourse import mybir as _mybir
    from concourse.bass_utils import run_bass_kernel_spmd as _run

    a = {k: np.asarray(v) for k, v in inputs.items()}

    def tiles(rows):
        return rows.T.reshape(-1, P, rows.shape[0]).transpose(1, 0, 2)

    def columns(v):
        return v.reshape(-1, P).T

    def states(v):
        v = v.reshape(NJ, 2, NS, -1).transpose(1, 2, 0, 3).reshape(P, NJ, -1)
        return v[:, :, 0] if v.shape[2] == 1 else v

    def both(prompt, sample):
        return tiles(np.concatenate([prompt.reshape(SEQ, -1), sample.reshape(TS_ALL, -1)], 0))

    TS_ALL = DB * DS
    w_up = a["w_up"][0].reshape(KD, P, 2 * FF).transpose(1, 0, 2)
    arrays = {
        "xT": both(a["x_prompt"], a["x_sample"]),
        "pT": both(a["p_prompt"], a["p_sample"]),
        "norm1_g": columns(a["norm1_g"]), "norm2_g": columns(a["norm2_g"]), "final_g": columns(a["final_g"]),
        "w_in": a["w_in"].reshape(KD, P, -1), "w_out": a["w_out"].reshape(KD, P, D),
        "w_val": w_up[:, :, 0:FF], "w_gate": w_up[:, :, FF:], "w_down": a["w_down"].reshape(KF, P, D),
        "conv_wb": np.concatenate([a["conv_w"][0], a["conv_b"]], 0).reshape(CONV + 1, KF, P).transpose(2, 1, 0),
        "state_conv": a["state_conv"].reshape(DB, 2, KF, P).transpose(3, 2, 0, 1),
        "w_pg": a["w_pg"].reshape(KD, P, D), "w_ple": a["w_ple"].reshape(KP, P, D),
        "w2a2": np.concatenate([a["rwkv_w2"][0], a["rwkv_a2"][0]], 0), "g2": a["rwkv_g2"][0], "mu": columns(a["shift_mu"]),
        "masks": rwkv_masks(), "seg": chunk_starts(), "rows8": sample_rows(),
        "state_rwkv": a["state_rwkv"].reshape(DB, HP, 2, HD, HD).transpose(2, 4, 0, 1, 3).reshape(P, DB, HP, HD),
        "state_shift": a["state_shift"].reshape(DB, ZT, P).transpose(2, 1, 0),
        "lam_re": states(a["ssm_lam_re"]), "lam_im": states(a["ssm_lam_im"]),
        "log_dt": states(np.repeat(a["ssm_log_dt"][0][:, None], NS, 1)),
        "b_re": states(a["ssm_b_re"]), "b_im": states(a["ssm_b_im"]),
        "c_re": states(a["ssm_c_re"][0].transpose(0, 2, 1)), "c_im": states(a["ssm_c_im"][0].transpose(0, 2, 1)),
        "ssm_d": np.tile(a["ssm_d"].reshape(NG_, GC).T, (L, 1)), "ident": np.eye(P, dtype=np.float32),
        "h0_re": states(a["state_ssm_re"][0].transpose(1, 2, 0)), "h0_im": states(a["state_ssm_im"][0].transpose(1, 2, 0)),
        "w_glu": a["ssm_w_glu"].reshape(KU, P, DSSM), "b_glu": columns(a["ssm_b_glu"]),
    }
    for n in ("w0", "a0", "k_k", "k_a", "r_k", "lnx_g", "lnx_b"):
        arrays[n] = columns(a["rwkv_" + n])
    arrays = {k: np.ascontiguousarray(v) for k, v in arrays.items()}
    shapes = {
        "yT": (P, KD, T), "ssm_re_p": (P, NJ), "ssm_im_p": (P, NJ), "ssm_re_s": (P, NJ, DB), "ssm_im_s": (P, NJ, DB),
        "rwkv_p": (P, HP, HD), "rwkv_s": (P, DB, HP, HD), "shift": (P, ZT, 1 + DB), "conv_p": (P, KF, 2), "conv_s": (P, KF, DB, 2),
    }
    nc = _bacc.Bacc("TRN2", target_bir_lowering=False, num_devices=1)
    ins = {k: nc.dram_tensor(f"in_{k}", v.shape, _mybir.dt.from_np(v.dtype), kind="ExternalInput").ap() for k, v in arrays.items()}
    outs = {k: nc.dram_tensor(f"out_{k}", v, F32, kind="ExternalOutput").ap() for k, v in shapes.items()}
    scratch = {"zr": nc.dram_tensor("scratch_zr", (ZT, P, T), F32, kind="Internal").ap()}
    hybrid_layer(nc, ins, outs, scratch)
    r = _run(nc, [{f"in_{k}": v for k, v in arrays.items()}], core_ids=[0]).results[0]
    o = {k: r[f"out_{k}"] for k in shapes}

    def from_states(v):
        return v.reshape(2, NS, NJ, -1).transpose(3, 2, 0, 1).reshape(1, -1, NG_, NS)

    y = o["yT"].transpose(2, 1, 0).reshape(T, D)
    shift = o["shift"].transpose(2, 1, 0).reshape(1 + DB, -1)
    return (
        y[None, 0:SEQ], y[SEQ:].reshape(DB, DS, D),
        from_states(o["ssm_re_p"]), from_states(o["ssm_im_p"]),
        o["rwkv_p"].reshape(2, HD, HP, HD).transpose(2, 0, 3, 1).reshape(1, 1, 2 * HP, HD, HD),
        shift[None, 0:1], o["conv_p"].transpose(2, 1, 0).reshape(1, 1, 2, FF),
        from_states(o["ssm_re_s"]), from_states(o["ssm_im_s"]),
        o["rwkv_s"].reshape(2, HD, DB, HP, HD).transpose(2, 3, 0, 4, 1).reshape(1, DB, 2 * HP, HD, HD),
        shift[None, 1:], o["conv_s"].transpose(2, 3, 1, 0).reshape(1, DB, 2, FF),
    )
```
